# Optimizing a Trainium2 kernel written in Bass

```python
import jax, jax.numpy as jnp
from jax import lax
import numpy as np
import math

D_MODEL = 1024
BATCH = 1
SEQ = 512
DEPTH = 2

GRID_W = 64
CTX_LEN = 256
N_MIXERS = 2
N_GLA_LAYERS = (DEPTH + 1) // 2
N_MLA_LAYERS = DEPTH // 2
EPS = 1e-6

GLA_HEADS = 4
GLA_DK = D_MODEL // 2 // GLA_HEADS
GLA_DV = D_MODEL // GLA_HEADS
GLA_GATE_RANK = 16
GLA_GATE_NORMALIZER = 16.0
GLA_CHUNK = 64
GLA_IN = 2 * GLA_HEADS * GLA_DK + 2 * GLA_HEADS * GLA_DV

MLA_HEADS = 8
MLA_NOPE = 128
MLA_ROPE = 64
MLA_QK = MLA_NOPE + MLA_ROPE
MLA_V = 128
MLA_Q_RANK = 384
MLA_KV_RANK = 256
MLA_DOWN = MLA_Q_RANK + MLA_KV_RANK + MLA_ROPE
ROPE_THETA = 10000.0
ROPE_FREQS = MLA_ROPE // 4
Q_BLOCK = 128

D_FF = 2816
CONV_W = 3


def rmsnorm(x, g):
    xf = x.astype(jnp.float32)
    y = xf * lax.rsqrt(jnp.mean(xf * xf, axis=-1, keepdims=True) + EPS)
    return (y * g.astype(jnp.float32)).astype(x.dtype)

def ada_modulation(cond, w, b):
    m = jax.nn.silu(cond) @ w + b
    return jnp.split(m, 6, axis=-1)

def modulate(x, g, shift, scale):
    return rmsnorm(x, g) * (1 + scale[..., None, :]) + shift[..., None, :]

def axial_rope_tables(length):
    rows = length // GRID_W
    t = jnp.arange(rows * GRID_W)
    row = (t // GRID_W).astype(jnp.float32)
    col = (t % GRID_W).astype(jnp.float32)
    inv = ROPE_THETA ** (-jnp.arange(ROPE_FREQS, dtype=jnp.float32) / ROPE_FREQS)
    ang = jnp.stack([row[:, None] * inv, col[:, None] * inv], axis=1)
    return jnp.cos(ang)[:, None], jnp.sin(ang)[:, None]

def apply_axial_rope(x, cos, sin):
    xr = x.astype(jnp.float32).reshape(*x.shape[:-1], 2, 2, ROPE_FREQS)
    x1, x2 = xr[..., 0, :], xr[..., 1, :]
    out = jnp.stack([x1 * cos - x2 * sin, x1 * sin + x2 * cos], axis=-2)
    return out.reshape(x.shape).astype(x.dtype)

def gla_project(h, w_in):
    B, L, _ = h.shape
    q, k, v, r = jnp.split(h @ w_in, [GLA_HEADS * GLA_DK, 2 * GLA_HEADS * GLA_DK,
                                      2 * GLA_HEADS * GLA_DK + GLA_HEADS * GLA_DV], axis=-1)
    q = q.reshape(B, L, GLA_HEADS, GLA_DK) * (GLA_DK ** -0.5)
    k = k.reshape(B, L, GLA_HEADS, GLA_DK)
    v = v.reshape(B, L, GLA_HEADS, GLA_DV)
    return q, k, v, r

def gla_log_decay(h, w1, w2, b):
    z = ((h @ w1) @ w2 + b).astype(jnp.float32)
    return (jax.nn.log_sigmoid(z) / GLA_GATE_NORMALIZER).reshape(*h.shape[:-1], GLA_HEADS, GLA_DK)

def gla_chunked(q, k, v, g, s0):
    B, L, H, _ = q.shape
    n = L // GLA_CHUNK
    def chunks(a):
        return a.reshape(B, n, GLA_CHUNK, H, a.shape[-1]).astype(jnp.float32)
    qc, kc, vc, gc = chunks(q), chunks(k), chunks(v), chunks(g)
    b = jnp.cumsum(gc, axis=2)
    b_last = b[:, :, -1:]
    q_dec = qc * jnp.exp(b)
    k_intra = kc * jnp.exp(-b)
    k_state = kc * jnp.exp(b_last - b)
    mask = jnp.tril(jnp.ones((GLA_CHUNK, GLA_CHUNK), dtype=bool))
    scores = jnp.where(mask, jnp.einsum('bnthd,bnshd->bnhts', q_dec, k_intra), 0.0)
    o_intra = jnp.einsum('bnhts,bnshv->bnthv', scores, vc)

    def step(S, xs):
        qd, ks, vv, bl = xs
        o = jnp.einsum('bthd,bhdv->bthv', qd, S)
        S = S * jnp.exp(bl)[..., None] + jnp.einsum('bthd,bthv->bhdv', ks, vv)
        return S, o

    xs = (jnp.moveaxis(q_dec, 1, 0), jnp.moveaxis(k_state, 1, 0),
          jnp.moveaxis(vc, 1, 0), jnp.moveaxis(b_last[:, :, 0], 1, 0))
    s_final, o_inter = lax.scan(step, s0.astype(jnp.float32), xs)
    o = o_intra + jnp.moveaxis(o_inter, 0, 1)
    return o.reshape(B, L, H, v.shape[-1]).astype(v.dtype), s_final

def gla_bidirectional(q, k, v, g_fwd, g_bwd, s_fwd0, s_bwd0):
    o_f, s_f = gla_chunked(q, k, v, g_fwd, s_fwd0)
    flip = lambda a: jnp.flip(a, axis=1)
    o_b, s_b = gla_chunked(flip(q), flip(k), flip(v), flip(g_bwd), s_bwd0)
    return o_f + flip(o_b), s_f, s_b

def gla_output(o, r, out_norm, w_out):
    B, L = o.shape[:2]
    o = rmsnorm(o, out_norm).reshape(B, L, GLA_HEADS * GLA_DV)
    return (o * jax.nn.silu(r)) @ w_out

def gla_mixer(h, hc, w_in, gate_w1, gate_w2, gate_b, out_norm, w_out, need_ctx_out):
    B = h.shape[0]
    s0 = jnp.zeros((B, GLA_HEADS, GLA_DK, GLA_DV), jnp.float32)
    qc, kc, vc, rc = gla_project(hc, w_in)
    gfc = gla_log_decay(hc, gate_w1[0], gate_w2[0], gate_b[0])
    gbc = gla_log_decay(hc, gate_w1[1], gate_w2[1], gate_b[1])
    oc, s_fwd, s_bwd = gla_bidirectional(qc, kc, vc, gfc, gbc, s0, s0)
    q, k, v, r = gla_project(h, w_in)
    gf = gla_log_decay(h, gate_w1[0], gate_w2[0], gate_b[0])
    gb = gla_log_decay(h, gate_w1[1], gate_w2[1], gate_b[1])
    o, _, _ = gla_bidirectional(q, k, v, gf, gb, s_fwd, s_bwd)
    out = gla_output(o, r, out_norm, w_out)
    out_c = gla_output(oc, rc, out_norm, w_out) if need_ctx_out else None
    return out, out_c

def split_norm(t, g):
    return jnp.concatenate([rmsnorm(t[..., :MLA_NOPE], g[:MLA_NOPE]),
                            rmsnorm(t[..., MLA_NOPE:], g[MLA_NOPE:])], axis=-1)

def mla_qkv(h, w_down, q_lora_norm, kv_lora_norm, w_uq, w_ukv, q_norm, k_norm, rope, want_q):
    B, L, _ = h.shape
    c_q, c_kv, k_pe = jnp.split(h @ w_down, [MLA_Q_RANK, MLA_Q_RANK + MLA_KV_RANK], axis=-1)
    kv = (rmsnorm(c_kv, kv_lora_norm) @ w_ukv).reshape(B, L, MLA_HEADS, MLA_NOPE + MLA_V)
    k_nope, v = kv[..., :MLA_NOPE], kv[..., MLA_NOPE:]
    k_nope = rmsnorm(k_nope, k_norm[:MLA_NOPE])
    k_pe = rmsnorm(k_pe, k_norm[MLA_NOPE:])[:, :, None, :]
    if rope is not None:
        k_pe = apply_axial_rope(k_pe, *rope)
    k = jnp.concatenate([k_nope, jnp.broadcast_to(k_pe, (B, L, MLA_HEADS, MLA_ROPE))], axis=-1)
    q = None
    if want_q:
        q = split_norm((rmsnorm(c_q, q_lora_norm) @ w_uq).reshape(B, L, MLA_HEADS, MLA_QK), q_norm)
        if rope is not None:
            q = jnp.concatenate([q[..., :MLA_NOPE], apply_axial_rope(q[..., MLA_NOPE:], *rope)], axis=-1)
    return q, k, v

def block_softmax_attention(q, k, v):
    B, L, H, Dh = q.shape
    nb = L // Q_BLOCK
    scale = Dh ** -0.5
    qb = jnp.moveaxis(q.reshape(B, nb, Q_BLOCK, H, Dh), 1, 0)
    def one(qblk):
        s = jnp.einsum('bqhd,bkhd->bhqk', qblk, k).astype(jnp.float32) * scale
        p = jax.nn.softmax(s, axis=-1).astype(v.dtype)
        return jnp.einsum('bhqk,bkhv->bqhv', p, v)
    o = lax.map(one, qb)
    return jnp.moveaxis(o, 0, 1).reshape(B, L, H, v.shape[-1])

def mla_mixer(h, hc, w_down, q_lora_norm, kv_lora_norm, w_uq, w_ukv, q_norm, k_norm, w_out, rope, need_ctx_out):
    B, L, _ = h.shape
    qc, kc, vc = mla_qkv(hc, w_down, q_lora_norm, kv_lora_norm, w_uq, w_ukv, q_norm, k_norm, None, need_ctx_out)
    q, k, v = mla_qkv(h, w_down, q_lora_norm, kv_lora_norm, w_uq, w_ukv, q_norm, k_norm, rope, True)
    o = block_softmax_attention(q, jnp.concatenate([kc, k], axis=1), jnp.concatenate([vc, v], axis=1))
    out = o.reshape(B, L, MLA_HEADS * MLA_V) @ w_out
    out_c = None
    if need_ctx_out:
        oc = block_softmax_attention(qc, kc, vc)
        out_c = oc.reshape(B, hc.shape[1], MLA_HEADS * MLA_V) @ w_out
    return out, out_c

def depthwise_conv3(u, w, b):
    up = jnp.pad(u, ((0, 0), (1, 1), (0, 0)))
    return up[:, :-2] * w[0] + up[:, 1:-1] * w[1] + up[:, 2:] * w[2] + b

def conv_ffn(h, w_up, conv_w, conv_b, w_down):
    u = depthwise_conv3(h @ w_up, conv_w, conv_b)
    a, g = jnp.split(u, 2, axis=-1)
    return (jax.nn.silu(g) * a) @ w_down

def first_inputs(seed: int = 0) -> dict:
    key = jax.random.key(seed)
    ks = jax.random.split(key, 32)
    nrm = lambda k, shape, s: jax.random.normal(k, shape, jnp.float32) * s
    gain = lambda k, shape: 1.0 + 0.05 * jax.random.normal(k, shape, jnp.float32)
    return {
        'x': nrm(ks[0], (BATCH, SEQ, D_MODEL), 1.0),
        'c': nrm(ks[1], (BATCH, D_MODEL), 1.0),
        'ctx': nrm(ks[2], (BATCH, CTX_LEN, D_MODEL), 1.0),
        'c_ctx': nrm(ks[3], (D_MODEL,), 1.0),
        'w_ada': nrm(ks[4], (DEPTH, D_MODEL, 6 * D_MODEL), 0.5 * D_MODEL ** -0.5),
        'b_ada': nrm(ks[5], (DEPTH, 6 * D_MODEL), 0.02),
        'norm_mix': gain(ks[6], (DEPTH, D_MODEL)),
        'norm_ffn': gain(ks[7], (DEPTH, D_MODEL)),
        'gla_w_in': nrm(ks[8], (N_GLA_LAYERS, D_MODEL, GLA_IN), D_MODEL ** -0.5),
        'gla_gate_w1': nrm(ks[9], (N_GLA_LAYERS, 2, D_MODEL, GLA_GATE_RANK), D_MODEL ** -0.5),
        'gla_gate_w2': nrm(ks[10], (N_GLA_LAYERS, 2, GLA_GATE_RANK, GLA_HEADS * GLA_DK), GLA_GATE_RANK ** -0.5),
        'gla_gate_b': nrm(ks[11], (N_GLA_LAYERS, 2, GLA_HEADS * GLA_DK), 0.1),
        'gla_out_norm': gain(ks[12], (N_GLA_LAYERS, GLA_DV)),
        'gla_w_out': nrm(ks[13], (N_GLA_LAYERS, GLA_HEADS * GLA_DV, D_MODEL), (GLA_HEADS * GLA_DV) ** -0.5),
        'mla_w_down': nrm(ks[14], (N_MLA_LAYERS, D_MODEL, MLA_DOWN), D_MODEL ** -0.5),
        'mla_q_lora_norm': gain(ks[15], (N_MLA_LAYERS, MLA_Q_RANK)),
        'mla_kv_lora_norm': gain(ks[16], (N_MLA_LAYERS, MLA_KV_RANK)),
        'mla_w_uq': nrm(ks[17], (N_MLA_LAYERS, MLA_Q_RANK, MLA_HEADS * MLA_QK), MLA_Q_RANK ** -0.5),
        'mla_w_ukv': nrm(ks[18], (N_MLA_LAYERS, MLA_KV_RANK, MLA_HEADS * (MLA_NOPE + MLA_V)), MLA_KV_RANK ** -0.5),
        'mla_q_norm': gain(ks[19], (N_MLA_LAYERS, MLA_QK)),
        'mla_k_norm': gain(ks[20], (N_MLA_LAYERS, MLA_QK)),
        'mla_w_out': nrm(ks[21], (N_MLA_LAYERS, MLA_HEADS * MLA_V, D_MODEL), (MLA_HEADS * MLA_V) ** -0.5),
        'ffn_w_up': nrm(ks[22], (DEPTH, D_MODEL, 2 * D_FF), D_MODEL ** -0.5),
        'ffn_conv_w': nrm(ks[23], (DEPTH, CONV_W, 2 * D_FF), CONV_W ** -0.5),
        'ffn_conv_b': nrm(ks[24], (DEPTH, 2 * D_FF), 0.02),
        'ffn_w_down': nrm(ks[25], (DEPTH, D_FF, D_MODEL), D_FF ** -0.5),
    }

def first_block(x, c, ctx, c_ctx, w_ada, b_ada, norm_mix, norm_ffn,
              gla_w_in, gla_gate_w1, gla_gate_w2, gla_gate_b, gla_out_norm, gla_w_out,
              mla_w_down, mla_q_lora_norm, mla_kv_lora_norm, mla_w_uq, mla_w_ukv,
              mla_q_norm, mla_k_norm, mla_w_out,
              ffn_w_up, ffn_conv_w, ffn_conv_b, ffn_w_down):
    rope = axial_rope_tables(x.shape[1])
    xc = ctx
    for i in range(DEPTH):
        last = i == DEPTH - 1
        j = i // N_MIXERS
        sh1, sc1, g1, sh2, sc2, g2 = ada_modulation(c, w_ada[i], b_ada[i])
        csh1, csc1, cg1, csh2, csc2, cg2 = ada_modulation(c_ctx, w_ada[i], b_ada[i])
        h = modulate(x, norm_mix[i], sh1, sc1)
        hc = modulate(xc, norm_mix[i], csh1, csc1)
        if i % N_MIXERS == 0:
            o, oc = gla_mixer(h, hc, gla_w_in[j], gla_gate_w1[j], gla_gate_w2[j], gla_gate_b[j],
                              gla_out_norm[j], gla_w_out[j], not last)
        else:
            o, oc = mla_mixer(h, hc, mla_w_down[j], mla_q_lora_norm[j], mla_kv_lora_norm[j],
                              mla_w_uq[j], mla_w_ukv[j], mla_q_norm[j], mla_k_norm[j], mla_w_out[j],
                              rope, not last)
        x = x + g1[:, None, :] * o
        x = x + g2[:, None, :] * conv_ffn(modulate(x, norm_ffn[i], sh2, sc2),
                                          ffn_w_up[i], ffn_conv_w[i], ffn_conv_b[i], ffn_w_down[i])
        if not last:
            xc = xc + cg1 * oc
            xc = xc + cg2 * conv_ffn(modulate(xc, norm_ffn[i], csh2, csc2),
                                     ffn_w_up[i], ffn_conv_w[i], ffn_conv_b[i], ffn_w_down[i])
    return x


CHUNK = 64
HEAD_DIM = 64
H_A = 8
LEFT_CHUNKS = 8
REL_MAX = 256
H_B = 4
H_C = 8
H_IDX = 4
D_IDX = 64
TOPK_MAX = 256
H_X = 4
MEM_LEN = 256
D_FF_2 = -(-8 * D_MODEL // (3 * 256)) * 256
QB = 128

W_A = H_A * HEAD_DIM
W_B = H_B * 2 * HEAD_DIM
W_C = H_C * HEAD_DIM
IN_SPLITS = (W_A, W_A, W_A, W_B, W_B, W_B, W_C, W_C, W_C, H_IDX * D_IDX, D_IDX, H_IDX, 3 * D_MODEL)
N_IN = 3 * W_A + 3 * W_B + 3 * W_C + H_IDX * D_IDX + D_IDX + H_IDX + 3 * D_MODEL
REL_TABLE = CHUNK + REL_MAX


def rmsnorm_2(x, g):
    x32 = x.astype(jnp.float32)
    y = x32 * lax.rsqrt(jnp.mean(x32 * x32, axis=-1, keepdims=True) + EPS)
    return y.astype(x.dtype) * g

def rope_tables(seq):
    pos = jnp.arange(seq, dtype=jnp.float32)
    inv = ROPE_THETA ** (-jnp.arange(0, HEAD_DIM, 2, dtype=jnp.float32) / HEAD_DIM)
    ang = pos[:, None] * inv[None, :]
    return jnp.cos(ang), jnp.sin(ang)

def apply_rope(x, cos, sin):
    extra = x.ndim - 3
    shp = (cos.shape[0],) + (1,) * extra + (cos.shape[1],)
    c = cos.reshape(shp).astype(x.dtype)
    s = sin.reshape(shp).astype(x.dtype)
    x1, x2 = jnp.split(x, 2, axis=-1)
    return jnp.concatenate([x1 * c - x2 * s, x2 * c + x1 * s], axis=-1)

def masked_softmax(scores, mask):
    return jax.nn.softmax(jnp.where(mask, scores.astype(jnp.float32), -jnp.inf), axis=-1)

def chunk_band_attention(q, k, v, rel_bias):
    b, s, h, d = q.shape
    nc = s // CHUNK
    band = LEFT_CHUNKS + 1
    pad = ((0, 0), (LEFT_CHUNKS * CHUNK, 0), (0, 0), (0, 0))
    kp = jnp.pad(k, pad)
    vp = jnp.pad(v, pad)
    i = jnp.arange(CHUNK)[:, None]
    j = jnp.arange(band * CHUNK)[None, :]
    rel = jnp.clip(LEFT_CHUNKS * CHUNK + i - j, -(CHUNK - 1), REL_MAX) + (CHUNK - 1)
    bias = rel_bias[:, rel].astype(jnp.float32)
    key_off = jnp.arange(band * CHUNK) // CHUNK - LEFT_CHUNKS
    scale = d ** -0.5

    def one_chunk(n):
        start = n * CHUNK
        qn = lax.dynamic_slice_in_dim(q, start, CHUNK, axis=1)
        kn = lax.dynamic_slice_in_dim(kp, start, band * CHUNK, axis=1)
        vn = lax.dynamic_slice_in_dim(vp, start, band * CHUNK, axis=1)
        sc = jnp.einsum('bqhd,bkhd->bhqk', qn, kn).astype(jnp.float32) * scale + bias[None]
        valid = (n + key_off >= 0)[None, None, None, :]
        p = masked_softmax(sc, valid).astype(v.dtype)
        return jnp.einsum('bhqk,bkhd->bqhd', p, vn)

    o = lax.map(one_chunk, jnp.arange(nc))
    return o.transpose(1, 0, 2, 3, 4).reshape(b, s, h * d)

def diff_attention(q, k, v, lam, lambda_init, subln):
    b, s, h, _, d = q.shape
    key_chunk = jnp.arange(s) // CHUNK
    scale = d ** -0.5

    def one_block(n):
        qn = lax.dynamic_slice_in_dim(q, n * QB, QB, axis=1)
        sc = jnp.einsum('bqhcd,bkhcd->bhcqk', qn, k).astype(jnp.float32) * scale
        q_chunk = (n * QB + jnp.arange(QB)) // CHUNK
        valid = key_chunk[None, :] <= q_chunk[:, None]
        p = masked_softmax(sc, valid)
        a = p[:, :, 0] - lam * p[:, :, 1]
        return jnp.einsum('bhqk,bkhe->bqhe', a.astype(v.dtype), v)

    o = lax.map(one_block, jnp.arange(s // QB))
    o = o.transpose(1, 0, 2, 3, 4).reshape(b, s, h, 2 * d)
    o = rmsnorm_2(o, subln) * (1.0 - lambda_init)
    return o.reshape(b, s, h * 2 * d)

def dsa_attention(q, k, v, q_idx, k_idx, w_idx, topk):
    b, s, h, d = q.shape
    key_pos = jnp.arange(s)
    gather = jax.vmap(lambda t, idx: t[idx])
    scale = d ** -0.5

    def one_chunk(n):
        start = n * CHUNK
        qn = lax.dynamic_slice_in_dim(q, start, CHUNK, axis=1)
        qi = lax.dynamic_slice_in_dim(q_idx, start, CHUNK, axis=1)
        wi = lax.dynamic_slice_in_dim(w_idx, start, CHUNK, axis=1).astype(jnp.float32)
        logits = jnp.einsum('bqhd,bsd->bqhs', qi, k_idx).astype(jnp.float32) * D_IDX ** -0.5
        score = jnp.einsum('bqhs,bqh->bqs', jax.nn.relu(logits), wi)
        admissible = key_pos < start + CHUNK
        score = jnp.where(admissible[None, None, :], score, -jnp.inf)
        vals, idx = lax.top_k(score, topk)
        valid = jnp.isfinite(vals)
        kg = gather(k, idx)
        vg = gather(v, idx)
        sc = jnp.einsum('bqhd,bqkhd->bhqk', qn, kg).astype(jnp.float32) * scale
        p = masked_softmax(sc, valid[:, None]).astype(v.dtype)
        return jnp.einsum('bhqk,bqkhd->bqhd', p, vg)

    o = lax.map(one_chunk, jnp.arange(s // CHUNK))
    return o.transpose(1, 0, 2, 3, 4).reshape(b, s, h * d)

def memory_cross_attention(hn, mem_n, w_q, w_kv, w_o):
    b, s, _ = hn.shape
    m = mem_n.shape[1]
    q = (hn @ w_q).reshape(b, s, H_X, HEAD_DIM)
    kv = (mem_n @ w_kv).reshape(b, m, 2, H_X, HEAD_DIM)
    sc = jnp.einsum('bqhd,bmhd->bhqm', q, kv[:, :, 0]).astype(jnp.float32) * HEAD_DIM ** -0.5
    p = jax.nn.softmax(sc, axis=-1).astype(hn.dtype)
    o = jnp.einsum('bhqm,bmhd->bqhd', p, kv[:, :, 1]).reshape(b, s, H_X * HEAD_DIM)
    return o @ w_o

def swiglu(hn, w_gu, w_down):
    g, u = jnp.split(hn @ w_gu, 2, axis=-1)
    return (jax.nn.silu(g) * u) @ w_down

def second_inputs(seed: int = 0) -> dict:
    key = jax.random.key(seed)
    ks = jax.random.split(key, 20)

    def normal(k, shape, scale):
        return jax.random.normal(k, shape, jnp.float32) * scale

    def gain(k, shape):
        return 1.0 + normal(k, shape, 0.05)

    return {
        'x': normal(ks[0], (BATCH, SEQ, D_MODEL), 1.0),
        'mem': normal(ks[1], (BATCH, MEM_LEN, D_MODEL), 1.0),
        'norm_mix': gain(ks[2], (DEPTH, D_MODEL)),
        'w_in': normal(ks[3], (DEPTH, D_MODEL, N_IN), D_MODEL ** -0.5),
        'rel_bias_a': normal(ks[4], (DEPTH, H_A, REL_TABLE), 0.5),
        'lambda_vecs': normal(ks[5], (DEPTH, 4, HEAD_DIM), 0.1),
        'subln_b': gain(ks[6], (DEPTH, 2 * HEAD_DIM)),
        'w_up_a': normal(ks[7], (DEPTH, W_A, D_MODEL), W_A ** -0.5),
        'w_up_b': normal(ks[8], (DEPTH, W_B, D_MODEL), W_B ** -0.5),
        'w_up_c': normal(ks[9], (DEPTH, W_C, D_MODEL), W_C ** -0.5),
        'w_out': normal(ks[10], (DEPTH, D_MODEL, D_MODEL), D_MODEL ** -0.5),
        'norm_cross': gain(ks[11], (DEPTH, D_MODEL)),
        'w_q_x': normal(ks[12], (DEPTH, D_MODEL, H_X * HEAD_DIM), D_MODEL ** -0.5),
        'w_kv_x': normal(ks[13], (DEPTH, D_MODEL, 2 * H_X * HEAD_DIM), D_MODEL ** -0.5),
        'w_o_x': normal(ks[14], (DEPTH, H_X * HEAD_DIM, D_MODEL), (H_X * HEAD_DIM) ** -0.5),
        'norm_ffn': gain(ks[15], (DEPTH, D_MODEL)),
        'w_gu': normal(ks[16], (DEPTH, D_MODEL, 2 * D_FF_2), D_MODEL ** -0.5),
        'w_down': normal(ks[17], (DEPTH, D_FF_2, D_MODEL), D_FF_2 ** -0.5),
        'mem_norm': gain(ks[18], (D_MODEL,)),
        'final_norm': gain(ks[19], (D_MODEL,)),
    }

def second_block(x, mem, norm_mix, w_in, rel_bias_a, lambda_vecs, subln_b, w_up_a, w_up_b, w_up_c,
              w_out, norm_cross, w_q_x, w_kv_x, w_o_x, norm_ffn, w_gu, w_down, mem_norm, final_norm):
    b, s, _ = x.shape
    topk = min(TOPK_MAX, s // 4)
    cos, sin = rope_tables(s)
    offsets = [int(o) for o in np.cumsum(IN_SPLITS)[:-1]]
    mem_n = rmsnorm_2(mem, mem_norm)
    shp_a = (b, s, H_A, HEAD_DIM)
    shp_b = (b, s, H_B, 2, HEAD_DIM)
    shp_c = (b, s, H_C, HEAD_DIM)
    for l in range(DEPTH):
        xn = rmsnorm_2(x, norm_mix[l])
        (qa, ka, va, qb, kb, vb, qc, kc, vc, qi, ki, wi, gates) = jnp.split(xn @ w_in[l], offsets, axis=-1)
        o_a = chunk_band_attention(qa.reshape(shp_a), ka.reshape(shp_a), va.reshape(shp_a), rel_bias_a[l])
        lam_init = 0.8 - 0.6 * math.exp(-0.3 * l)
        lv = lambda_vecs[l].astype(jnp.float32)
        lam = jnp.exp(jnp.sum(lv[0] * lv[1])) - jnp.exp(jnp.sum(lv[2] * lv[3])) + lam_init
        o_b = diff_attention(apply_rope(qb.reshape(shp_b), cos, sin), apply_rope(kb.reshape(shp_b), cos, sin),
                             vb.reshape(b, s, H_B, 2 * HEAD_DIM), lam, lam_init, subln_b[l])
        o_c = dsa_attention(apply_rope(qc.reshape(shp_c), cos, sin), apply_rope(kc.reshape(shp_c), cos, sin),
                            vc.reshape(shp_c),
                            apply_rope(qi.reshape(b, s, H_IDX, D_IDX), cos, sin),
                            apply_rope(ki[:, :, None, :], cos, sin)[:, :, 0],
                            wi * H_IDX ** -0.5, topk)
        g = jax.nn.sigmoid(gates).reshape(b, s, 3, D_MODEL)
        y = (g[:, :, 0] * (o_a @ w_up_a[l]) + g[:, :, 1] * (o_b @ w_up_b[l])
             + g[:, :, 2] * (o_c @ w_up_c[l]))
        x = x + y @ w_out[l]
        x = x + memory_cross_attention(rmsnorm_2(x, norm_cross[l]), mem_n, w_q_x[l], w_kv_x[l], w_o_x[l])
        x = x + swiglu(rmsnorm_2(x, norm_ffn[l]), w_gu[l], w_down[l])
    return rmsnorm_2(x, final_norm)


def setup_inputs(seed=0):
    out = dict(first_inputs(seed))
    for name, value in second_inputs(seed + 1).items():
        if name != "x":
            out[name + "_2"] = value
    return out


def reference(
    x, c, ctx, c_ctx, w_ada, b_ada, norm_mix, norm_ffn, gla_w_in, gla_gate_w1, gla_gate_w2,
    gla_gate_b, gla_out_norm, gla_w_out, mla_w_down, mla_q_lora_norm, mla_kv_lora_norm,
    mla_w_uq, mla_w_ukv, mla_q_norm, mla_k_norm, mla_w_out, ffn_w_up, ffn_conv_w, ffn_conv_b,
    ffn_w_down, mem_2, norm_mix_2, w_in_2, rel_bias_a_2, lambda_vecs_2, subln_b_2, w_up_a_2,
    w_up_b_2, w_up_c_2, w_out_2, norm_cross_2, w_q_x_2, w_kv_x_2, w_o_x_2, norm_ffn_2, w_gu_2,
    w_down_2, mem_norm_2, final_norm_2,
):
    x = first_block(
        x, c, ctx, c_ctx, w_ada, b_ada, norm_mix, norm_ffn, gla_w_in, gla_gate_w1, gla_gate_w2,
        gla_gate_b, gla_out_norm, gla_w_out, mla_w_down, mla_q_lora_norm, mla_kv_lora_norm,
        mla_w_uq, mla_w_ukv, mla_q_norm, mla_k_norm, mla_w_out, ffn_w_up, ffn_conv_w,
        ffn_conv_b, ffn_w_down,
    )
    return second_block(
        x, mem_2, norm_mix_2, w_in_2, rel_bias_a_2, lambda_vecs_2, subln_b_2, w_up_a_2,
        w_up_b_2, w_up_c_2, w_out_2, norm_cross_2, w_q_x_2, w_kv_x_2, w_o_x_2, norm_ffn_2,
        w_gu_2, w_down_2, mem_norm_2, final_norm_2,
    )


_drawn_inputs = setup_inputs


def setup_inputs(seed=0):
    import zlib

    import numpy as np

    out = dict(_drawn_inputs(seed))
    spreads = {}
    factors = {'gla_gate_b': 3.245,
     'gla_out_norm': 3.416,
     'mla_q_lora_norm': 8.0,
     'mla_kv_lora_norm': 3.79,
     'mla_q_norm': 8.0,
     'mla_k_norm': 8.0,
     'ffn_conv_b': 3.058,
     'norm_cross_2': 6.989,
     'mem_norm_2': 4.821}
    for name, (base, spread) in spreads.items():
        noise = np.random.default_rng([zlib.crc32(name.encode()), seed]).standard_normal(out[name].shape)
        drawn = base * np.exp(spread * noise) if base else spread * noise
        out[name] = __import__('jax').numpy.asarray(drawn.astype(out[name].dtype))
    for name, factor in factors.items():
        out[name] = (out[name] * factor).astype(out[name].dtype)
    return out
```

```python
import math
from contextlib import ExitStack

import numpy as np

import concourse.bass as bass
from concourse import mybir

F32 = mybir.dt.float32
ALU = mybir.AluOpType
ACT = mybir.ActivationFunctionType
AXX = mybir.AxisListType.X

P = 128
D = 1024
DT = D // P
CTX, SEQ = 256, 512
TOK = CTX + SEQ
BANK = 512
EPS = 1e-6
NEG = -1e30
TAKEN = -3e38
ALL = [(0, CTX), (CTX, SEQ)]
MAIN = [(CTX, SEQ)]
FF = 2816
FT = FF // P
GLA_H, GLA_DK, GLA_DV, GLA_C = 4, 128, 256, 64
GATE_NORM = 16.0
MLA_H, NOPE, ROPE = 8, 128, 64
Q_RANK, KV_RANK = 384, 256
HD = 64
TOPK = 128
SLOT = 4096
SLOTS = 4
ARENA = 20900

VECTORS = [("c", 8), ("c_ctx", 8), ("b_ada", 96), ("norm_mix", 16), ("norm_ffn", 16), ("gate_b", 8),
           ("gla_out_norm", 2), ("q_lora_norm", 3), ("kv_lora_norm", 2), ("q_norm_nope", 1),
           ("q_norm_rope", 1), ("k_norm_nope", 1), ("k_norm_rope", 1), ("conv_w", 264), ("conv_b", 88),
           ("norm_mix_2", 16), ("subln", 2), ("norm_cross", 16), ("norm_ffn_2", 16), ("mem_norm", 8),
           ("final_norm", 8)]
VAT = {}
_n = 0
for _name, _w in VECTORS:
    VAT[_name] = _n
    _n += _w
NVEC = _n
MATS = ["ident", "mean1024", "mean384", "mean256", "mean128", "mean64", "perm_axial", "perm_half",
        "mask_fwd", "mask_bwd", "flip"]


def shape_constants():
    m = {}
    i = np.arange(P)
    m["ident"] = np.eye(P)
    for d in (1024, 384, 256, 128):
        m[f"mean{d}"] = np.full((P, P), 1.0 / d)
    m["mean64"] = (i[:, None] // 64 == i[None] // 64) / 64.0
    for name, half in (("perm_axial", 16), ("perm_half", 32)):
        first = (i // half) % 2 == 0
        a = np.zeros((P, P))
        a[i[first] + half, i[first]] = -1.0
        a[i[~first] - half, i[~first]] = 1.0
        m[name] = a
    same = i[:, None] // GLA_C == i[None] // GLA_C
    m["mask_fwd"] = same & (i[:, None] <= i[None])
    m["mask_bwd"] = same & (i[:, None] >= i[None])
    m["flip"] = np.eye(P)[::-1]
    mats = np.stack([m[n].astype(np.float32) for n in MATS], 1)
    t = np.arange(SEQ)
    inv = np.float32(10000.0) ** (-np.arange(16, dtype=np.float32) / np.float32(16))
    ang = np.stack([(t // 64).astype(np.float32)[:, None] * inv, (t % 64).astype(np.float32)[:, None] * inv], 1)
    p = np.arange(P) % 64
    axial = ang[:, p // 32, p % 16].T
    inv = np.float32(10000.0) ** (-np.arange(0, 64, 2, dtype=np.float32) / np.float32(64))
    half = (t.astype(np.float32)[:, None] * inv)[:, p % 32].T
    rope = np.stack([np.stack([np.cos(a), np.sin(a)], 1) for a in (axial, half)], 1).astype(np.float32)
    return np.ascontiguousarray(mats), np.ascontiguousarray(rope)


class Counts:

    def __init__(self, known=None):
        self.known = known
        self.n = {}
        self.at = {}
        self.bank = {}
        self.chunk = {}


def build(nc, io, counts):
    known = counts.known
    ctx = ExitStack()
    with ctx:
        def sb(name, shape):
            return ctx.enter_context(nc.sbuf_tensor(name, shape, F32))

        X = sb("X", [P, DT, TOK])
        H = sb("H", [P, DT, TOK])
        ring = sb("ring", [P, SLOTS, SLOT])
        vec = sb("vec", [P, NVEC])
        mats = sb("mats", [P, len(MATS), P])
        cond = sb("cond", [P, DT, 2])
        modv = sb("modv", [P, 2, 48, 2])
        gain = sb("gain", [P, 2, 2, 2, DT])
        arena = sb("arena", [P, ARENA])
        eps = sb("eps", [P, 1])
        ada_rows = sb("ada_rows", [2, 2, BANK])
        ps = ctx.enter_context(nc.psum_tensor("ps", [P, 8, BANK], F32))

        def mat(name):
            return mats[:, MATS.index(name), :]

        def v(name, i, n=1):
            return vec[:, VAT[name] + i:VAT[name] + i + n]

        class Carve:
            def __init__(self, at=0):
                self.at = at

            def __call__(self, *shape):
                n = int(np.prod(shape))
                a = arena[:, self.at:self.at + n]
                self.at += n
                assert self.at <= ARENA, self.at
                if len(shape) == 2:
                    return a.rearrange("p (a b) -> p a b", b=shape[1])
                if len(shape) == 3:
                    return a.rearrange("p (a b c) -> p a b c", b=shape[1], c=shape[2])
                if len(shape) == 4:
                    return a.rearrange("p (a b c d) -> p a b c d", b=shape[1], c=shape[2], d=shape[3])
                return a

        pe_done = ctx.enter_context(nc.semaphore("pe_done"))
        act_done = ctx.enter_context(nc.semaphore("act_done"))
        dve_done = ctx.enter_context(nc.semaphore("dve_done"))
        slot_loaded = [ctx.enter_context(nc.semaphore(f"slot_loaded_{i}")) for i in range(SLOTS)]
        consts_loaded = ctx.enter_context(nc.semaphore("consts_loaded"))
        x_loaded = ctx.enter_context(nc.semaphore("x_loaded"))
        stage_loaded = ctx.enter_context(nc.semaphore("stage_loaded"))
        out_stored = ctx.enter_context(nc.semaphore("out_stored"))

        def mark(e, *keys):
            counts.n[e] = counts.n.get(e, 0) + 1
            for k in keys:
                counts.at.setdefault(k, {})[e] = counts.n[e]
            return 1

        def at(key, e=None):
            if known is None:
                return 1
            if e is None:
                (n,) = known.at[key].values()
                return n
            return known.at[key].get(e, 0)

        def meet(e, eng, name):
            counts.at.setdefault(("end", name), {})[e] = counts.n.get(e, 0)
            eng.wait_ge(pe_done, at(("end", name), "pe"))
            eng.wait_ge(act_done, at(("end", name), "act"))
            eng.wait_ge(dve_done, at(("end", name), "dve"))

        def cols(w, a, b):
            return w.rearrange("(t p) n -> p t n", p=P)[:, :, a:b]

        plan = []

        def weights_list():
            def ada(l, c):
                plan.append((("ada", l, c), [(0, cols(io["w_ada"][l], 512 * c, 512 * c + 512))]))

            for c in range(4):
                ada(0, c)
            g_in = io["gla_w_in"][0]
            for h in range(GLA_H):
                w = [(0, cols(g_in, h * 128, h * 128 + 128)), (128, cols(g_in, 512 + h * 128, 640 + h * 128)),
                     (256, cols(g_in, 1024 + h * 256, 1280 + h * 256))]
                plan.append((("gla_in", h), w))
                ada(0, 4 + 2 * h)
                ada(0, 5 + 2 * h)
            for c in range(2):
                plan.append((("gla_r", c), [(0, cols(g_in, 2048 + 512 * c, 2560 + 512 * c))]))
            for c in range(2):
                plan.append((("gla_out", c), [(0, cols(io["gla_w_out"][0], 512 * c, 512 * c + 512))]))

            def ffn(tag, up, down, extra):
                for c in range(FT // 2):
                    plan.append((("up", tag, c), [(0, cols(up, 256 * c, 256 * c + 256)),
                                                  (256, cols(up, FF + 256 * c, FF + 256 * c + 256))]))
                    extra(c)
                for n in range(DT):
                    plan.append((("down", tag, n), [(0, cols(down, 128 * n, 128 * n + 128))]))

            def ada1(c):
                ada(1, c)
                if c == FT // 2 - 1:
                    ada(1, c + 1)

            ffn("a0", io["ffn_w_up"][0], io["ffn_w_down"][0], ada1)
            dn = io["mla_w_down"][0]
            plan.append((("mla_dq",), [(0, cols(dn, 0, Q_RANK))]))
            plan.append((("mla_dkv",), [(0, cols(dn, Q_RANK, Q_RANK + KV_RANK + ROPE))]))
            for g in range(2):
                plan.append((("mla_uq", g), [(0, cols(io["mla_w_uq"][0], 768 * g, 768 * g + 768))]))
                plan.append((("mla_ukv", g), [(0, cols(io["mla_w_ukv"][0], 1024 * g, 1024 * g + 1024))]))
            for c in range(2):
                plan.append((("mla_out", c), [(0, cols(io["mla_w_out"][0], 512 * c, 512 * c + 512))]))
            ffn("a1", io["ffn_w_up"][1], io["ffn_w_down"][1], lambda c: None)
            for l in range(2):
                w = io["w_in_2"][l]
                plan.append((("idx", l), [(0, cols(w, 4608, 4608 + 324))]))
                for c in range(9):
                    plan.append((("in", l, c), [(0, cols(w, 512 * c, 512 * c + 512))]))
                for c in range(2):
                    for b, u in enumerate(("w_up_a_2", "w_up_b_2", "w_up_c_2")):
                        g0 = 4608 + 324 + 1024 * b + 512 * c
                        plan.append((("gate", l, b, c), [(0, cols(w, g0, g0 + 512))]))
                        plan.append((("mixup", l, b, c), [(0, cols(io[u][l], 512 * c, 512 * c + 512))]))
                for c in range(2):
                    plan.append((("mixout", l, c), [(0, cols(io["w_out_2"][l], 512 * c, 512 * c + 512))]))
                plan.append((("xkv", l), [(0, cols(io["w_kv_x_2"][l], 0, 512))]))
                plan.append((("xq", l), [(0, cols(io["w_q_x_2"][l], 0, 256))]))
                plan.append((("xo", l), [(0, cols(io["w_o_x_2"][l], 0, 1024))]))
                ffn(f"b{l}", io["w_gu_2"][l], io["w_down_2"][l], lambda c: None)

        weights_list()
        where = {}
        loads = [0] * SLOTS
        for i, (key, parts) in enumerate(plan):
            loads[i % SLOTS] += 16 * len(parts)
            where[key] = (i, loads[i % SLOTS])

        def weights(key):
            i, n = where[key]
            parts = plan[i][1]
            width = parts[-1][0] + parts[-1][1].shape[2]
            kt = parts[0][1].shape[1]
            nc.tensor.wait_ge(slot_loaded[i % SLOTS], n)
            return ring[:, i % SLOTS, 0:kt * width].rearrange("p (t n) -> p t n", n=width)

        def used(key):
            return ("slot_used", where[key][0])

        bank_user = [None] * 8
        turn = [0]

        def take(key, bank=None):
            if bank is None:
                bank = turn[0] % 8
                turn[0] += 1
            counts.bank[key] = bank
            if bank_user[bank] is not None:
                if by_act := at(("free", bank_user[bank]), "act"):
                    nc.tensor.wait_ge(act_done, by_act)
                if by_dve := at(("free", bank_user[bank]), "dve"):
                    nc.tensor.wait_ge(dve_done, by_dve)
            bank_user[bank] = key
            return ps[:, bank, :]

        def bank_of(key):
            return ps[:, known.bank[key] if known else 0, :]

        def mms(out, pairs):
            for i, (l, r) in enumerate(pairs):
                m = nc.tensor.matmul(out, l, r, start=(i == 0), stop=(i == len(pairs) - 1))
            return m

        def norm_pe(items):
            for key, src, sq, dst, mean, gains, shifts, r in items:
                n = src[0].shape[-1]
                k = src[0].shape[0]
                out = take(("ms", key))[0:k, 0:n]
                for i in range(len(src)):
                    nc.tensor.wait_ge(act_done, at(("sq", key, i)))
                    m = nc.tensor.matmul(out, mean[0:k, 0:k], sq[i], start=(i == 0), stop=(i == len(src) - 1))
                m.then_inc(pe_done, mark("pe", ("ms", key)))

        def norm_act(items):
            users = {}
            for j, (key, src, sq, dst, mean, gains, shifts, r) in enumerate(items):
                for i in range(len(src)):
                    tag = (str(sq[i].tensor.name), sq[i].offset)
                    if tag in users:
                        nc.scalar.wait_ge(pe_done, at(("ms", users[tag])))
                    users[tag] = key
                    nc.scalar.activation(sq[i], src[i], ACT.Square).then_inc(act_done, mark("act", ("sq", key, i)))
                if j:
                    rstd_act(items, j - 1)
            rstd_act(items, len(items) - 1)

        def rstd_act(items, j):
            key, src, sq, dst, mean, gains, shifts, r = items[j]
            k, n = r.shape
            for jj in range(j - 1, -1, -1):
                if items[jj][7].offset == r.offset:
                    nc.scalar.wait_ge(dve_done, at(("scaled", items[jj][0], len(items[jj][1]) - 1)))
                    break
            nc.scalar.wait_ge(pe_done, at(("ms", key)))
            nc.scalar.activation(r, bank_of(("ms", key))[0:k, 0:n], ACT.Ln, bias=eps[0:k, :]).then_inc(act_done, mark("act", ("ln", key), ("free", ("ms", key))))
            nc.scalar.wait_ge(act_done, at(("ln", key)))
            nc.scalar.activation(r, r, ACT.Exp, scale=-0.5).then_inc(act_done, mark("act", ("rstd", key)))
            shift_act(key, dst, shifts)

        def ln_exp_tables():
            nc.scalar.preload_act_table_set("natural_log_exp_and_others")

        def shift_act(key, dst, shifts):
            if shifts is None:
                return
            for i in range(len(dst)):
                nc.scalar.wait_ge(dve_done, at(("scaled", key, i)))
                nc.scalar.activation(dst[i], dst[i], ACT.Identity, bias=shifts[i]).then_inc(act_done, mark("act", ("normed", key)))

        def norm_dve(items):
            for key, src, sq, dst, mean, gains, shifts, r in items:
                nc.vector.wait_ge(act_done, at(("rstd", key)))
                for i in range(len(src)):
                    m = nc.vector.scalar_tensor_tensor(dst[i], src[i], gains[i], r, ALU.mult, ALU.mult)
                    m.then_inc(dve_done, mark("dve", ("scaled", key, i), *([("normed", key)] if shifts is None else [])))

        def block_norm(key, groups, gains, shifts, carve, src=X, dst=H):
            r = carve(TOK)
            items = []
            for t0, tn in groups:
                c = 0 if t0 else 1
                s = [src[:, k, t0:t0 + tn] for k in range(DT)]
                d = [dst[:, k, t0:t0 + tn] for k in range(DT)]
                items.append(((key, t0), s, d, d, mat("mean1024"), [gains(k, c) for k in range(DT)],
                              [shifts(k, c) for k in range(DT)] if shifts else None, r[:, t0:t0 + tn]))
            return items

        def adaln(key, groups, l, which):
            return block_norm(key, groups, lambda k, c: gain[:, l, which, c, k:k + 1],
                              lambda k, c: modv[:, l, 24 * which + k, c:c + 1], Carve())

        def run_norm(key, items):
            return {"pe": lambda: norm_pe(items), "act": lambda: norm_act(items), "dve": lambda: norm_dve(items)}

        def ada_pe(l, c):
            w = weights(("ada", l, c))
            out = take(("ada", l, c))
            m = mms(out[0:2, :], [(cond[:, k, :], w[:, k, :]) for k in range(DT)])
            m.then_inc(pe_done, mark("pe", ("ada", l, c), used(("ada", l, c))))

        def ada_turn_pe(l, c):
            nc.tensor.wait_ge(act_done, at(("ada_rows", l, c)))
            out = take(("ada_turned", l, c))
            for j in range(4):
                m = nc.tensor.transpose(out[:, 2 * j:2 * j + 2], ada_rows[0:2, c % 2, 128 * j:128 * j + 128],
                                        mat("ident")[0:2, 0:2])
            m.then_inc(pe_done, mark("pe", ("ada_turned", l, c)))

        def ada_act(l, c):
            nc.scalar.wait_ge(pe_done, at(("ada", l, c)))
            if c >= 2:
                nc.scalar.wait_ge(pe_done, at(("ada_turned", l, c - 2)))
            nc.scalar.copy(ada_rows[0:2, c % 2, :], bank_of(("ada", l, c))[0:2, :]).then_inc(
                act_done, mark("act", ("ada_rows", l, c), ("free", ("ada", l, c))))

        def ada_dve(l, c):
            nc.vector.wait_ge(pe_done, at(("ada_turned", l, c)))
            for s in range(2):
                m = nc.vector.tensor_tensor(
                    modv[:, l, 4 * c:4 * c + 4, s],
                    bank_of(("ada_turned", l, c))[:, 0:8].rearrange("p (j s) -> p j s", s=2)[:, :, s],
                    v("b_ada", 48 * l + 4 * c, 4), ALU.add)
                m.then_inc(dve_done, mark("dve", ("mod", l, c), ("free", ("ada_turned", l, c))))

        def gains_dve(l, which):
            for c in range(2 + 6 * which, 4 + 6 * which):
                nc.vector.wait_ge(dve_done, at(("mod", l, c)))
            for s in range(2):
                nc.vector.scalar_tensor_tensor(
                    gain[:, l, which, s, :], modv[:, l, 8 + 24 * which:16 + 24 * which, s], 1.0,
                    v(("norm_mix", "norm_ffn")[which], 8 * l, 8), ALU.add, ALU.mult).then_inc(dve_done, mark("dve", ("gain", l, which)))

        def residual_pe(key, chunks, act_in, groups):
            for ck, n0, nn in chunks:
                w = weights(ck)
                kt = w.shape[1]
                for j in range(nn):
                    for t0, tn in groups:
                        out = take((key, n0 + j, t0))[:, 0:tn]
                        m = mms(out, [(w[:, k, 128 * j:128 * j + 128], act_in(k, t0, tn)) for k in range(kt)])
                        m.then_inc(pe_done, mark("pe", (key, n0 + j, t0), used(ck)))

        def residual_dve(key, groups, g):
            for n in range(DT):
                for t0, tn in groups:
                    nc.vector.wait_ge(pe_done, at((key, n, t0)))
                    x = X[:, n, t0:t0 + tn]
                    o = bank_of((key, n, t0))[:, 0:tn]
                    if g is None:
                        m = nc.vector.tensor_tensor(x, o, x, ALU.add)
                    else:
                        m = nc.vector.scalar_tensor_tensor(x, o, g(n, 0 if t0 else 1), x, ALU.mult, ALU.add)
                    m.then_inc(dve_done, mark("dve", ("free", (key, n, t0)), ("res", key)))

        def start_pool():
            nc.gpsimd.dma_start(vec[:, :], io["vec"]).then_inc(consts_loaded, 16)
            nc.gpsimd.dma_start(mats[:, :, :], io["mats"]).then_inc(consts_loaded, 16)
            nc.gpsimd.dma_start(X[:, :, :], io["xT"]).then_inc(x_loaded, 16)
            w1 = gla_buf()["w1"]
            w2 = gla_buf()["w2"]
            for d in range(2):
                nc.gpsimd.dma_start(w1[:, d], io["gla_gate_w1"][0, d].rearrange("(t p) r -> p t r", p=P)
                                    ).then_inc(stage_loaded, 16)
                nc.gpsimd.dma_start(w2[0:16, d], io["gla_gate_w2"][0, d]).then_inc(stage_loaded, 16)
            loaded["gla_gates"] = 64

        loaded = {"gla_gates": 64}
        stage_total = [64]

        def stage_load(key, pairs):
            for dst, src in pairs:
                nc.gpsimd.dma_start(dst, src).then_inc(stage_loaded, 16)
                stage_total[0] += 16
            counts.at[("load", key)] = stage_total[0]

        def need_load(eng, key):
            if known:
                eng.wait_ge(stage_loaded, known.at[("load", key)])

        def start_act():
            nc.scalar.wait_ge(consts_loaded, 32)
            for s, name in enumerate(("c", "c_ctx")):
                nc.scalar.activation(cond[:, :, s], v(name, 0, 8), ACT.Silu).then_inc(act_done, mark("act", ("cond",)))
            for c in range(4):
                ada_act(0, c)

        def start_pe():
            nc.tensor.wait_ge(consts_loaded, 32)
            nc.tensor.wait_ge(act_done, at(("cond",)))
            for c in range(4):
                ada_pe(0, c)
                if c:
                    ada_turn_pe(0, c - 1)
            ada_turn_pe(0, 3)

        def start_dve():
            nc.vector.memset(eps[:, :], EPS).then_inc(dve_done, mark("dve", ("eps",)))
            nc.vector.wait_ge(consts_loaded, 32)
            for c in range(4):
                ada_dve(0, c)
            gains_dve(0, 0)

        def gla_buf():
            a = Carve()
            b = {}
            b["O"] = a(8, TOK)
            b["w1"] = a(2, DT, 16)
            b["w2"] = a(2, 512)
            b["z"] = a(2, TOK)
            b["reset"] = a(TOK)
            b["Q"] = a(TOK)
            b["K"] = a(TOK)
            b["V"] = a(6, 256)
            for d in range(2):
                for n in ("B", "E", "QD", "KI"):
                    b[n, d] = a(TOK)
                b["KT", d] = b["B", d].rearrange("p (t c) -> p t c", c=P)
                b["S", d] = a(2, 256)
                b["A", d] = a(P)
                b["EL", d] = a(12)
            return b

        gb = gla_buf()

        def gla_z_pe():
            nc.tensor.wait_ge(stage_loaded, loaded["gla_gates"])
            for d in range(2):
                for t0, tn in ALL:
                    out = take(("z", d, t0))[0:16, 0:tn]
                    m = mms(out, [(gb["w1"][:, d, k, :], H[:, k, t0:t0 + tn]) for k in range(DT)])
                    m.then_inc(pe_done, mark("pe", ("z", d, t0)))

        def gla_z_act():
            for d in range(2):
                for t0, tn in ALL:
                    nc.scalar.wait_ge(pe_done, at(("z", d, t0)))
                    nc.scalar.copy(gb["z"][0:16, d, t0:t0 + tn], bank_of(("z", d, t0))[0:16, 0:tn]).then_inc(act_done, mark("act", ("zs", d), ("free", ("z", d, t0))))

        def gla_z_dve():
            nc.vector.memset(gb["reset"], 1.0).then_inc(dve_done, mark("dve", ("reset1",)))
            nc.vector.wait_ge(dve_done, at(("reset1",)))
            nc.vector.memset(gb["reset"].rearrange("p (n c) -> p n c", c=GLA_C)[:, :, 0:1], 0.0).then_inc(dve_done, mark("dve", ("reset",)))
            nc.vector.memset(gb["O"], 0.0).then_inc(dve_done, mark("dve", ("Ozero",)))

        def gla_proj_pe(h):
            w = weights(("gla_in", h))
            for n, c0 in (("q", 0), ("k", 128)):
                for t0, tn in ALL:
                    out = take((n, h, t0))[:, 0:tn]
                    m = mms(out, [(w[:, k, c0:c0 + 128], H[:, k, t0:t0 + tn]) for k in range(DT)])
                    m.then_inc(pe_done, mark("pe", (n, h, t0)))
            for d in range(2):
                nc.tensor.wait_ge(act_done, at(("zs", d)))
                for t0, tn in ALL:
                    out = take(("g", h, d, t0))[:, 0:tn]
                    m = mms(out, [(gb["w2"][0:16, d, 128 * h:128 * h + 128], gb["z"][0:16, d, t0:t0 + tn])])
                    m.then_inc(pe_done, mark("pe", ("g", h, d, t0)))
            for t in range(6):
                out = take(("v", h, t))[:, 0:256]
                m = mms(out, [(H[:, k, 128 * t:128 * t + 128], w[:, k, 256:512]) for k in range(DT)])
                m.then_inc(pe_done, mark("pe", ("v", h, t), used(("gla_in", h))))
            ada_pe(0, 4 + 2 * h)
            ada_pe(0, 5 + 2 * h)
            for d in range(2):
                nc.tensor.wait_ge(dve_done, at(("KS", h, d)))
                for half in range(2):
                    out = take(("kt", h, d, half))
                    for i in range(3):
                        t = 3 * half + i
                        m = nc.tensor.transpose(out[:, 128 * i:128 * i + 128], gb["E", d][:, 128 * t:128 * t + 128], mat("ident"))
                    m.then_inc(pe_done, mark("pe", ("kt", h, d, half)))

            ada_turn_pe(0, 4 + 2 * h)
            ada_turn_pe(0, 5 + 2 * h)

        def gla_proj_act(h):
            for n, buf, sc in (("q", "Q", GLA_DK ** -0.5), ("k", "K", 1.0)):
                for t0, tn in ALL:
                    nc.scalar.wait_ge(pe_done, at((n, h, t0)))
                    nc.scalar.activation(gb[buf][:, t0:t0 + tn], bank_of((n, h, t0))[:, 0:tn], ACT.Identity, scale=sc).then_inc(act_done, mark("act", (buf, h), ("free", (n, h, t0))))
            for d in range(2):
                E = gb["E", d]
                for t0, tn in ALL:
                    nc.scalar.wait_ge(pe_done, at(("g", h, d, t0)))
                    nc.scalar.activation(E[:, t0:t0 + tn], bank_of(("g", h, d, t0))[:, 0:tn], ACT.Abs,
                                                     bias=v("gate_b", 4 * d + h)).then_inc(act_done, mark("act", ("abs", h, d), ("free", ("g", h, d, t0))))
            for d in range(2):
                E = gb["E", d]
                nc.scalar.wait_ge(act_done, at(("abs", h, d)))
                nc.scalar.activation(E, E, ACT.Exp, scale=-1.0).then_inc(act_done, mark("act", ("eabs", h, d)))
                nc.scalar.wait_ge(act_done, at(("eabs", h, d)))
                nc.scalar.activation(E, E, ACT.Ln, bias=1.0).then_inc(act_done, mark("act", ("softplus", h, d)))
            for t in range(6):
                nc.scalar.wait_ge(pe_done, at(("v", h, t)))
                nc.scalar.copy(gb["V"][:, t, :], bank_of(("v", h, t))[:, 0:256]).then_inc(act_done, mark("act", ("V", h), ("free", ("v", h, t))))
            ada_act(0, 4 + 2 * h)
            ada_act(0, 5 + 2 * h)
            for d in range(2):
                E, B = gb["E", d], gb["B", d]
                nc.scalar.wait_ge(dve_done, at(("B", h, d)))
                nc.scalar.activation(E, B, ACT.Exp, scale=1.0 / GATE_NORM).then_inc(act_done, mark("act", ("E1", h, d)))
            for d in range(2):
                E, B = gb["E", d], gb["B", d]
                nc.scalar.wait_ge(dve_done, at(("QD", h, d)))
                nc.scalar.activation(E, B, ACT.Exp, scale=-1.0 / GATE_NORM).then_inc(act_done, mark("act", ("E2", h, d)))
            for d in range(2):
                E = gb["E", d]
                nc.scalar.wait_ge(dve_done, at(("rest", h, d)))
                nc.scalar.activation(E, E, ACT.Exp, scale=1.0 / GATE_NORM).then_inc(act_done, mark("act", ("E3", h, d)))
            for d in range(2):
                for half in range(2):
                    nc.scalar.wait_ge(pe_done, at(("kt", h, d, half)))
                    nc.scalar.copy(gb["KT", d][:, 3 * half:3 * half + 3, :],
                                               bank_of(("kt", h, d, half))[:, 0:384].rearrange("p (t c) -> p t c", c=P)).then_inc(act_done, mark("act", ("KT", h, d), ("free", ("kt", h, d, half))))

        def chunks(a):
            return a.rearrange("p (n c) -> p n c", c=GLA_C)

        def gla_proj_dve(h):
            for d in range(2):
                for t0, tn in ALL:
                    nc.vector.wait_ge(act_done, at(("abs", h, d)))
                    nc.vector.tensor_scalar(gb["KI", d][:, t0:t0 + tn], bank_of(("g", h, d, t0))[:, 0:tn],
                                                        v("gate_b", 4 * d + h), 0.0, ALU.add, ALU.min).then_inc(dve_done, mark("dve", ("minz", h, d), ("free", ("g", h, d, t0))))
            for d in range(2):
                G, E, B = gb["KI", d], gb["E", d], gb["B", d]
                nc.vector.wait_ge(act_done, at(("softplus", h, d)))
                nc.vector.wait_ge(dve_done, at(("minz", h, d)))
                nc.vector.tensor_tensor(G, G, E, ALU.subtract).then_inc(dve_done, mark("dve", ("G", h, d)))
                nc.vector.wait_ge(dve_done, at(("G", h, d)))
                if d == 0:
                    o, g = B, G
                else:
                    o, g = B[:, ::-1], G[:, ::-1]
                nc.vector.tensor_tensor_scan(o, gb["reset"], g, 0.0, ALU.mult, ALU.add).then_inc(dve_done, mark("dve", ("B", h, d)))
            for d in range(2):
                nc.vector.wait_ge(act_done, at(("E1", h, d)))
                nc.vector.wait_ge(act_done, at(("Q", h)))
                E = gb["E", d]
                nc.vector.tensor_tensor(gb["QD", d], gb["Q"], E, ALU.mult).then_inc(dve_done, mark("dve", ("QD0", h, d)))
                last = GLA_C - 1 if d == 0 else 0
                nc.vector.tensor_copy(gb["EL", d], chunks(E)[:, :, last]).then_inc(dve_done, mark("dve", ("QD", h, d)))
            for d in range(2):
                E, B = gb["E", d], gb["B", d]
                last = GLA_C - 1 if d == 0 else 0
                nc.vector.wait_ge(act_done, at(("E2", h, d)))
                nc.vector.wait_ge(act_done, at(("K", h)))
                nc.vector.tensor_tensor(gb["KI", d], gb["K"], E, ALU.mult).then_inc(dve_done, mark("dve", ("KI", h, d)))
                nc.vector.wait_ge(dve_done, at(("KI", h, d)))
                bl = chunks(B)[:, :, last:last + 1].broadcast_to([P, TOK // GLA_C, GLA_C])
                nc.vector.tensor_tensor(chunks(E), bl, chunks(B), ALU.subtract).then_inc(dve_done, mark("dve", ("rest", h, d)))
            for d in range(2):
                nc.vector.wait_ge(act_done, at(("E3", h, d)))
                nc.vector.tensor_tensor(gb["E", d], gb["K"], gb["E", d], ALU.mult).then_inc(dve_done, mark("dve", ("KS", h, d)))
            ada_dve(0, 4 + 2 * h)
            ada_dve(0, 5 + 2 * h)

        TILES = [[0, 1, 2, 3, 4, 5], [1, 0, 5, 4, 3, 2]]

        def gla_scan_pe(h):
            nc.tensor.wait_ge(act_done, at(("V", h)))
            for s in range(6):
                for d in range(2):
                    t = TILES[d][s]
                    tk = slice(128 * t, 128 * t + 128)
                    nc.tensor.wait_ge(act_done, at(("KT", h, d)))
                    nc.tensor.wait_ge(dve_done, at(("QD", h, d)))
                    out = take(("a", h, s, d))[:, 0:128]
                    mms(out, [(gb["KI", d][:, tk], gb["QD", d][:, tk])]).then_inc(pe_done, mark("pe", ("a", h, s, d)))
                o = {}
                for d in range(2):
                    t = TILES[d][s]
                    nc.tensor.wait_ge(dve_done, at(("A", h, s, d)))
                    o[d] = take(("o", h, s, d))
                    for e in range(2):
                        nc.tensor.matmul(o[d][:, 128 * e:128 * e + 128], gb["V"][:, t, 128 * e:128 * e + 128], gb["A", d],
                                         start=(e == 0), stop=False, skip_group_check=True)
                for i in range(2):
                    for d in range(2):
                        t = TILES[d][s]
                        c = i if d == 0 else 1 - i
                        nc.tensor.wait_ge(dve_done, at(("S", h, 2 * s + i, d)))
                        S = gb["S", d][:, (2 * s + i) % 2, :]
                        ck = slice(128 * t + 64 * c, 128 * t + 64 * c + 64)
                        for e in range(2):
                            m = nc.tensor.matmul(o[d][:, 128 * e + 64 * c:128 * e + 64 * c + 64], S[:, 128 * e:128 * e + 128],
                                                 gb["QD", d][:, ck], start=False, stop=(i == 1), skip_group_check=True)
                        m.then_inc(pe_done, mark("pe", ("o", h, s, d)))
                        if 2 * s + i < 11:
                            out = take(("kv", h, 2 * s + i, d))[:, 0:256]
                            m = mms(out, [(gb["KT", d][64 * c:64 * c + 64, t, :], gb["V"][64 * c:64 * c + 64, t, :])])
                            m.then_inc(pe_done, mark("pe", ("kv", h, 2 * s + i, d)))

        def gla_scan_dve(h):
            for d in range(2):
                nc.vector.memset(gb["S", d][:, 0, :], 0.0).then_inc(dve_done, mark("dve", ("S", h, 0, d)))
            for s in range(6):
                for d in range(2):
                    nc.vector.wait_ge(pe_done, at(("a", h, s, d)))
                    if s:
                        nc.vector.wait_ge(pe_done, at(("o", h, s - 1, d)))
                    nc.vector.tensor_tensor(gb["A", d], bank_of(("a", h, s, d))[:, 0:128],
                                                        mat(("mask_fwd", "mask_bwd")[d]), ALU.mult).then_inc(dve_done, mark("dve", ("A", h, s, d), ("free", ("a", h, s, d))))
                for i in range(2):
                    for d in range(2):
                        n = 2 * s + i
                        t = TILES[d][s]
                        c = 2 * t + (i if d == 0 else 1 - i)
                        if n < 11:
                            nc.vector.wait_ge(pe_done, at(("kv", h, n, d)))
                            nc.vector.wait_ge(dve_done, at(("S", h, n, d)))
                            nc.vector.scalar_tensor_tensor(
                                gb["S", d][:, (n + 1) % 2, :], gb["S", d][:, n % 2, :], gb["EL", d][:, c:c + 1],
                                bank_of(("kv", h, n, d))[:, 0:256], ALU.mult, ALU.add).then_inc(dve_done, mark("dve", ("S", h, n + 1, d), ("free", ("kv", h, n, d))))
                for d in range(2):
                    t = TILES[d][s]
                    nc.vector.wait_ge(pe_done, at(("o", h, s, d)))
                    o = gb["O"][:, 2 * h:2 * h + 2, 128 * t:128 * t + 128]
                    if ("Oadd", h, t) in counts.at:
                        nc.vector.wait_ge(dve_done, at(("Oadd1", h, t)))
                    nc.vector.tensor_tensor(
                        o, bank_of(("o", h, s, d))[:, 0:256].rearrange("p (e t) -> p e t", e=2), o, ALU.add).then_inc(dve_done, mark("dve", ("Oadd", h, t), ("free", ("o", h, s, d)), *([] if ("Oadd", h, t) in counts.at else [("Oadd1", h, t)])))

        ga = Carve(8 * TOK)
        Y = ga(8, TOK)
        R0 = ga(2, SEQ)
        SR = ga(2, SEQ)
        gla_items = []
        for _h in range(GLA_H):
            for _t0, _tn in ALL:
                _s = [gb["O"][:, 2 * _h + e, _t0:_t0 + _tn] for e in range(2)]
                _d = [Y[:, 2 * _h + e, _t0:_t0 + _tn] for e in range(2)]
                gla_items.append((("glan", _h, _t0), _s, _d, _d, mat("mean256"), [v("gla_out_norm", e) for e in range(2)],
                                  None, R0[:, len(gla_items) % 2, 0:_tn]))

        def gla_r_pe():
            for c in range(2):
                w = weights(("gla_r", c))
                for j in range(4):
                    for t0, tn in ALL:
                        out = take(("r", 4 * c + j, t0))[:, 0:tn]
                        m = mms(out, [(w[:, k, 128 * j:128 * j + 128], H[:, k, t0:t0 + tn]) for k in range(DT)])
                        m.then_inc(pe_done, mark("pe", ("r", 4 * c + j, t0), used(("gla_r", c))))

        def gla_r_act():
            i = 0
            for n in range(8):
                for t0, tn in ALL:
                    nc.scalar.wait_ge(pe_done, at(("r", n, t0)))
                    if i >= 2:
                        nc.scalar.wait_ge(dve_done, at(("y", i - 2)))
                    nc.scalar.activation(SR[:, i % 2, 0:tn], bank_of(("r", n, t0))[:, 0:tn], ACT.Silu).then_inc(act_done, mark("act", ("silu_r", i), ("free", ("r", n, t0))))
                    i += 1

        def gla_r_dve():
            i = 0
            for n in range(8):
                for t0, tn in ALL:
                    nc.vector.wait_ge(act_done, at(("silu_r", i)))
                    nc.vector.wait_ge(dve_done, at(("normed", ("glan", n // 2, t0))))
                    y = Y[:, n, t0:t0 + tn]
                    nc.vector.tensor_tensor(y, y, SR[:, i % 2, 0:tn], ALU.mult).then_inc(dve_done, mark("dve", ("y", i)))
                    i += 1

        fa = Carve()
        inter = fa(FT, TOK)
        conv = fa(2, 2, TOK)

        def up_pe(tag, groups, extra):
            for c in range(FT // 2):
                w = weights(("up", tag, c))
                for jj in range(2):
                    j = 2 * c + jj
                    for part in range(2):
                        for t0, tn in groups:
                            out = take(("up", tag, j, part, t0))[:, 0:tn]
                            c0 = 256 * part + 128 * jj
                            m = mms(out, [(w[:, k, c0:c0 + 128], H[:, k, t0:t0 + tn]) for k in range(DT)])
                            m.then_inc(pe_done, mark("pe", ("up", tag, j, part, t0), used(("up", tag, c))))
                extra(c)

        def conv_act(tag, l, groups, extra):
            for j in range(FT):
                if j >= 2:
                    nc.scalar.wait_ge(dve_done, at(("inter", tag, j - 2)))
                for part in range(2):
                    t = 22 * part + j
                    for t0, tn in groups:
                        key = ("up", tag, j, part, t0)
                        nc.scalar.wait_ge(pe_done, at(key))
                        nc.scalar.activation(
                            conv[:, j % 2, part, t0:t0 + tn], bank_of(key)[:, 0:tn], ACT.Identity,
                            scale=v("conv_w", 132 * l + 44 + t), bias=v("conv_b", 44 * l + t)).then_inc(act_done, mark("act", ("mid", tag, j, part, t0), ("free", key)))
                g = conv[:, j % 2, 1, groups[0][0]:TOK]
                nc.scalar.wait_ge(dve_done, at(("conv", tag, j, 1)))
                nc.scalar.activation(g, g, ACT.Silu).then_inc(act_done, mark("act", ("silu", tag, j)))
                if j % 2:
                    extra(j // 2)

        def conv_dve(tag, l, groups, extra):
            for j in range(FT):
                for part in range(2):
                    t = 22 * part + j
                    for t0, tn in groups:
                        key = ("up", tag, j, part, t0)
                        u = bank_of(key)
                        cv = conv[:, j % 2, part, :]
                        nc.vector.wait_ge(act_done, at(("mid", tag, j, part, t0)))
                        nc.vector.scalar_tensor_tensor(
                            cv[:, t0 + 1:t0 + tn], u[:, 0:tn - 1], v("conv_w", 132 * l + t), cv[:, t0 + 1:t0 + tn],
                            ALU.mult, ALU.add).then_inc(dve_done, mark("dve", ("left", tag, j, part, t0)))
                        nc.vector.wait_ge(dve_done, at(("left", tag, j, part, t0)))
                        nc.vector.scalar_tensor_tensor(
                            cv[:, t0:t0 + tn - 1], u[:, 1:tn], v("conv_w", 132 * l + 88 + t), cv[:, t0:t0 + tn - 1],
                            ALU.mult, ALU.add).then_inc(dve_done, mark("dve", ("conv", tag, j, part), ("free", key)))
                nc.vector.wait_ge(act_done, at(("silu", tag, j)))
                nc.vector.wait_ge(dve_done, at(("conv", tag, j, 0)))
                t0 = groups[0][0]
                nc.vector.tensor_tensor(inter[:, j, t0:TOK], conv[:, j % 2, 0, t0:TOK],
                                                    conv[:, j % 2, 1, t0:TOK], ALU.mult).then_inc(dve_done, mark("dve", ("inter", tag, j)))
                if j % 2:
                    extra(j // 2)

        def swiglu_act(tag):
            for j in range(FT):
                nc.scalar.wait_ge(pe_done, at(("up", tag, j, 0, CTX)))
                if j >= 2:
                    nc.scalar.wait_ge(dve_done, at(("inter", tag, j - 2)))
                key = ("up", tag, j, 0, CTX)
                nc.scalar.activation(conv[:, j % 2, 0, 0:SEQ], bank_of(key), ACT.Silu).then_inc(act_done, mark("act", ("silu", tag, j), ("free", key)))

        def swiglu_dve(tag):
            for j in range(FT):
                key = ("up", tag, j, 1, CTX)
                nc.vector.wait_ge(pe_done, at(key))
                nc.vector.wait_ge(act_done, at(("silu", tag, j)))
                nc.vector.tensor_tensor(inter[:, j, CTX:TOK], bank_of(key), conv[:, j % 2, 0, 0:SEQ], ALU.mult).then_inc(dve_done, mark("dve", ("inter", tag, j), ("free", key)))

        def down_pe(tag, groups):
            residual_pe(("dn", tag), [(("down", tag, n), n, 1) for n in range(DT)],
                        lambda k, t0, tn: inter[:, k, t0:t0 + tn], groups)

        def attention(name, items, scale, P_, PT, S_, small, combine=None):
            N = len(items)

            def sm(i, c, what):
                at = ((i % 4) * 2 + c) * 4 + what
                return small[:, at:at + 1]

            def scores_ap(i, c):
                it = items[i]
                b = (i % 2) * 2 + c
                return ps[:, b:b + 2, :].rearrange("p b n -> p (b n)")[:, 0:it["keys"]] if it["keys"] > BANK else ps[:, b, 0:it["keys"]]

            def skeys(i, c):
                it = items[i]
                return [(name, "s", i, c, b) for b in range(-(-it["keys"] // BANK))]

            def scores_pe(i):
                it = items[i]
                for c in range(len(it["prods"])):
                    for b, key in enumerate(skeys(i, c)):
                        k0, k1 = BANK * b, min(BANK * b + BANK, it["keys"])
                        out = take(key, (i % 2) * 2 + c + b)[:, 0:k1 - k0]
                        m = mms(out, [(q, k[:, k0:k1]) for q, k in it["prods"][c]])
                        m.then_inc(pe_done, mark("pe", (name, "scores", i, c)))

            def trans_pe(i):
                it = items[i]
                nc.tensor.wait_ge(dve_done, at((name, "p", i)))
                nb = it["keys"] // P
                for b in range(0, nb, 4):
                    out = take((name, "t", i, b), 4 + b // 4 if it["keys"] > BANK else 4 + i % 2)
                    for k in range(b, min(b + 4, nb)):
                        m = nc.tensor.transpose(out[:, 128 * (k - b):128 * (k - b) + 128],
                                                P_[:, i % 3, 0, 128 * k:128 * k + 128], mat("ident"))
                    m.then_inc(pe_done, mark("pe", (name, "t", i, b)))

            def pv_pe(i):
                it = items[i]
                nb = it["keys"] // P
                po, pn = it["part"]
                nc.tensor.wait_ge(act_done, at((name, "pt", i)))
                out = take((name, "o", i), 6 + i % 2)[po:po + pn, 0:P]
                m = mms(out, [(it["v"](k), PT[:, i % 2, 128 * k:128 * k + 128]) for k in range(nb)])
                m.then_inc(pe_done, mark("pe", (name, "o", i)))

            def pe():
                for s in range(N + 3):
                    if s < N:
                        scores_pe(s)
                    if 0 <= s - 2 < N:
                        trans_pe(s - 2)
                    if 0 <= s - 3 < N:
                        pv_pe(s - 3)

            def smax_dve(i):
                it = items[i]
                for c in range(len(it["prods"])):
                    nc.vector.wait_ge(pe_done, at((name, "scores", i, c)))
                    s = scores_ap(i, c)
                    if it["mask"] == "edge":
                        nc.vector.memset(s[0:64, it["keys"] - 64:it["keys"]], NEG).then_inc(dve_done, mark("dve", (name, "edge", i, c)))
                        nc.vector.wait_ge(dve_done, at((name, "edge", i, c)))
                    elif it["mask"] is not None:
                        if i >= 2:
                            nc.vector.wait_ge(act_done, at((name, "e", i - 2)))
                        sc, bias = it["mask"]
                        S = S_[:, i % 2, 0:it["keys"]]
                        nc.vector.scalar_tensor_tensor(S, s, sc, bias, ALU.mult, ALU.add).then_inc(dve_done, mark("dve", (name, "biased", i), *[("free", k) for k in skeys(i, c)]))
                        nc.vector.wait_ge(dve_done, at((name, "biased", i)))
                        s = S
                    nc.vector.tensor_reduce(sm(i, c, 0), s, AXX, ALU.max).then_inc(dve_done, mark("dve", (name, "max", i, c)))
                    nc.vector.wait_ge(dve_done, at((name, "max", i, c)))
                    nc.vector.tensor_scalar(sm(i, c, 1), sm(i, c, 0), -scale, None, ALU.mult).then_inc(dve_done, mark("dve", (name, "nmax", i, c)))

            def norm_dve_(i):
                it = items[i]
                p = P_[:, i % 3, 0, 0:it["keys"]]
                for c in range(len(it["prods"])):
                    nc.vector.wait_ge(act_done, at((name, "e", i, c)))
                    nc.vector.reciprocal(sm(i, c, 3), sm(i, c, 2)).then_inc(dve_done, mark("dve", (name, "r", i, c)))
                if len(it["prods"]) == 2:
                    p1 = P_[:, i % 3, 1, 0:it["keys"]]
                    nc.vector.wait_ge(dve_done, at((name, "r", i, 1)))
                    nc.vector.tensor_scalar(p1, p1, sm(i, 1, 3), combine, ALU.mult, ALU.mult).then_inc(dve_done, mark("dve", (name, "p1", i)))
                    nc.vector.wait_ge(dve_done, at((name, "p1", i)))
                    nc.vector.scalar_tensor_tensor(p, p, sm(i, 0, 3), p1, ALU.mult, ALU.add).then_inc(dve_done, mark("dve", (name, "p", i)))
                else:
                    nc.vector.wait_ge(dve_done, at((name, "r", i, 0)))
                    nc.vector.tensor_scalar(p, p, sm(i, 0, 3), None, ALU.mult).then_inc(dve_done, mark("dve", (name, "p", i)))

            def dve():
                for s in range(N + 1):
                    if s < N:
                        smax_dve(s)
                    if s:
                        norm_dve_(s - 1)

            def exp_act(i):
                it = items[i]
                if i >= 3:
                    for b in range(0, it["keys"] // P, 4):
                        if (name, "t", i - 3, b) in (known.at if known else {}):
                            nc.scalar.wait_ge(pe_done, at((name, "t", i - 3, b)))
                    nc.scalar.wait_ge(pe_done, at((name, "t", i - 3, 0)))
                for c in range(len(it["prods"])):
                    nc.scalar.wait_ge(dve_done, at((name, "nmax", i, c)))
                    biased = it["mask"] is not None and it["mask"] != "edge"
                    s = S_[:, i % 2, 0:it["keys"]] if biased else scores_ap(i, c)
                    nc.scalar.activation(P_[:, i % 3, c, 0:it["keys"]], s, ACT.Exp, scale=scale,
                                                     bias=sm(i, c, 1), accum_out=sm(i, c, 2)).then_inc(act_done, mark("act", (name, "e", i, c), (name, "e", i), *([] if biased else [("free", k) for k in skeys(i, c)])))

            def pt_act(i):
                it = items[i]
                nb = it["keys"] // P
                if i >= 2:
                    nc.scalar.wait_ge(pe_done, at((name, "o", i - 2)))
                for b in range(0, nb, 4):
                    nc.scalar.wait_ge(pe_done, at((name, "t", i, b)))
                    n = 128 * (min(b + 4, nb) - b)
                    nc.scalar.copy(PT[:, i % 2, 128 * b:128 * b + n],
                                               ps[:, 4 + b // 4 if it["keys"] > BANK else 4 + i % 2, 0:n]).then_inc(act_done, mark("act", (name, "pt", i), ("free", (name, "t", i, b))))

            def o_act(i):
                po, pn = items[i]["part"]
                nc.scalar.wait_ge(pe_done, at((name, "o", i)))
                nc.scalar.copy(items[i]["out"], ps[po:po + pn, 6 + i % 2, 0:P]).then_inc(act_done, mark("act", ("free", (name, "o", i)), (name, "O")))

            def act():
                for s in range(N + 3):
                    if s < N:
                        exp_act(s)
                    if 0 <= s - 2 < N:
                        pt_act(s - 2)
                    if 0 <= s - 3 < N:
                        o_act(s - 3)

            return {"pe": pe, "act": act, "dve": dve}

        def rope_pe(items, perm):
            for key, a, k, ready in items:
                if by_act := at(ready, "act"):
                    nc.tensor.wait_ge(act_done, by_act)
                if by_dve := at(ready, "dve"):
                    nc.tensor.wait_ge(dve_done, by_dve)
                out = take(("rot", key))[0:k, :]
                mms(out, [(mat(perm)[0:k, 0:k], a)]).then_inc(pe_done, mark("pe", ("rot", key)))

        def rope_dve(items, tab, tmp):
            for i, (key, a, k, ready) in enumerate(items):
                nc.vector.wait_ge(pe_done, at(("rot", key)))
                u = tmp[0:k, i % 2, :]
                if i >= 2:
                    nc.vector.wait_ge(dve_done, at(("roped", items[i - 2][0])))
                nc.vector.tensor_tensor(u, bank_of(("rot", key))[0:k, :], tab[0:k, 1, :], ALU.mult).then_inc(dve_done, mark("dve", ("ru", key), ("free", ("rot", key))))
                nc.vector.tensor_tensor(a, a, tab[0:k, 0, :], ALU.mult).then_inc(dve_done, mark("dve", ("rc", key)))
                nc.vector.wait_ge(dve_done, at(("rc", key)))
                nc.vector.tensor_tensor(a, a, u, ALU.add).then_inc(dve_done, mark("dve", ("roped", key)))

        ma = Carve()
        tabs = ma(2, SEQ)
        CQ = ma(3, SEQ)
        CKV = ma(2, TOK)
        KPE = ma(TOK)
        SQ = ma(3, SEQ)
        MR = ma(2, SEQ)
        RT = SQ[:, 0:2, :]
        Q4 = ma(4, SEQ)
        QP = ma(2, SEQ)
        K4 = ma(4, TOK)
        V4 = ma(6, SEQ)
        MP = ma(3, 1, TOK)
        MPT = ma(2, TOK)
        MS = ma(32)

        def down_items():
            its = [(("cq",), [CQ[:, k, :] for k in range(3)], [SQ[:, k, :] for k in range(3)], [CQ[:, k, :] for k in range(3)],
                    mat("mean384"), [v("q_lora_norm", k) for k in range(3)], None, MR[:, 0, :])]
            for i, (t0, tn) in enumerate(ALL):
                t = [CKV[:, k, t0:t0 + tn] for k in range(2)]
                its.append((("ckv", t0), t, [SQ[:, k, 0:tn] for k in range(2)], t, mat("mean256"),
                            [v("kv_lora_norm", k) for k in range(2)], None, MR[:, 0, 0:tn]))
            for i, (t0, tn) in enumerate(ALL):
                t = [KPE[0:64, t0:t0 + tn]]
                its.append((("kpe", t0), t, [SQ[0:64, 0, 0:tn]], t, mat("mean64"), [v("k_norm_rope", 0)[0:64]], None,
                            MR[0:64, 0, 0:tn]))
            return its

        mla_down_items = down_items()

        def mla_down_pe():
            w = weights(("mla_dq",))
            for n in range(3):
                out = take(("dq", n))
                m = mms(out, [(w[:, k, 128 * n:128 * n + 128], H[:, k, CTX:TOK]) for k in range(DT)])
                m.then_inc(pe_done, mark("pe", ("dq", n), used(("mla_dq",))))
            w = weights(("mla_dkv",))
            for n in range(3):
                mm = 128 if n < 2 else 64
                for t0, tn in ALL:
                    out = take(("dkv", n, t0))[0:mm, 0:tn]
                    m = mms(out, [(w[:, k, 128 * n:128 * n + mm], H[:, k, t0:t0 + tn]) for k in range(DT)])
                    m.then_inc(pe_done, mark("pe", ("dkv", n, t0), used(("mla_dkv",))))

        def mla_down_act():
            for n in range(3):
                nc.scalar.wait_ge(pe_done, at(("dq", n)))
                nc.scalar.copy(CQ[:, n, :], bank_of(("dq", n))).then_inc(act_done, mark("act", ("free", ("dq", n)), ("CQ",)))
            for n in range(3):
                for t0, tn in ALL:
                    nc.scalar.wait_ge(pe_done, at(("dkv", n, t0)))
                    dst = CKV[:, n, t0:t0 + tn] if n < 2 else KPE[0:64, t0:t0 + tn]
                    k = 128 if n < 2 else 64
                    nc.scalar.copy(dst, bank_of(("dkv", n, t0))[0:k, 0:tn]).then_inc(act_done, mark("act", ("free", ("dkv", n, t0)), ("CKV",)))

        kpe_rope = [("kpe", KPE[0:64, CTX:TOK], 64, ("normed", ("kpe", CTX)))]

        def mla_rest_pe():
            norm_pe(mla_down_items)
            rope_pe(kpe_rope, "perm_axial")

        def mla_rest_act():
            nc.scalar.wait_ge(act_done, at(("CKV",)))
            norm_act(mla_down_items)

        def mla_rest_dve():
            norm_dve(mla_down_items)
            need_load(nc.vector, "axial")
            rope_dve(kpe_rope, tabs, RT)
            nc.vector.wait_ge(dve_done, at(("roped", "kpe")))
            nc.vector.tensor_copy(KPE[64:128, :], KPE[0:64, :]).then_inc(dve_done, mark("dve", ("kpe2",)))

        def uq_pe(g):
            w = weights(("mla_uq", g)).rearrange("p t (h c) -> p t h c", c=192)
            for h in range(4):
                out = take(("uq", g, h))
                m = mms(out, [(w[:, k, h, 0:128], CQ[:, k, :]) for k in range(3)])
                m.then_inc(pe_done, mark("pe", ("uq", g, h)))
            for i in range(2):
                for half in range(2):
                    out = take(("uqr", g, i, half))[0:64, :]
                    m = mms(out, [(w[:, k, 2 * i + half, 128:192], CQ[:, k, :]) for k in range(3)])
                    m.then_inc(pe_done, mark("pe", ("uqr", g, i, half), used(("mla_uq", g))))
            w = weights(("mla_ukv", g)).rearrange("p t (h c) -> p t h c", c=256)
            for h in range(4):
                for t0, tn in ALL:
                    out = take(("uk", g, h, t0))[:, 0:tn]
                    m = mms(out, [(w[:, k, h, 0:128], CKV[:, k, t0:t0 + tn]) for k in range(2)])
                    m.then_inc(pe_done, mark("pe", ("uk", g, h, t0)))
            for t in range(6):
                out = take(("uv", g, t)).rearrange("p (h c) -> p h c", c=128)
                m = mms(out, [(CKV[:, k, 128 * t:128 * t + 128], w[:, k, :, 128:256]) for k in range(2)])
                m.then_inc(pe_done, mark("pe", ("uv", g, t), used(("mla_ukv", g))))

        def uq_act(g):
            for h in range(4):
                nc.scalar.wait_ge(pe_done, at(("uq", g, h)))
                nc.scalar.copy(Q4[:, h, :], bank_of(("uq", g, h))).then_inc(act_done, mark("act", ("free", ("uq", g, h)), ("Q4", g)))
            for i in range(2):
                for half in range(2):
                    nc.scalar.wait_ge(pe_done, at(("uqr", g, i, half)))
                    nc.scalar.copy(QP[64 * half:64 * half + 64, i, :], bank_of(("uqr", g, i, half))[0:64, :]).then_inc(act_done, mark("act", ("free", ("uqr", g, i, half)), ("Q4", g)))
            for h in range(4):
                for t0, tn in ALL:
                    nc.scalar.wait_ge(pe_done, at(("uk", g, h, t0)))
                    nc.scalar.copy(K4[:, h, t0:t0 + tn], bank_of(("uk", g, h, t0))[:, 0:tn]).then_inc(act_done, mark("act", ("free", ("uk", g, h, t0)), ("Q4", g)))

        def uq_dve(g):
            for t in range(6):
                nc.vector.wait_ge(pe_done, at(("uv", g, t)))
                nc.vector.tensor_copy(V4[:, t, :], bank_of(("uv", g, t))).then_inc(dve_done, mark("dve", ("free", ("uv", g, t)), ("V4", g)))

        def qk_items(g):
            its = []

            def add(key, t, mean, gn, n):
                i = len(its) % 2
                its.append((key, [t], [SQ[:, i, 0:n]], [t], mat(mean), [gn], None, MR[:, i, 0:n]))

            for i in range(2):
                add(("qp", g, i), QP[:, i, :], "mean64", v("q_norm_rope", 0), SEQ)
            for h in range(4):
                add(("qn", g, h), Q4[:, h, :], "mean128", v("q_norm_nope", 0), SEQ)
                for t0, tn in ALL:
                    add(("kn", g, h, t0), K4[:, h, t0:t0 + tn], "mean128", v("k_norm_nope", 0), tn)
            return its

        def mla_attention(g):
            its = []
            for h in range(4):
                e = 64 * (h % 2)
                for qt in range(4):
                    qs = slice(128 * qt, 128 * qt + 128)
                    its.append(dict(keys=TOK, mask=None, part=(0, P),
                                    prods=[[(Q4[:, h, qs], K4[:, h, :]),
                                            (QP[e:e + 64, h // 2, qs], KPE[e:e + 64, :])]],
                                    v=lambda k, h=h: V4[:, k, 128 * h:128 * h + 128],
                                    out=H[:, 4 * g + h, CTX + 128 * qt:CTX + 128 * qt + 128]))
            return attention(("mla", g), its, 192 ** -0.5, MP, MPT, None, MS)

        mla_att = [mla_attention(g) for g in range(2)]
        mla_qk = [qk_items(g) for g in range(2)]
        q_rope = [[(("qp", g, i), QP[:, i, :], P, ("normed", ("qp", g, i))) for i in range(2)] for g in range(2)]

        ba = Carve()
        btab = ba(2, SEQ)
        OO = [ba(4, SEQ) for _ in range(3)]
        QB = ba(4, SEQ)
        KB = ba(4, SEQ)
        VB = ba(4, SEQ)
        M_ = ba(4, SEQ)
        BP = ba(3, 2, SEQ)
        BPT = ba(2, SEQ)
        BS_ = ba(2, SEQ)
        BSM = ba(32)
        WI = ba(4, 4)
        LV = ba(4, HD)
        LAM = ba(8)
        MX8 = ba(8)
        BRT = BPT
        TT = Carve(1024 + 4 * SEQ)(8, SEQ)
        bc = Carve(1024 + 4 * SEQ)
        QI = bc(2, SEQ)
        KIX = bc(SEQ)
        WK = bc(2, SEQ)
        IT = bc(2, SEQ)
        Y2 = Carve(1024 + 3 * 2048)(8, SEQ)
        xa = Carve(1024)
        XQ = xa(2, SEQ)
        XK = xa(2, CTX)
        XV = xa(2, CTX)
        XO = xa(2, SEQ)
        XP = xa(3, 1, CTX)
        XPT = xa(2, CTX)
        XS = xa(32)
        h_main = [H[:, k, CTX:TOK] for k in range(DT)]

        def idx_pe(l):
            w = weights(("idx", l))
            for n in range(3):
                k_ = 128 if n < 2 else 64
                out = take(("ip", l, n))[0:k_, :]
                mms(out, [(w[:, k, 128 * n:128 * n + k_], h_main[k]) for k in range(DT)]).then_inc(pe_done, mark("pe", ("ip", l, n)))
            out = take(("wi", l))
            for t in range(4):
                m = mms(out[:, 4 * t:4 * t + 4], [(H[:, k, CTX + 128 * t:CTX + 128 * t + 128], w[:, k, 320:324]) for k in range(DT)])
            m.then_inc(pe_done, mark("pe", ("wi", l), used(("idx", l))))
            rope_pe(idx_rope[l], "perm_half")

        idx_rope = [[(("ix", l, n), QI[:, n, :] if n < 2 else KIX[0:64, :], P if n < 2 else 64, ("ips", l, n))
                     for n in range(3)] for l in range(2)]

        def idx_act(l):
            for n in range(3):
                k_ = 128 if n < 2 else 64
                dst = QI[:, n, :] if n < 2 else KIX[0:64, :]
                nc.scalar.wait_ge(pe_done, at(("ip", l, n)))
                nc.scalar.copy(dst, bank_of(("ip", l, n))[0:k_, :]).then_inc(act_done, mark("act", ("free", ("ip", l, n)), ("ips", l, n)))

        def idx_dve(l):
            nc.vector.wait_ge(pe_done, at(("wi", l)))
            nc.vector.tensor_scalar(WI, bank_of(("wi", l))[:, 0:16].rearrange("p (t h) -> p t h", h=4),
                                                0.5 * HD ** -0.5, None, ALU.mult).then_inc(dve_done, mark("dve", ("free", ("wi", l)), ("WI", l)))
            need_load(nc.vector, ("half", l))
            rope_dve(idx_rope[l], btab, BRT)
            nc.vector.wait_ge(dve_done, at(("roped", ("ix", l, 2))))
            nc.vector.tensor_copy(KIX[64:128, :], KIX[0:64, :]).then_inc(dve_done, mark("dve", ("kix2", l)))

        def logits_pe(l):
            for qt in range(1, 4):
                n = 128 * qt + 128
                for h in range(4):
                    e = 64 * (h % 2)
                    out = take(("lg", l, qt, h))[:, 0:n]
                    m = mms(out, [(QI[e:e + 64, h // 2, 128 * qt:128 * qt + 128], KIX[e:e + 64, 0:n])])
                    m.then_inc(pe_done, mark("pe", ("lg", l, qt, h)))

        def topk_dve(l):
            nc.vector.memset(M_[:, 0, 0:P], 0.0).then_inc(dve_done, mark("dve", ("m0", l)))
            nc.vector.wait_ge(dve_done, at(("m0", l)))
            nc.vector.memset(M_[0:64, 0, 64:128], NEG).then_inc(dve_done, mark("dve", ("mask", l)))
            for qt in range(1, 4):
                n = 128 * qt + 128
                cur, tmp, acc = WK[:, 0, 0:n], IT[:, 0, 0:n], WK[:, 1, 0:n]
                for h in range(4):
                    nc.vector.wait_ge(pe_done, at(("lg", l, qt, h)))
                    dst = acc if h == 0 else tmp
                    if h >= 2:
                        nc.vector.wait_ge(dve_done, at(("acc", l, qt, h - 1)))
                    elif h == 0 and qt > 1:
                        nc.vector.wait_ge(dve_done, at(("m1", l, qt - 1)))
                    nc.vector.tensor_scalar(dst, bank_of(("lg", l, qt, h))[:, 0:n], 0.0, WI[:, qt, h:h + 1],
                                                        ALU.max, ALU.mult).then_inc(dve_done, mark("dve", ("free", ("lg", l, qt, h)), ("lr", l, qt, h)))
                    if h:
                        nc.vector.wait_ge(dve_done, at(("lr", l, qt, h)))
                        nc.vector.tensor_tensor(acc, acc, tmp, ALU.add).then_inc(dve_done, mark("dve", ("acc", l, qt, h)))
                nc.vector.wait_ge(dve_done, at(("acc", l, qt, 3)))
                nc.vector.memset(acc[0:64, n - 64:n], NEG).then_inc(dve_done, mark("dve", ("sc", l, qt, 0)))
                a, b = acc, cur
                for r in range(TOPK // 8):
                    nc.vector.wait_ge(dve_done, at(("sc", l, qt, r)))
                    nc.vector.max(MX8, a).then_inc(dve_done, mark("dve", ("mx", l, qt, r)))
                    nc.vector.wait_ge(dve_done, at(("mx", l, qt, r)))
                    nc.vector.match_replace(b, MX8, a, TAKEN).then_inc(dve_done, mark("dve", ("sc", l, qt, r + 1)))
                    a, b = b, a
                nc.vector.wait_ge(dve_done, at(("sc", l, qt, TOPK // 8)))
                nc.vector.tensor_scalar(M_[:, qt, 0:n], a, 0.1 * TAKEN, NEG, ALU.is_gt, ALU.mult).then_inc(dve_done, mark("dve", ("m1", l, qt)))
                nc.vector.wait_ge(dve_done, at(("m1", l, qt)))
                nc.vector.memset(M_[0:64, qt, n - 64:n], NEG).then_inc(dve_done, mark("dve", ("mask", l)))

        def qkv_pe(l, b, rope):
            for n, c in enumerate((3 * b, 3 * b + 1)):
                w = weights(("in", l, c))
                for j in range(4):
                    out = take(("qk", l, b, n, j))
                    m = mms(out, [(w[:, k, 128 * j:128 * j + 128], h_main[k]) for k in range(DT)])
                    m.then_inc(pe_done, mark("pe", ("qk", l, b, n, j), used(("in", l, c))))
            w = weights(("in", l, 3 * b + 2))
            for t in range(4):
                out = take(("vv", l, b, t))
                m = mms(out, [(H[:, k, CTX + 128 * t:CTX + 128 * t + 128], w[:, k, :]) for k in range(DT)])
                m.then_inc(pe_done, mark("pe", ("vv", l, b, t), used(("in", l, 3 * b + 2))))
            if rope:
                rope_pe(qk_rope(l, b), "perm_half")

        def qk_rope(l, b):
            return [(("qk", l, b, n, j), (QB, KB)[n][:, j, :], P, ("qks", l, b, n, j)) for n in range(2) for j in range(4)]

        def qkv_act(l, b):
            for n in range(2):
                for j in range(4):
                    nc.scalar.wait_ge(pe_done, at(("qk", l, b, n, j)))
                    nc.scalar.copy((QB, KB)[n][:, j, :], bank_of(("qk", l, b, n, j))).then_inc(act_done, mark("act", ("free", ("qk", l, b, n, j)), ("qks", l, b, n, j)))
            for t in range(4):
                nc.scalar.wait_ge(pe_done, at(("vv", l, b, t)))
                nc.scalar.copy(VB[:, t, :], bank_of(("vv", l, b, t))).then_inc(act_done, mark("act", ("free", ("vv", l, b, t))))

        def flip_pe(l):
            need_load(nc.tensor, ("tt", l))
            for h in range(8):
                out = take(("fl", l, h))
                mms(out, [(mat("flip"), TT[:, h, :])]).then_inc(pe_done, mark("pe", ("fl", l, h)))

        def flip_act(l):
            for h in range(8):
                nc.scalar.wait_ge(pe_done, at(("fl", l, h)))
                nc.scalar.copy(TT[:, h, :], bank_of(("fl", l, h))).then_inc(act_done, mark("act", ("free", ("fl", l, h)), ("TT", l)))

        def mix_attention(l, b):
            its = []
            nh = 4 if b == 1 else 8
            for h in range(nh):
                for qt in range(4):
                    n = 128 * qt + 128
                    qs = slice(128 * qt, 128 * qt + 128)
                    if b == 1:
                        prods = [[(QB[e:e + 64, h, qs], KB[e:e + 64, h, :])] for e in (0, 64)]
                        part, vv = (0, P), (lambda k, h=h: VB[:, k, 128 * h:128 * h + 128])
                        out = OO[1][:, h, qs]
                        mask = "edge"
                    else:
                        e = 64 * (h % 2)
                        prods = [[(QB[e:e + 64, h // 2, qs], KB[e:e + 64, h // 2, :])]]
                        part, vv = (e, 64), (lambda k, h=h: VB[:, k, 64 * h:64 * h + 64])
                        out = OO[b][e:e + 64, h // 2, qs]
                        mask = (HD ** -0.5, TT[:, h, 384 - 128 * qt:512]) if b == 0 else (1.0, M_[:, qt, 0:n])
                    its.append(dict(keys=n, mask=mask, part=part, prods=prods, v=vv, out=out))
            return attention(("mix", l, b), its, 1.0 if b == 0 else HD ** -0.5, BP, BPT, BS_, BSM,
                             combine=LAM[:, 4:5] if b == 1 else None)

        mix_att = {(l, b): mix_attention(l, b) for l in range(2) for b in range(3)}

        def lam_init(l):
            return 0.8 - 0.6 * math.exp(-0.3 * l)

        def lambda_dve(l):
            need_load(nc.vector, ("half", l))
            for i in range(2):
                nc.vector.tensor_tensor(LV[:, 2 * i, :], LV[:, 2 * i, :], LV[:, 2 * i + 1, :], ALU.mult).then_inc(dve_done, mark("dve", ("lm", l, i)))
                nc.vector.wait_ge(dve_done, at(("lm", l, i)))
                nc.vector.tensor_reduce(LAM[:, i:i + 1], LV[:, 2 * i, :], AXX, ALU.add).then_inc(dve_done, mark("dve", ("ls", l)))
            nc.vector.wait_ge(act_done, at(("le", l)))
            nc.vector.tensor_tensor(LAM[:, 5:6], LAM[:, 3:4], LAM[:, 2:3], ALU.subtract).then_inc(dve_done, mark("dve", ("ld", l)))
            nc.vector.wait_ge(dve_done, at(("ld", l)))
            nc.vector.tensor_scalar(LAM[:, 4:5], LAM[:, 5:6], -lam_init(l), None, ALU.add).then_inc(dve_done, mark("dve", ("lam", l)))

        def lambda_act(l):
            nc.scalar.wait_ge(dve_done, at(("ls", l)))
            nc.scalar.activation(LAM[:, 2:4], LAM[:, 0:2], ACT.Exp).then_inc(act_done, mark("act", ("le", l)))

        def subln_items(l):
            its = []
            for h in range(4):
                o = OO[1][:, h, :]
                its.append((("subln", l, h), [o], [BP[:, 0, h % 2, :]], [o], mat("mean128"), [LAM[:, 6:7]], None,
                            BP[:, 1, h % 2, :]))
            return its

        def gate_pe(l):
            for c in range(2):
                for b in range(3):
                    w = weights(("gate", l, b, c))
                    for j in range(4):
                        out = take(("gt", l, b, c, j))
                        m = mms(out, [(w[:, k, 128 * j:128 * j + 128], h_main[k]) for k in range(DT)])
                        m.then_inc(pe_done, mark("pe", ("gt", l, b, c, j), used(("gate", l, b, c))))
                    w = weights(("mixup", l, b, c))
                    for j in range(4):
                        out = take(("mu", l, b, c, j))
                        m = mms(out, [(w[:, k, 128 * j:128 * j + 128], OO[b][:, k, :]) for k in range(4)])
                        m.then_inc(pe_done, mark("pe", ("mu", l, b, c, j), used(("mixup", l, b, c))))

        GS4 = Carve(1024 + 3 * 2048 + 8 * SEQ)
        GSB = GS4(4, SEQ)
        YTB = GS4(2, SEQ)

        def gate_act(l):
            i = 0
            for c in range(2):
                for b in range(3):
                    for j in range(4):
                        nc.scalar.wait_ge(pe_done, at(("gt", l, b, c, j)))
                        if i >= 4:
                            nc.scalar.wait_ge(dve_done, at(("gated", l, i - 4)))
                        nc.scalar.activation(GSB[:, i % 4, :], bank_of(("gt", l, b, c, j)), ACT.Sigmoid).then_inc(act_done, mark("act", ("free", ("gt", l, b, c, j)), ("sig", l, i)))
                        i += 1

        def gate_dve(l):
            i = 0
            for c in range(2):
                for b in range(3):
                    for j in range(4):
                        nc.vector.wait_ge(pe_done, at(("mu", l, b, c, j)))
                        nc.vector.wait_ge(act_done, at(("sig", l, i)))
                        y = Y2[:, 4 * c + j, :]
                        dst = y if b == 0 else YTB[:, i % 2, :]
                        if b and (i - 2) // 4 % 3:
                            nc.vector.wait_ge(dve_done, at(("summed", l, i - 2)))
                        nc.vector.tensor_tensor(dst, bank_of(("mu", l, b, c, j)), GSB[:, i % 4, :], ALU.mult).then_inc(dve_done, mark("dve", ("free", ("mu", l, b, c, j)), ("gated", l, i)))
                        if b:
                            nc.vector.wait_ge(dve_done, at(("gated", l, i)))
                            nc.vector.tensor_tensor(y, y, dst, ALU.add).then_inc(dve_done, mark("dve", ("summed", l, i)))
                        i += 1

        def cross_pe(l):
            w = weights(("xkv", l))
            for j in range(2):
                out = take(("xk", l, j))[:, 0:CTX]
                mms(out, [(w[:, k, 128 * j:128 * j + 128], X[:, k, 0:CTX]) for k in range(DT)]).then_inc(pe_done, mark("pe", ("xk", l, j)))
            for t in range(2):
                out = take(("xv", l, t))[:, 0:CTX]
                m = mms(out, [(X[:, k, 128 * t:128 * t + 128], w[:, k, 256:512]) for k in range(DT)])
                m.then_inc(pe_done, mark("pe", ("xv", l, t), used(("xkv", l))))
            w = weights(("xq", l))
            for j in range(2):
                out = take(("xq", l, j))
                m = mms(out, [(w[:, k, 128 * j:128 * j + 128], h_main[k]) for k in range(DT)])
                m.then_inc(pe_done, mark("pe", ("xq", l, j), used(("xq", l))))

        def cross_act(l):
            for n, dst, w in (("xk", XK, CTX), ("xv", XV, CTX), ("xq", XQ, SEQ)):
                for j in range(2):
                    nc.scalar.wait_ge(pe_done, at((n, l, j)))
                    nc.scalar.copy(dst[:, j, :], bank_of((n, l, j))[:, 0:w]).then_inc(act_done, mark("act", ("free", (n, l, j))))

        def cross_attention(l):
            its = []
            for h in range(4):
                e = 64 * (h % 2)
                for qt in range(4):
                    qs = slice(128 * qt, 128 * qt + 128)
                    its.append(dict(keys=CTX, mask=None, part=(e, 64),
                                    prods=[[(XQ[e:e + 64, h // 2, qs], XK[e:e + 64, h // 2, :])]],
                                    v=lambda k, h=h: XV[:, k, 64 * h:64 * h + 64], out=XO[e:e + 64, h // 2, qs]))
            return attention(("cross", l), its, HD ** -0.5, XP, XPT, None, XS)

        cross_att = [cross_attention(l) for l in range(2)]

        def plain_norm(key, name, l, src=None, groups=MAIN, dst=H, src_t=X):
            return block_norm(key, groups, lambda k, c: v(name, 8 * l + k), None, Carve(), src=src_t, dst=dst)

        def after_x(eng):
            eng.wait_ge(x_loaded, 16)

        def mod_gate(l, which):
            return lambda n, c: modv[:, l, 16 + 24 * which + n, c:c + 1]

        norms = {"n0": adaln("n0", ALL, 0, 0), "n0f": adaln("n0f", ALL, 0, 1), "n1": adaln("n1", ALL, 1, 0),
                 "n1f": adaln("n1f", MAIN, 1, 1),
                 "mem": plain_norm("mem", "mem_norm", 0, groups=[(0, CTX)], dst=X, src_t=H),
                 "final": plain_norm("final", "final_norm", 0)}
        for l in range(2):
            norms["m", l] = plain_norm(("m", l), "norm_mix_2", l)
            norms["x", l] = plain_norm(("x", l), "norm_cross", l)
            norms["f", l] = plain_norm(("f", l), "norm_ffn_2", l)
            norms["subln", l] = subln_items(l)

        def hide_dve(l):
            nc.vector.memset(TT[0:64, :, 448:512], NEG).then_inc(dve_done, mark("dve", ("ttm", l)))
            nc.vector.wait_ge(dve_done, at(("ttm", l)))

        def subln_gain_dve(l):
            nc.vector.tensor_scalar(LAM[:, 6:7], v("subln", l), 1.0 - lam_init(l), None, ALU.mult).then_inc(
                dve_done, mark("dve", ("sg", l)))
            nc.vector.wait_ge(dve_done, at(("sg", l)))

        def ada1_pe(c):
            ada_pe(1, c)
            if c:
                ada_turn_pe(1, c - 1)
            if c == FT // 2 - 1:
                ada_pe(1, c + 1)
                ada_turn_pe(1, c)
                ada_turn_pe(1, c + 1)

        def ada1_act(c):
            ada_act(1, c)
            if c == FT // 2 - 1:
                ada_act(1, c + 1)

        def ada1_dve(c):
            if c:
                ada_dve(1, c - 1)
            if c == FT // 2 - 1:
                ada_dve(1, c)
                ada_dve(1, c + 1)

        def nothing(c):
            pass

        block = ctx.enter_context(nc.Block())

        @block.sync
        def _(sp):
            for i, (key, parts) in enumerate(plan):
                if i >= SLOTS:
                    sp.wait_ge(pe_done, at(("slot_used", i - SLOTS)))
                width = parts[-1][0] + parts[-1][1].shape[2]
                kt = parts[0][1].shape[1]
                slot = ring[:, i % SLOTS, 0:kt * width].rearrange("p (t n) -> p t n", n=width)
                for c0, src in parts:
                    sp.dma_start(slot[:, :, c0:c0 + src.shape[2]], src).then_inc(slot_loaded[i % SLOTS], 16)
            sp.wait_ge(dve_done, at(("end", "final"), "dve"))
            sp.dma_start(io["outT"], H[:, :, CTX:TOK]).then_inc(out_stored, 16)
            sp.wait_ge(out_stored, 16)

        @block.tensor
        def _(pe):
            start_pe()
            meet("pe", pe, "start")
            norm_pe(norms["n0"])
            meet("pe", pe, "norm0")
            gla_z_pe()
            meet("pe", pe, "gla_z")
            for h in range(GLA_H):
                gla_proj_pe(h)
                meet("pe", pe, ("gla_proj", h))
                gla_scan_pe(h)
                meet("pe", pe, ("gla_scan", h))
            norm_pe(gla_items)
            gla_r_pe()
            meet("pe", pe, "gla_norm")
            residual_pe("gla_o", [(("gla_out", c), 4 * c, 4) for c in range(2)],
                        lambda k, t0, tn: Y[:, k, t0:t0 + tn], ALL)
            meet("pe", pe, "gla_out")
            norm_pe(norms["n0f"])
            meet("pe", pe, "norm0f")
            up_pe("a0", ALL, ada1_pe)
            meet("pe", pe, "up0")
            down_pe("a0", ALL)
            meet("pe", pe, "down0")
            norm_pe(norms["n1"])
            meet("pe", pe, "norm1")
            mla_down_pe()
            meet("pe", pe, "mla_down")
            mla_rest_pe()
            meet("pe", pe, "mla_rest")
            for g in range(2):
                uq_pe(g)
                meet("pe", pe, ("mla_up", g))
                norm_pe(mla_qk[g])
                rope_pe(q_rope[g], "perm_axial")
                meet("pe", pe, ("mla_qk", g))
                mla_att[g]["pe"]()
                meet("pe", pe, ("mla_att", g))
            residual_pe("mla_o", [(("mla_out", c), 4 * c, 4) for c in range(2)],
                        lambda k, t0, tn: H[:, k, t0:t0 + tn], MAIN)
            meet("pe", pe, "mla_out")
            norm_pe(norms["n1f"])
            meet("pe", pe, "norm1f")
            up_pe("a1", MAIN, nothing)
            meet("pe", pe, "up1")
            down_pe("a1", MAIN)
            meet("pe", pe, "down1")
            norm_pe(norms["mem"])
            meet("pe", pe, "memnorm")
            for l in range(2):
                norm_pe(norms["m", l])
                meet("pe", pe, ("norm_m", l))
                idx_pe(l)
                meet("pe", pe, ("idx", l))
                logits_pe(l)
                qkv_pe(l, 0, False)
                meet("pe", pe, ("topk", l))
                flip_pe(l)
                meet("pe", pe, ("toeplitz", l))
                mix_att[l, 0]["pe"]()
                meet("pe", pe, ("attA", l))
                qkv_pe(l, 1, True)
                meet("pe", pe, ("qkv1", l))
                mix_att[l, 1]["pe"]()
                meet("pe", pe, ("att1", l))
                norm_pe(norms["subln", l])
                meet("pe", pe, ("subln", l))
                qkv_pe(l, 2, True)
                meet("pe", pe, ("qkv2", l))
                mix_att[l, 2]["pe"]()
                meet("pe", pe, ("att2", l))
                gate_pe(l)
                meet("pe", pe, ("gate", l))
                residual_pe(("mo", l), [(("mixout", l, c), 4 * c, 4) for c in range(2)],
                            lambda k, t0, tn: Y2[:, k, :], MAIN)
                meet("pe", pe, ("mixout", l))
                norm_pe(norms["x", l])
                meet("pe", pe, ("norm_x", l))
                cross_pe(l)
                meet("pe", pe, ("cross", l))
                cross_att[l]["pe"]()
                meet("pe", pe, ("crossatt", l))
                residual_pe(("xo", l), [(("xo", l), 0, 8)], lambda k, t0, tn: XO[:, k, :], MAIN)
                meet("pe", pe, ("crossout", l))
                norm_pe(norms["f", l])
                meet("pe", pe, ("norm_f", l))
                up_pe(f"b{l}", MAIN, nothing)
                meet("pe", pe, ("upb", l))
                down_pe(f"b{l}", MAIN)
                meet("pe", pe, ("downb", l))
            norm_pe(norms["final"])
            meet("pe", pe, "final")

        @block.scalar
        def _(act):
            start_act()
            ln_exp_tables()
            meet("act", act, "start")
            after_x(act)
            norm_act(norms["n0"])
            meet("act", act, "norm0")
            gla_z_act()
            meet("act", act, "gla_z")
            for h in range(GLA_H):
                gla_proj_act(h)
                meet("act", act, ("gla_proj", h))
                meet("act", act, ("gla_scan", h))
            norm_act(gla_items)
            gla_r_act()
            ln_exp_tables()
            meet("act", act, "gla_norm")
            meet("act", act, "gla_out")
            norm_act(norms["n0f"])
            meet("act", act, "norm0f")
            conv_act("a0", 0, ALL, ada1_act)
            ln_exp_tables()
            meet("act", act, "up0")
            meet("act", act, "down0")
            norm_act(norms["n1"])
            meet("act", act, "norm1")
            mla_down_act()
            meet("act", act, "mla_down")
            mla_rest_act()
            meet("act", act, "mla_rest")
            for g in range(2):
                uq_act(g)
                meet("act", act, ("mla_up", g))
                norm_act(mla_qk[g])
                meet("act", act, ("mla_qk", g))
                mla_att[g]["act"]()
                meet("act", act, ("mla_att", g))
            meet("act", act, "mla_out")
            norm_act(norms["n1f"])
            meet("act", act, "norm1f")
            conv_act("a1", 1, MAIN, nothing)
            ln_exp_tables()
            meet("act", act, "up1")
            meet("act", act, "down1")
            need_load(act, "mem")
            norm_act(norms["mem"])
            meet("act", act, "memnorm")
            for l in range(2):
                norm_act(norms["m", l])
                meet("act", act, ("norm_m", l))
                idx_act(l)
                meet("act", act, ("idx", l))
                qkv_act(l, 0)
                lambda_act(l)
                meet("act", act, ("topk", l))
                flip_act(l)
                meet("act", act, ("toeplitz", l))
                mix_att[l, 0]["act"]()
                meet("act", act, ("attA", l))
                qkv_act(l, 1)
                meet("act", act, ("qkv1", l))
                mix_att[l, 1]["act"]()
                meet("act", act, ("att1", l))
                norm_act(norms["subln", l])
                meet("act", act, ("subln", l))
                qkv_act(l, 2)
                meet("act", act, ("qkv2", l))
                mix_att[l, 2]["act"]()
                meet("act", act, ("att2", l))
                gate_act(l)
                ln_exp_tables()
                meet("act", act, ("gate", l))
                meet("act", act, ("mixout", l))
                norm_act(norms["x", l])
                meet("act", act, ("norm_x", l))
                cross_act(l)
                meet("act", act, ("cross", l))
                cross_att[l]["act"]()
                meet("act", act, ("crossatt", l))
                meet("act", act, ("crossout", l))
                norm_act(norms["f", l])
                meet("act", act, ("norm_f", l))
                swiglu_act(f"b{l}")
                ln_exp_tables()
                meet("act", act, ("upb", l))
                meet("act", act, ("downb", l))
            norm_act(norms["final"])
            meet("act", act, "final")

        @block.vector
        def _(dve):
            start_dve()
            meet("dve", dve, "start")
            after_x(dve)
            norm_dve(norms["n0"])
            meet("dve", dve, "norm0")
            gla_z_dve()
            meet("dve", dve, "gla_z")
            for h in range(GLA_H):
                gla_proj_dve(h)
                meet("dve", dve, ("gla_proj", h))
                gla_scan_dve(h)
                meet("dve", dve, ("gla_scan", h))
            norm_dve(gla_items)
            gla_r_dve()
            meet("dve", dve, "gla_norm")
            gains_dve(0, 1)
            residual_dve("gla_o", ALL, mod_gate(0, 0))
            meet("dve", dve, "gla_out")
            norm_dve(norms["n0f"])
            meet("dve", dve, "norm0f")
            conv_dve("a0", 0, ALL, ada1_dve)
            meet("dve", dve, "up0")
            gains_dve(1, 0)
            gains_dve(1, 1)
            residual_dve(("dn", "a0"), ALL, mod_gate(0, 1))
            meet("dve", dve, "down0")
            norm_dve(norms["n1"])
            meet("dve", dve, "norm1")
            meet("dve", dve, "mla_down")
            mla_rest_dve()
            meet("dve", dve, "mla_rest")
            for g in range(2):
                uq_dve(g)
                meet("dve", dve, ("mla_up", g))
                norm_dve(mla_qk[g])
                rope_dve(q_rope[g], tabs, RT)
                meet("dve", dve, ("mla_qk", g))
                mla_att[g]["dve"]()
                meet("dve", dve, ("mla_att", g))
            residual_dve("mla_o", MAIN, mod_gate(1, 0))
            meet("dve", dve, "mla_out")
            norm_dve(norms["n1f"])
            meet("dve", dve, "norm1f")
            conv_dve("a1", 1, MAIN, nothing)
            meet("dve", dve, "up1")
            residual_dve(("dn", "a1"), MAIN, mod_gate(1, 1))
            meet("dve", dve, "down1")
            need_load(dve, "mem")
            norm_dve(norms["mem"])
            meet("dve", dve, "memnorm")
            for l in range(2):
                norm_dve(norms["m", l])
                meet("dve", dve, ("norm_m", l))
                idx_dve(l)
                meet("dve", dve, ("idx", l))
                topk_dve(l)
                lambda_dve(l)
                meet("dve", dve, ("topk", l))
                meet("dve", dve, ("toeplitz", l))
                hide_dve(l)
                mix_att[l, 0]["dve"]()
                meet("dve", dve, ("attA", l))
                rope_dve(qk_rope(l, 1), btab, BRT)
                meet("dve", dve, ("qkv1", l))
                mix_att[l, 1]["dve"]()
                meet("dve", dve, ("att1", l))
                subln_gain_dve(l)
                norm_dve(norms["subln", l])
                meet("dve", dve, ("subln", l))
                rope_dve(qk_rope(l, 2), btab, BRT)
                meet("dve", dve, ("qkv2", l))
                mix_att[l, 2]["dve"]()
                meet("dve", dve, ("att2", l))
                gate_dve(l)
                meet("dve", dve, ("gate", l))
                residual_dve(("mo", l), MAIN, None)
                meet("dve", dve, ("mixout", l))
                norm_dve(norms["x", l])
                meet("dve", dve, ("norm_x", l))
                meet("dve", dve, ("cross", l))
                cross_att[l]["dve"]()
                meet("dve", dve, ("crossatt", l))
                residual_dve(("xo", l), MAIN, None)
                meet("dve", dve, ("crossout", l))
                norm_dve(norms["f", l])
                meet("dve", dve, ("norm_f", l))
                swiglu_dve(f"b{l}")
                meet("dve", dve, ("upb", l))
                residual_dve(("dn", f"b{l}"), MAIN, None)
                meet("dve", dve, ("downb", l))
            norm_dve(norms["final"])
            meet("dve", dve, "final")

        @block.gpsimd
        def _(pool):
            start_pool()
            meet("pool", pool, "norm1")
            stage_load("axial", [(tabs, io["rope"][:, 0])])
            meet("pool", pool, "mla_out")
            stage_load("mem", [(H[:, :, 0:CTX], io["memT"])])
            for l in range(2):
                meet("pool", pool, ("norm_m", l))
                stage_load(("half", l), [(btab, io["rope"][:, 1]),
                                         (LV, io["lambda_vecs_2"][l].partition_broadcast(P))])
                meet("pool", pool, ("topk", l))
                stage_load(("tt", l), [(TT[:, h, :], bass.AP(tensor=io["relb"].tensor, offset=(l * 8 + h) * 639,
                                                             ap=[[1, P], [1, SEQ]])) for h in range(8)])


WEIGHTS = ["w_ada", "gla_w_in", "gla_gate_w1", "gla_gate_w2", "gla_w_out", "mla_w_down", "mla_w_uq", "mla_w_ukv",
           "mla_w_out", "ffn_w_up", "ffn_w_down", "w_in_2", "w_up_a_2", "w_up_b_2", "w_up_c_2", "w_out_2", "w_q_x_2",
           "w_kv_x_2", "w_o_x_2", "w_gu_2", "w_down_2", "lambda_vecs_2"]


def kernel(**inputs):
    import concourse.bacc as bacc
    from concourse.bass_utils import run_bass_kernel_spmd

    a = {k: np.asarray(x) for k, x in inputs.items()}

    def by_partition(x):
        return x.reshape(-1, P).T

    def twice(x):
        return np.concatenate([x, x])

    vectors = dict(
        c=a["c"], c_ctx=a["c_ctx"], b_ada=a["b_ada"], norm_mix=a["norm_mix"], norm_ffn=a["norm_ffn"],
        gate_b=a["gla_gate_b"], gla_out_norm=a["gla_out_norm"], q_lora_norm=a["mla_q_lora_norm"],
        kv_lora_norm=a["mla_kv_lora_norm"], q_norm_nope=a["mla_q_norm"][:, :NOPE],
        q_norm_rope=twice(a["mla_q_norm"][:, NOPE:]), k_norm_nope=a["mla_k_norm"][:, :NOPE],
        k_norm_rope=twice(a["mla_k_norm"][:, NOPE:]), conv_w=a["ffn_conv_w"], conv_b=a["ffn_conv_b"],
        norm_mix_2=a["norm_mix_2"], subln=a["subln_b_2"], norm_cross=a["norm_cross_2"],
        norm_ffn_2=a["norm_ffn_2"], mem_norm=a["mem_norm_2"], final_norm=a["final_norm_2"])
    arrays = {n: np.ascontiguousarray(a[n]) for n in WEIGHTS}
    arrays["vec"] = np.ascontiguousarray(np.concatenate([by_partition(vectors[n]) for n, _ in VECTORS], 1))
    arrays["mats"], arrays["rope"] = shape_constants()

    def feature_major(x):
        return x.reshape(-1, DT, P).transpose(2, 1, 0)

    arrays["xT"] = np.ascontiguousarray(np.concatenate([feature_major(a["ctx"][0]), feature_major(a["x"][0])], 2))
    arrays["memT"] = np.ascontiguousarray(feature_major(a["mem_2"][0]))
    at = np.clip(SEQ - 1 - np.arange(639), -63, 256) + 63
    arrays["relb"] = np.ascontiguousarray(a["rel_bias_a_2"][:, :, at])

    def make(counts):
        nc = bacc.Bacc("TRN2", target_bir_lowering=False, num_devices=1)
        io = {n: nc.dram_tensor(f"in_{n}", x.shape, F32, kind="ExternalInput").ap() for n, x in arrays.items()}
        io["outT"] = nc.dram_tensor("out_0", (P, DT, SEQ), F32, kind="ExternalOutput").ap()
        build(nc, io, counts)
        return nc

    first = Counts()
    make(first)
    nc = make(Counts(first))
    r = run_bass_kernel_spmd(nc, [{f"in_{n}": x for n, x in arrays.items()}], core_ids=[0])
    out = np.asarray(r.results[0]["out_0"])
    return np.ascontiguousarray(out.transpose(2, 1, 0)).reshape(1, SEQ, D)
```

```python
import math
from contextlib import ExitStack

import numpy as np

import concourse.bass as bass
from concourse import mybir

F32 = mybir.dt.float32
F32R = mybir.dt.float32r
ALU = mybir.AluOpType
ACT = mybir.ActivationFunctionType
AXX = mybir.AxisListType.X

P = 128
D = 1024
DT = D // P
CTX, SEQ = 256, 512
TOK = CTX + SEQ
BANK = 512
EPS = 1e-6
NEG = -1e30
TAKEN = -3e38
ALL = [(0, CTX), (CTX, SEQ)]
MAIN = [(CTX, SEQ)]
FF = 2816
FT = FF // P
GLA_H, GLA_DK, GLA_DV, GLA_C = 4, 128, 256, 64
GATE_NORM = 16.0
MLA_H, NOPE, ROPE = 8, 128, 64
Q_RANK, KV_RANK = 384, 256
HD = 64
TOPK = 128
SLOT = 2048
SLOTS = 4
SPLITS = 2
STAGE = 14500
GROUP = 3

VECTORS = [("c", 8), ("c_ctx", 8), ("b_ada", 96), ("norm_mix", 16), ("norm_ffn", 16), ("gate_b", 8),
           ("gla_out_norm", 2), ("q_lora_norm", 3), ("kv_lora_norm", 2), ("q_norm_nope", 1),
           ("q_norm_rope", 1), ("k_norm_nope", 1), ("k_norm_rope", 1), ("conv_w", 264), ("conv_b", 88),
           ("norm_mix_2", 16), ("subln", 2), ("norm_cross", 16), ("norm_ffn_2", 16), ("mem_norm", 8),
           ("final_norm", 8)]
VAT = {}
_n = 0
for _name, _w in VECTORS:
    VAT[_name] = _n
    _n += _w
NVEC = _n
MATS = ["ident", "mean1024", "mean384", "mean256", "mean128", "mean64", "perm_axial", "perm_half",
        "mask_fwd", "mask_bwd", "flip"]


def shape_constants():
    m = {}
    i = np.arange(P)
    m["ident"] = np.eye(P)
    for d in (1024, 384, 256, 128):
        m[f"mean{d}"] = np.full((P, P), 1.0 / d)
    m["mean64"] = (i[:, None] // 64 == i[None] // 64) / 64.0
    for name, half in (("perm_axial", 16), ("perm_half", 32)):
        first = (i // half) % 2 == 0
        a = np.zeros((P, P))
        a[i[first] + half, i[first]] = -1.0
        a[i[~first] - half, i[~first]] = 1.0
        m[name] = a
    same = i[:, None] // GLA_C == i[None] // GLA_C
    m["mask_fwd"] = same & (i[:, None] <= i[None])
    m["mask_bwd"] = same & (i[:, None] >= i[None])
    m["flip"] = np.eye(P)[::-1]
    mats = np.stack([m[n].astype(np.float32) for n in MATS], 1)
    t = np.arange(SEQ)
    inv = np.float32(10000.0) ** (-np.arange(16, dtype=np.float32) / np.float32(16))
    ang = np.stack([(t // 64).astype(np.float32)[:, None] * inv, (t % 64).astype(np.float32)[:, None] * inv], 1)
    p = np.arange(P) % 64
    axial = ang[:, p // 32, p % 16].T
    inv = np.float32(10000.0) ** (-np.arange(0, 64, 2, dtype=np.float32) / np.float32(64))
    half = (t.astype(np.float32)[:, None] * inv)[:, p % 32].T
    rope = np.stack([np.stack([np.cos(a), np.sin(a)], 1) for a in (axial, half)], 1).astype(np.float32)
    return np.ascontiguousarray(mats), np.ascontiguousarray(rope)


class Counts:

    def __init__(self, known=None):
        self.known = known
        self.n = {}
        self.at = {}
        self.bank = {}
        self.chunk = {}


def build(nc, io, counts):
    known = counts.known
    ctx = ExitStack()
    with ctx:
        def sb(name, shape):
            return ctx.enter_context(nc.sbuf_tensor(name, shape, F32))

        X = sb("X", [P, DT, TOK])
        ring = sb("ring", [P, SLOTS, SLOT])
        vec = sb("vec", [P, NVEC])
        mats = sb("mats", [P, len(MATS), P])
        cond = sb("cond", [P, DT, 2])
        modv = sb("modv", [P, 2, 48, 2])
        gain = sb("gain", [P, 2, 2, 2, DT])
        eps = sb("eps", [P, 1])
        ada_rows = sb("ada_rows", [2, 2, BANK])
        WH = ctx.enter_context(nc.sbuf_tensor("WH", [P, SPLITS, SLOT], F32R))
        WL = ctx.enter_context(nc.sbuf_tensor("WL", [P, SPLITS, SLOT], F32R))
        HALF = DT * TOK
        WHOLE = 2 * HALF + STAGE
        shared = sb("shared", [P, WHOLE])
        base = nc.lookup_mloc(shared).addr

        def overlay(name, shape, dtype, at_word):
            return nc.alloc_sbuf_tensor_at(name, shape, dtype, offset=base + 4 * at_word)

        H = overlay("H", [P, DT, TOK], F32, 0)
        arena_a = overlay("arena_a", [P, WHOLE - HALF], F32, HALF)
        HH = overlay("HH", [P, DT, TOK], F32R, 0)
        HL = overlay("HL", [P, DT, TOK], F32R, HALF)
        stage_b = overlay("stage_b", [P, STAGE], F32, 2 * HALF)
        inter_words = 2 * GROUP * TOK
        IH = overlay("IH", [P, 2, GROUP, TOK], F32R, 2 * HALF)
        IL = overlay("IL", [P, 2, GROUP, TOK], F32R, 2 * HALF + inter_words)
        conv = overlay("conv", [P, 2, 2, TOK], F32, 2 * HALF + 2 * inter_words)
        ps = ctx.enter_context(nc.psum_tensor("ps", [P, 8, BANK], F32))

        def mat(name):
            return mats[:, MATS.index(name), :]

        def v(name, i, n=1):
            return vec[:, VAT[name] + i:VAT[name] + i + n]

        class Carve:
            def __init__(self, at=0, arena=None):
                self.at = at
                self.arena = stage_b if arena is None else arena

            def __call__(self, *shape):
                n = int(np.prod(shape))
                a = self.arena[:, self.at:self.at + n]
                self.at += n
                assert self.at <= self.arena.shape[1], self.at
                if len(shape) == 2:
                    return a.rearrange("p (a b) -> p a b", b=shape[1])
                if len(shape) == 3:
                    return a.rearrange("p (a b c) -> p a b c", b=shape[1], c=shape[2])
                if len(shape) == 4:
                    return a.rearrange("p (a b c d) -> p a b c d", b=shape[1], c=shape[2], d=shape[3])
                return a

        pe_done = ctx.enter_context(nc.semaphore("pe_done"))
        act_done = ctx.enter_context(nc.semaphore("act_done"))
        dve_done = ctx.enter_context(nc.semaphore("dve_done"))
        slot_loaded = [ctx.enter_context(nc.semaphore(f"slot_loaded_{i}")) for i in range(SLOTS)]
        consts_loaded = ctx.enter_context(nc.semaphore("consts_loaded"))
        x_loaded = ctx.enter_context(nc.semaphore("x_loaded"))
        stage_loaded = ctx.enter_context(nc.semaphore("stage_loaded"))
        out_stored = ctx.enter_context(nc.semaphore("out_stored"))

        def mark(e, *keys):
            counts.n[e] = counts.n.get(e, 0) + 1
            for k in keys:
                counts.at.setdefault(k, {})[e] = counts.n[e]
            return 1

        def at(key, e=None):
            if known is None:
                return 1
            if e is None:
                (n,) = known.at[key].values()
                return n
            return known.at[key].get(e, 0)

        def meet(e, eng, name):
            counts.at.setdefault(("end", name), {})[e] = counts.n.get(e, 0)
            eng.wait_ge(pe_done, at(("end", name), "pe"))
            eng.wait_ge(act_done, at(("end", name), "act"))
            eng.wait_ge(dve_done, at(("end", name), "dve"))

        def cols(w, a, b):
            return w.rearrange("(t p) n -> p t n", p=P)[:, :, a:b]

        plan = []

        def piece(key, parts, split=False):
            plan.append((key, parts, split))

        def pieces(key, w, a, b, split=False, width=256):
            for i, c0 in enumerate(range(a, b, width)):
                piece((key, i), [(0, cols(w, c0, min(c0 + width, b)))], split)

        def weights_list():
            def ada(l, c):
                pieces(("ada", l, c), io["w_ada"][l], 512 * c, 512 * c + 512)

            for c in range(4):
                ada(0, c)
            g_in = io["gla_w_in"][0]
            for h in range(GLA_H):
                piece((("gla_in", h), 0), [(0, cols(g_in, h * 128, h * 128 + 128)),
                                           (128, cols(g_in, 512 + h * 128, 640 + h * 128))])
                piece((("gla_in", h), 1), [(0, cols(g_in, 1024 + h * 256, 1280 + h * 256))])
                ada(0, 4 + 2 * h)
                ada(0, 5 + 2 * h)
            pieces("gla_r", g_in, 2048, 3072)
            pieces("gla_out", io["gla_w_out"][0], 0, D)

            def ffn(tag, up, down, extra):
                def ups(g):
                    for j in range(GROUP * g, min(GROUP * g + GROUP, FT)):
                        piece(("up", tag, j), [(0, cols(up, 128 * j, 128 * j + 128)),
                                               (128, cols(up, FF + 128 * j, FF + 128 * j + 128))], True)
                        if j % 2:
                            extra(j // 2)

                def downs(g):
                    rows = down[128 * GROUP * g:128 * min(GROUP * g + GROUP, FT), :]
                    pieces(("down", tag, g), rows, 0, D, True, 512)

                for g in range(-(-FT // GROUP)):
                    ups(g)
                    if g:
                        downs(g - 1)
                downs(FT // GROUP)

            def ada1(c):
                ada(1, c)
                if c == FT // 2 - 1:
                    ada(1, c + 1)

            ffn("a0", io["ffn_w_up"][0], io["ffn_w_down"][0], ada1)
            dn = io["mla_w_down"][0]
            pieces("mla_down", dn, 0, 512, True)
            pe0 = Q_RANK + KV_RANK
            piece(("mla_down", 2), [(0, cols(dn, 512, pe0 + ROPE)), (192, cols(dn, pe0, pe0 + ROPE))], True)
            for g in range(2):
                pieces(("mla_uq", g), io["mla_w_uq"][0], 768 * g, 768 * g + 768, False, 384)
                piece(("mla_ukv", g), [(0, cols(io["mla_w_ukv"][0], 1024 * g, 1024 * g + 1024))])
            pieces("mla_out", io["mla_w_out"][0], 0, D)
            ffn("a1", io["ffn_w_up"][1], io["ffn_w_down"][1], lambda c: None)
            for l in range(2):
                w = io["w_in_2"][l]
                for b in (0, 2, 1):
                    if b == 2:
                        piece(("idx", l, 0), [(0, cols(w, 4608, 4864))], True)
                        piece(("idx", l, 1), [(0, cols(w, 4864, 4928)), (64, cols(w, 4864, 4932))], True)
                    for n in range(3):
                        c0 = 1536 * b + 512 * n
                        pieces(("in", l, b, n), w, c0, c0 + 512, True)
                for c in range(2):
                    for b, u in enumerate(("w_up_a_2", "w_up_b_2", "w_up_c_2")):
                        g0 = 4608 + 324 + 1024 * b + 512 * c
                        pieces(("gate", l, b, c), w, g0, g0 + 512, True)
                        piece(("mixup", l, b, c), [(0, cols(io[u][l], 512 * c, 512 * c + 512))])
                pieces(("mixout", l), io["w_out_2"][l], 0, D)
                pieces(("xkv", l), io["w_kv_x_2"][l], 0, 512)
                piece(("xq", l), [(0, cols(io["w_q_x_2"][l], 0, 256))], True)
                piece(("xo", l), [(0, cols(io["w_o_x_2"][l], 0, 1024))])
                ffn(f"b{l}", io["w_gu_2"][l], io["w_down_2"][l], lambda c: None)

        weights_list()
        where = {}
        loads = [0] * SLOTS
        splits = []
        for i, (key, parts, split) in enumerate(plan):
            loads[i % SLOTS] += 16 * len(parts)
            where[key] = (i, loads[i % SLOTS])
            if split:
                splits.append(key)
        split_at = {key: k for k, key in enumerate(splits)}

        def after(key):
            k = split_at[key] + 1
            if k < len(splits) and where[splits[k]][0] - where[key][0] > SLOTS + 1:
                return len(splits)
            return k

        def piece_shape(key):
            parts = plan[where[key][0]][1]
            return parts[0][1].shape[1], parts[-1][0] + parts[-1][1].shape[2]

        def raw_slot(key):
            kt, width = piece_shape(key)
            return ring[:, where[key][0] % SLOTS, 0:kt * width]

        def weights(key):
            i, n = where[key]
            nc.tensor.wait_ge(slot_loaded[i % SLOTS], n)
            return raw_slot(key).rearrange("p (t n) -> p t n", n=piece_shape(key)[1])

        def split_slot(key, part):
            kt, width = piece_shape(key)
            return part[:, split_at[key] % SPLITS, 0:kt * width]

        def split_act(k):
            if k >= len(splits):
                return
            key = splits[k]
            i, n = where[key]
            if k >= SPLITS:
                nc.scalar.wait_ge(pe_done, at(("split_used", k - SPLITS)))
            nc.scalar.wait_ge(slot_loaded[i % SLOTS], n)
            nc.scalar.copy(split_slot(key, WH), raw_slot(key)).then_inc(act_done, mark("act", ("rounded", k)))

        def split_dve(k):
            if k >= len(splits):
                return
            key = splits[k]
            nc.vector.wait_ge(act_done, at(("rounded", k)))
            nc.vector.tensor_tensor(split_slot(key, WL), raw_slot(key), split_slot(key, WH).bitcast(F32),
                                    ALU.subtract).then_inc(dve_done, mark("dve", ("split", k), used(key)))

        def split_weights(key):
            nc.tensor.wait_ge(dve_done, at(("split", split_at[key])))
            n = piece_shape(key)[1]
            return tuple(split_slot(key, part).rearrange("p (t n) -> p t n", n=n) for part in (WH, WL))

        def split_used(key):
            return ("split_used", split_at[key])

        def used(key):
            return ("slot_used", where[key][0])

        bank_user = [None] * 8
        turn = [0]

        def take(key, bank=None):
            if bank is None:
                bank = turn[0] % 8
                turn[0] += 1
            counts.bank[key] = bank
            if bank_user[bank] is not None:
                if by_act := at(("free", bank_user[bank]), "act"):
                    nc.tensor.wait_ge(act_done, by_act)
                if by_dve := at(("free", bank_user[bank]), "dve"):
                    nc.tensor.wait_ge(dve_done, by_dve)
            bank_user[bank] = key
            return ps[:, bank, :]

        def bank_of(key):
            return ps[:, known.bank[key] if known else 0, :]

        def mms(out, pairs):
            for i, (l, r) in enumerate(pairs):
                m = nc.tensor.matmul(out, l, r, start=(i == 0), stop=(i == len(pairs) - 1))
            return m

        def mms3(out, pairs):
            return mms(out, [p for (lh, ll), (rh, rl) in pairs for p in ((lh, rh), (lh, rl), (ll, rh))])

        def norm_pe(items):
            for key, src, sq, dst, mean, gains, shifts, r in items:
                n = src[0].shape[-1]
                k = src[0].shape[0]
                out = take(("ms", key))[0:k, 0:n]
                for i in range(len(src)):
                    nc.tensor.wait_ge(act_done, at(("sq", key, i)))
                    m = nc.tensor.matmul(out, mean[0:k, 0:k], sq[i], start=(i == 0), stop=(i == len(src) - 1))
                m.then_inc(pe_done, mark("pe", ("ms", key)))

        def norm_act(items):
            users = {}
            for j, (key, src, sq, dst, mean, gains, shifts, r) in enumerate(items):
                for i in range(len(src)):
                    tag = (str(sq[i].tensor.name), sq[i].offset)
                    if tag in users:
                        nc.scalar.wait_ge(pe_done, at(("ms", users[tag])))
                    users[tag] = key
                    nc.scalar.activation(sq[i], src[i], ACT.Square).then_inc(act_done, mark("act", ("sq", key, i)))
                if j:
                    rstd_act(items, j - 1)
            rstd_act(items, len(items) - 1)

        def rstd_act(items, j):
            key, src, sq, dst, mean, gains, shifts, r = items[j]
            k, n = r.shape
            for jj in range(j - 1, -1, -1):
                if items[jj][7].offset == r.offset:
                    nc.scalar.wait_ge(dve_done, at(("scaled", items[jj][0], len(items[jj][1]) - 1)))
                    break
            nc.scalar.wait_ge(pe_done, at(("ms", key)))
            nc.scalar.activation(r, bank_of(("ms", key))[0:k, 0:n], ACT.Ln, bias=eps[0:k, :]).then_inc(act_done, mark("act", ("ln", key), ("free", ("ms", key))))
            nc.scalar.wait_ge(act_done, at(("ln", key)))
            nc.scalar.activation(r, r, ACT.Exp, scale=-0.5).then_inc(act_done, mark("act", ("rstd", key)))
            shift_act(key, dst, shifts)

        def ln_exp_tables():
            nc.scalar.preload_act_table_set("natural_log_exp_and_others")

        def shift_act(key, dst, shifts):
            if shifts is None:
                return
            for i in range(len(dst)):
                nc.scalar.wait_ge(dve_done, at(("scaled", key, i)))
                nc.scalar.activation(dst[i], dst[i], ACT.Identity, bias=shifts[i]).then_inc(act_done, mark("act", ("normed", key)))

        def norm_dve(items):
            for key, src, sq, dst, mean, gains, shifts, r in items:
                nc.vector.wait_ge(act_done, at(("rstd", key)))
                for i in range(len(src)):
                    m = nc.vector.scalar_tensor_tensor(dst[i], src[i], gains[i], r, ALU.mult, ALU.mult)
                    m.then_inc(dve_done, mark("dve", ("scaled", key, i), *([("normed", key)] if shifts is None else [])))

        def block_norm(key, t0, tn, src, sq, dst, gains, shifts, r):
            return ((key, t0), src, sq, dst, mat("mean1024"), gains, shifts, r[:, 0:tn])

        def gla_input_norm():
            r = Carve(0, arena_a)(TOK)
            items = []
            for c, (t0, tn) in ((1, ALL[0]), (0, ALL[1])):
                h = [H[:, k, t0:t0 + tn] for k in range(DT)]
                items.append(block_norm("n0", t0, tn, [X[:, k, t0:t0 + tn] for k in range(DT)], h, h,
                                        [gain[:, 0, 0, c, k:k + 1] for k in range(DT)],
                                        [modv[:, 0, k, c:c + 1] for k in range(DT)], r[:, t0:t0 + tn]))
            return items

        nb = Carve()
        NSQ = nb(3, SEQ)
        NF = nb(3, SEQ)
        NR = nb(TOK)

        def tiles_of(groups):
            return [(i, k, t0, tn) for i, (t0, tn, k) in enumerate((t0, tn, k) for t0, tn in groups for k in range(DT))]

        def hnorm_pe(spec):
            key, groups, gains, shifts = spec
            for i, k, t0, tn in tiles_of(groups):
                if k == 0:
                    out = take(("hms", key, t0))[:, 0:tn]
                nc.tensor.wait_ge(act_done, at(("hsq", key, i)))
                m = nc.tensor.matmul(out, mat("mean1024"), NSQ[:, i % 3, 0:tn], start=(k == 0), stop=(k == DT - 1))
                m.then_inc(pe_done, mark("pe", ("hsq_read", key, i), ("hms", key, t0)))

        def hnorm_act(spec):
            key, groups, gains, shifts = spec
            for i, k, t0, tn in tiles_of(groups):
                if i >= 3:
                    nc.scalar.wait_ge(pe_done, at(("hsq_read", key, i - 3)))
                nc.scalar.activation(NSQ[:, i % 3, 0:tn], X[:, k, t0:t0 + tn], ACT.Square).then_inc(
                    act_done, mark("act", ("hsq", key, i)))
            for i, k, t0, tn in tiles_of(groups):
                r = NR[:, t0:t0 + tn]
                if k == 0:
                    nc.scalar.wait_ge(pe_done, at(("hms", key, t0)))
                    nc.scalar.activation(r, bank_of(("hms", key, t0))[:, 0:tn], ACT.Ln, bias=eps[:, :]).then_inc(
                        act_done, mark("act", ("hln", key, t0), ("free", ("hms", key, t0))))
                    nc.scalar.wait_ge(act_done, at(("hln", key, t0)))
                    nc.scalar.activation(r, r, ACT.Exp, scale=-0.5).then_inc(act_done, mark("act", ("hr", key, t0)))
                nc.scalar.wait_ge(dve_done, at(("hscaled", key, i)))
                bias = shifts(k, 0 if t0 else 1) if shifts else 0.0
                nc.scalar.activation(HH[:, k, t0:t0 + tn], NF[:, i % 3, 0:tn], ACT.Identity, bias=bias).then_inc(
                    act_done, mark("act", ("hh", key, i)))

        def hnorm_dve(spec):
            key, groups, gains, shifts = spec

            def rest(i, k, t0, tn):
                nc.vector.wait_ge(act_done, at(("hh", key, i)))
                f, hh = NF[:, i % 3, 0:tn], HH[:, k, t0:t0 + tn].bitcast(F32)
                if shifts:
                    m = nc.vector.scalar_tensor_tensor(HL[:, k, t0:t0 + tn], f, shifts(k, 0 if t0 else 1), hh,
                                                       ALU.add, ALU.subtract)
                else:
                    m = nc.vector.tensor_tensor(HL[:, k, t0:t0 + tn], f, hh, ALU.subtract)
                m.then_inc(dve_done, mark("dve", ("hl", key, i)))

            tiles = tiles_of(groups)
            for i, k, t0, tn in tiles:
                if k == 0:
                    nc.vector.wait_ge(act_done, at(("hr", key, t0)))
                if i >= 3:
                    nc.vector.wait_ge(dve_done, at(("hl", key, i - 3)))
                nc.vector.scalar_tensor_tensor(NF[:, i % 3, 0:tn], X[:, k, t0:t0 + tn], gains(k, 0 if t0 else 1),
                                               NR[:, t0:t0 + tn], ALU.mult, ALU.mult).then_inc(
                                                   dve_done, mark("dve", ("hscaled", key, i)))
                if i >= 2:
                    rest(*tiles[i - 2])
            rest(*tiles[-2])
            rest(*tiles[-1])

        def adaln(key, groups, l, which):
            return (key, groups, lambda k, c: gain[:, l, which, c, k:k + 1],
                    lambda k, c: modv[:, l, 24 * which + k, c:c + 1])

        def hs(k, t0, tn):
            return HH[:, k, t0:t0 + tn], HL[:, k, t0:t0 + tn]

        def two(w, k, a, b):
            return w[0][:, k, a:b], w[1][:, k, a:b]

        def ada_pe(l, c):
            out = take(("ada", l, c))
            for i in range(2):
                w = weights((("ada", l, c), i))
                m = mms(out[0:2, 256 * i:256 * i + 256], [(cond[:, k, :], w[:, k, :]) for k in range(DT)])
                m.then_inc(pe_done, mark("pe", ("ada", l, c), used((("ada", l, c), i))))

        def ada_turn_pe(l, c):
            nc.tensor.wait_ge(act_done, at(("ada_rows", l, c)))
            out = take(("ada_turned", l, c))
            for j in range(4):
                m = nc.tensor.transpose(out[:, 2 * j:2 * j + 2], ada_rows[0:2, c % 2, 128 * j:128 * j + 128],
                                        mat("ident")[0:2, 0:2])
            m.then_inc(pe_done, mark("pe", ("ada_turned", l, c)))

        def ada_act(l, c):
            nc.scalar.wait_ge(pe_done, at(("ada", l, c)))
            if c >= 2:
                nc.scalar.wait_ge(pe_done, at(("ada_turned", l, c - 2)))
            nc.scalar.copy(ada_rows[0:2, c % 2, :], bank_of(("ada", l, c))[0:2, :]).then_inc(
                act_done, mark("act", ("ada_rows", l, c), ("free", ("ada", l, c))))

        def ada_dve(l, c):
            nc.vector.wait_ge(pe_done, at(("ada_turned", l, c)))
            for s in range(2):
                m = nc.vector.tensor_tensor(
                    modv[:, l, 4 * c:4 * c + 4, s],
                    bank_of(("ada_turned", l, c))[:, 0:8].rearrange("p (j s) -> p j s", s=2)[:, :, s],
                    v("b_ada", 48 * l + 4 * c, 4), ALU.add)
                m.then_inc(dve_done, mark("dve", ("mod", l, c), ("free", ("ada_turned", l, c))))

        def gains_dve(l, which):
            for c in range(2 + 6 * which, 4 + 6 * which):
                nc.vector.wait_ge(dve_done, at(("mod", l, c)))
            for s in range(2):
                nc.vector.scalar_tensor_tensor(
                    gain[:, l, which, s, :], modv[:, l, 8 + 24 * which:16 + 24 * which, s], 1.0,
                    v(("norm_mix", "norm_ffn")[which], 8 * l, 8), ALU.add, ALU.mult).then_inc(dve_done, mark("dve", ("gain", l, which)))

        def residual_pe(key, act_in, groups, chunks=None):
            for ck, n0, nn in chunks or [((key, i), 2 * i, 2) for i in range(DT // 2)]:
                w = weights(ck)
                kt = w.shape[1]
                for j in range(nn):
                    for t0, tn in groups:
                        out = take((key, "out", n0 + j, t0))[:, 0:tn]
                        m = mms(out, [(w[:, k, 128 * j:128 * j + 128], act_in(k, t0, tn)) for k in range(kt)])
                        m.then_inc(pe_done, mark("pe", (key, "out", n0 + j, t0), used(ck)))

        def residual_dve(key, groups, g):
            for n in range(DT):
                for t0, tn in groups:
                    nc.vector.wait_ge(pe_done, at((key, "out", n, t0)))
                    x = X[:, n, t0:t0 + tn]
                    o = bank_of((key, "out", n, t0))[:, 0:tn]
                    if g is None:
                        m = nc.vector.tensor_tensor(x, o, x, ALU.add)
                    else:
                        m = nc.vector.scalar_tensor_tensor(x, o, g(n, 0 if t0 else 1), x, ALU.mult, ALU.add)
                    m.then_inc(dve_done, mark("dve", ("free", (key, "out", n, t0)), ("res", key)))

        def start_pool():
            nc.gpsimd.dma_start(vec[:, :], io["vec"]).then_inc(consts_loaded, 16)
            nc.gpsimd.dma_start(mats[:, :, :], io["mats"]).then_inc(consts_loaded, 16)
            nc.gpsimd.dma_start(X[:, :, :], io["xT"]).then_inc(x_loaded, 16)
            w1 = gla_buf()["w1"]
            w2 = gla_buf()["w2"]
            for d in range(2):
                nc.gpsimd.dma_start(w1[:, d], io["gla_gate_w1"][0, d].rearrange("(t p) r -> p t r", p=P)
                                    ).then_inc(stage_loaded, 16)
                nc.gpsimd.dma_start(w2[0:16, d], io["gla_gate_w2"][0, d]).then_inc(stage_loaded, 16)
            loaded["gla_gates"] = 64

        loaded = {"gla_gates": 64}
        stage_total = [64]

        def stage_load(key, pairs):
            for dst, src in pairs:
                nc.gpsimd.dma_start(dst, src).then_inc(stage_loaded, 16)
                stage_total[0] += 16
            counts.at[("load", key)] = stage_total[0]

        def need_load(eng, key):
            if known:
                eng.wait_ge(stage_loaded, known.at[("load", key)])

        def start_act():
            nc.scalar.wait_ge(consts_loaded, 32)
            for s, name in enumerate(("c", "c_ctx")):
                nc.scalar.activation(cond[:, :, s], v(name, 0, 8), ACT.Silu).then_inc(act_done, mark("act", ("cond",)))
            for c in range(4):
                ada_act(0, c)

        def start_pe():
            nc.tensor.wait_ge(consts_loaded, 32)
            nc.tensor.wait_ge(act_done, at(("cond",)))
            for c in range(4):
                ada_pe(0, c)
                if c:
                    ada_turn_pe(0, c - 1)
            ada_turn_pe(0, 3)

        def start_dve():
            nc.vector.memset(eps[:, :], EPS).then_inc(dve_done, mark("dve", ("eps",)))
            nc.vector.wait_ge(consts_loaded, 32)
            for c in range(4):
                ada_dve(0, c)
            gains_dve(0, 0)

        def gla_buf():
            a = Carve(0, arena_a)
            b = {}
            b["O"] = a(8, TOK)
            b["w1"] = a(2, DT, 16)
            b["w2"] = a(2, 512)
            b["z"] = a(2, TOK)
            b["reset"] = a(TOK)
            b["Q"] = a(TOK)
            b["K"] = a(TOK)
            b["V"] = a(6, 256)
            for d in range(2):
                for n in ("B", "E", "QD", "KI"):
                    b[n, d] = a(TOK)
                b["KT", d] = b["B", d].rearrange("p (t c) -> p t c", c=P)
                b["S", d] = a(2, 256)
                b["A", d] = a(P)
                b["EL", d] = a(12)
            return b

        gb = gla_buf()

        def gla_z_pe():
            nc.tensor.wait_ge(stage_loaded, loaded["gla_gates"])
            for d in range(2):
                for t0, tn in ALL:
                    out = take(("z", d, t0))[0:16, 0:tn]
                    m = mms(out, [(gb["w1"][:, d, k, :], H[:, k, t0:t0 + tn]) for k in range(DT)])
                    m.then_inc(pe_done, mark("pe", ("z", d, t0)))

        def gla_z_act():
            for d in range(2):
                for t0, tn in ALL:
                    nc.scalar.wait_ge(pe_done, at(("z", d, t0)))
                    nc.scalar.copy(gb["z"][0:16, d, t0:t0 + tn], bank_of(("z", d, t0))[0:16, 0:tn]).then_inc(act_done, mark("act", ("zs", d), ("free", ("z", d, t0))))

        def gla_z_dve():
            nc.vector.memset(gb["reset"], 1.0).then_inc(dve_done, mark("dve", ("reset1",)))
            nc.vector.wait_ge(dve_done, at(("reset1",)))
            nc.vector.memset(gb["reset"].rearrange("p (n c) -> p n c", c=GLA_C)[:, :, 0:1], 0.0).then_inc(dve_done, mark("dve", ("reset",)))
            nc.vector.memset(gb["O"], 0.0).then_inc(dve_done, mark("dve", ("Ozero",)))

        def gla_proj_pe(h):
            w = weights((("gla_in", h), 0))
            for n, c0 in (("q", 0), ("k", 128)):
                for t0, tn in ALL:
                    out = take((n, h, t0))[:, 0:tn]
                    m = mms(out, [(w[:, k, c0:c0 + 128], H[:, k, t0:t0 + tn]) for k in range(DT)])
                    m.then_inc(pe_done, mark("pe", (n, h, t0), used((("gla_in", h), 0))))
            for d in range(2):
                nc.tensor.wait_ge(act_done, at(("zs", d)))
                for t0, tn in ALL:
                    out = take(("g", h, d, t0))[:, 0:tn]
                    m = mms(out, [(gb["w2"][0:16, d, 128 * h:128 * h + 128], gb["z"][0:16, d, t0:t0 + tn])])
                    m.then_inc(pe_done, mark("pe", ("g", h, d, t0)))
            w = weights((("gla_in", h), 1))
            for t in range(6):
                out = take(("v", h, t))[:, 0:256]
                m = mms(out, [(H[:, k, 128 * t:128 * t + 128], w[:, k, :]) for k in range(DT)])
                m.then_inc(pe_done, mark("pe", ("v", h, t), used((("gla_in", h), 1))))
            ada_pe(0, 4 + 2 * h)
            ada_pe(0, 5 + 2 * h)
            for d in range(2):
                nc.tensor.wait_ge(dve_done, at(("KS", h, d)))
                for half in range(2):
                    out = take(("kt", h, d, half))
                    for i in range(3):
                        t = 3 * half + i
                        m = nc.tensor.transpose(out[:, 128 * i:128 * i + 128], gb["E", d][:, 128 * t:128 * t + 128], mat("ident"))
                    m.then_inc(pe_done, mark("pe", ("kt", h, d, half)))

            ada_turn_pe(0, 4 + 2 * h)
            ada_turn_pe(0, 5 + 2 * h)

        def gla_proj_act(h):
            for n, buf, sc in (("q", "Q", GLA_DK ** -0.5), ("k", "K", 1.0)):
                for t0, tn in ALL:
                    nc.scalar.wait_ge(pe_done, at((n, h, t0)))
                    nc.scalar.activation(gb[buf][:, t0:t0 + tn], bank_of((n, h, t0))[:, 0:tn], ACT.Identity, scale=sc).then_inc(act_done, mark("act", (buf, h), ("free", (n, h, t0))))
            for d in range(2):
                E = gb["E", d]
                for t0, tn in ALL:
                    nc.scalar.wait_ge(pe_done, at(("g", h, d, t0)))
                    nc.scalar.activation(E[:, t0:t0 + tn], bank_of(("g", h, d, t0))[:, 0:tn], ACT.Abs,
                                                     bias=v("gate_b", 4 * d + h)).then_inc(act_done, mark("act", ("abs", h, d), ("free", ("g", h, d, t0))))
            for d in range(2):
                E = gb["E", d]
                nc.scalar.wait_ge(act_done, at(("abs", h, d)))
                nc.scalar.activation(E, E, ACT.Exp, scale=-1.0).then_inc(act_done, mark("act", ("eabs", h, d)))
                nc.scalar.wait_ge(act_done, at(("eabs", h, d)))
                nc.scalar.activation(E, E, ACT.Ln, bias=1.0).then_inc(act_done, mark("act", ("softplus", h, d)))
            for t in range(6):
                nc.scalar.wait_ge(pe_done, at(("v", h, t)))
                nc.scalar.copy(gb["V"][:, t, :], bank_of(("v", h, t))[:, 0:256]).then_inc(act_done, mark("act", ("V", h), ("free", ("v", h, t))))
            ada_act(0, 4 + 2 * h)
            ada_act(0, 5 + 2 * h)
            for d in range(2):
                E, B = gb["E", d], gb["B", d]
                nc.scalar.wait_ge(dve_done, at(("B", h, d)))
                nc.scalar.activation(E, B, ACT.Exp, scale=1.0 / GATE_NORM).then_inc(act_done, mark("act", ("E1", h, d)))
            for d in range(2):
                E, B = gb["E", d], gb["B", d]
                nc.scalar.wait_ge(dve_done, at(("QD", h, d)))
                nc.scalar.activation(E, B, ACT.Exp, scale=-1.0 / GATE_NORM).then_inc(act_done, mark("act", ("E2", h, d)))
            for d in range(2):
                E = gb["E", d]
                nc.scalar.wait_ge(dve_done, at(("rest", h, d)))
                nc.scalar.activation(E, E, ACT.Exp, scale=1.0 / GATE_NORM).then_inc(act_done, mark("act", ("E3", h, d)))
            for d in range(2):
                for half in range(2):
                    nc.scalar.wait_ge(pe_done, at(("kt", h, d, half)))
                    nc.scalar.copy(gb["KT", d][:, 3 * half:3 * half + 3, :],
                                               bank_of(("kt", h, d, half))[:, 0:384].rearrange("p (t c) -> p t c", c=P)).then_inc(act_done, mark("act", ("KT", h, d), ("free", ("kt", h, d, half))))

        def chunks(a):
            return a.rearrange("p (n c) -> p n c", c=GLA_C)

        def gla_proj_dve(h):
            for d in range(2):
                for t0, tn in ALL:
                    nc.vector.wait_ge(act_done, at(("abs", h, d)))
                    nc.vector.tensor_scalar(gb["KI", d][:, t0:t0 + tn], bank_of(("g", h, d, t0))[:, 0:tn],
                                                        v("gate_b", 4 * d + h), 0.0, ALU.add, ALU.min).then_inc(dve_done, mark("dve", ("minz", h, d), ("free", ("g", h, d, t0))))
            for d in range(2):
                G, E, B = gb["KI", d], gb["E", d], gb["B", d]
                nc.vector.wait_ge(act_done, at(("softplus", h, d)))
                nc.vector.wait_ge(dve_done, at(("minz", h, d)))
                nc.vector.tensor_tensor(G, G, E, ALU.subtract).then_inc(dve_done, mark("dve", ("G", h, d)))
                nc.vector.wait_ge(dve_done, at(("G", h, d)))
                if d == 0:
                    o, g = B, G
                else:
                    o, g = B[:, ::-1], G[:, ::-1]
                nc.vector.tensor_tensor_scan(o, gb["reset"], g, 0.0, ALU.mult, ALU.add).then_inc(dve_done, mark("dve", ("B", h, d)))
            for d in range(2):
                nc.vector.wait_ge(act_done, at(("E1", h, d)))
                nc.vector.wait_ge(act_done, at(("Q", h)))
                E = gb["E", d]
                nc.vector.tensor_tensor(gb["QD", d], gb["Q"], E, ALU.mult).then_inc(dve_done, mark("dve", ("QD0", h, d)))
                last = GLA_C - 1 if d == 0 else 0
                nc.vector.tensor_copy(gb["EL", d], chunks(E)[:, :, last]).then_inc(dve_done, mark("dve", ("QD", h, d)))
            for d in range(2):
                E, B = gb["E", d], gb["B", d]
                last = GLA_C - 1 if d == 0 else 0
                nc.vector.wait_ge(act_done, at(("E2", h, d)))
                nc.vector.wait_ge(act_done, at(("K", h)))
                nc.vector.tensor_tensor(gb["KI", d], gb["K"], E, ALU.mult).then_inc(dve_done, mark("dve", ("KI", h, d)))
                nc.vector.wait_ge(dve_done, at(("KI", h, d)))
                bl = chunks(B)[:, :, last:last + 1].broadcast_to([P, TOK // GLA_C, GLA_C])
                nc.vector.tensor_tensor(chunks(E), bl, chunks(B), ALU.subtract).then_inc(dve_done, mark("dve", ("rest", h, d)))
            for d in range(2):
                nc.vector.wait_ge(act_done, at(("E3", h, d)))
                nc.vector.tensor_tensor(gb["E", d], gb["K"], gb["E", d], ALU.mult).then_inc(dve_done, mark("dve", ("KS", h, d)))
            ada_dve(0, 4 + 2 * h)
            ada_dve(0, 5 + 2 * h)

        TILES = [[0, 1, 2, 3, 4, 5], [1, 0, 5, 4, 3, 2]]

        def gla_scan_pe(h):
            nc.tensor.wait_ge(act_done, at(("V", h)))
            for s in range(6):
                for d in range(2):
                    t = TILES[d][s]
                    tk = slice(128 * t, 128 * t + 128)
                    nc.tensor.wait_ge(act_done, at(("KT", h, d)))
                    nc.tensor.wait_ge(dve_done, at(("QD", h, d)))
                    out = take(("a", h, s, d))[:, 0:128]
                    mms(out, [(gb["KI", d][:, tk], gb["QD", d][:, tk])]).then_inc(pe_done, mark("pe", ("a", h, s, d)))
                o = {}
                for d in range(2):
                    t = TILES[d][s]
                    nc.tensor.wait_ge(dve_done, at(("A", h, s, d)))
                    o[d] = take(("o", h, s, d))
                    for e in range(2):
                        nc.tensor.matmul(o[d][:, 128 * e:128 * e + 128], gb["V"][:, t, 128 * e:128 * e + 128], gb["A", d],
                                         start=(e == 0), stop=False, skip_group_check=True)
                for i in range(2):
                    for d in range(2):
                        t = TILES[d][s]
                        c = i if d == 0 else 1 - i
                        nc.tensor.wait_ge(dve_done, at(("S", h, 2 * s + i, d)))
                        S = gb["S", d][:, (2 * s + i) % 2, :]
                        ck = slice(128 * t + 64 * c, 128 * t + 64 * c + 64)
                        for e in range(2):
                            m = nc.tensor.matmul(o[d][:, 128 * e + 64 * c:128 * e + 64 * c + 64], S[:, 128 * e:128 * e + 128],
                                                 gb["QD", d][:, ck], start=False, stop=(i == 1), skip_group_check=True)
                        m.then_inc(pe_done, mark("pe", ("o", h, s, d)))
                        if 2 * s + i < 11:
                            out = take(("kv", h, 2 * s + i, d))[:, 0:256]
                            m = mms(out, [(gb["KT", d][64 * c:64 * c + 64, t, :], gb["V"][64 * c:64 * c + 64, t, :])])
                            m.then_inc(pe_done, mark("pe", ("kv", h, 2 * s + i, d)))

        def gla_scan_dve(h):
            for d in range(2):
                nc.vector.memset(gb["S", d][:, 0, :], 0.0).then_inc(dve_done, mark("dve", ("S", h, 0, d)))
            for s in range(6):
                for d in range(2):
                    nc.vector.wait_ge(pe_done, at(("a", h, s, d)))
                    if s:
                        nc.vector.wait_ge(pe_done, at(("o", h, s - 1, d)))
                    nc.vector.tensor_tensor(gb["A", d], bank_of(("a", h, s, d))[:, 0:128],
                                                        mat(("mask_fwd", "mask_bwd")[d]), ALU.mult).then_inc(dve_done, mark("dve", ("A", h, s, d), ("free", ("a", h, s, d))))
                for i in range(2):
                    for d in range(2):
                        n = 2 * s + i
                        t = TILES[d][s]
                        c = 2 * t + (i if d == 0 else 1 - i)
                        if n < 11:
                            nc.vector.wait_ge(pe_done, at(("kv", h, n, d)))
                            nc.vector.wait_ge(dve_done, at(("S", h, n, d)))
                            nc.vector.scalar_tensor_tensor(
                                gb["S", d][:, (n + 1) % 2, :], gb["S", d][:, n % 2, :], gb["EL", d][:, c:c + 1],
                                bank_of(("kv", h, n, d))[:, 0:256], ALU.mult, ALU.add).then_inc(dve_done, mark("dve", ("S", h, n + 1, d), ("free", ("kv", h, n, d))))
                for d in range(2):
                    t = TILES[d][s]
                    nc.vector.wait_ge(pe_done, at(("o", h, s, d)))
                    o = gb["O"][:, 2 * h:2 * h + 2, 128 * t:128 * t + 128]
                    if ("Oadd", h, t) in counts.at:
                        nc.vector.wait_ge(dve_done, at(("Oadd1", h, t)))
                    nc.vector.tensor_tensor(
                        o, bank_of(("o", h, s, d))[:, 0:256].rearrange("p (e t) -> p e t", e=2), o, ALU.add).then_inc(dve_done, mark("dve", ("Oadd", h, t), ("free", ("o", h, s, d)), *([] if ("Oadd", h, t) in counts.at else [("Oadd1", h, t)])))

        ga = Carve(8 * TOK, arena_a)
        Y = ga(8, TOK)
        R0 = ga(2, SEQ)
        SR = ga(2, SEQ)
        gla_items = []
        for _h in range(GLA_H):
            for _t0, _tn in ALL:
                _s = [gb["O"][:, 2 * _h + e, _t0:_t0 + _tn] for e in range(2)]
                _d = [Y[:, 2 * _h + e, _t0:_t0 + _tn] for e in range(2)]
                gla_items.append((("glan", _h, _t0), _s, _d, _d, mat("mean256"), [v("gla_out_norm", e) for e in range(2)],
                                  None, R0[:, len(gla_items) % 2, 0:_tn]))

        def gla_r_pe():
            for c in range(4):
                w = weights(("gla_r", c))
                for j in range(2):
                    for t0, tn in ALL:
                        out = take(("r", 2 * c + j, t0))[:, 0:tn]
                        m = mms(out, [(w[:, k, 128 * j:128 * j + 128], H[:, k, t0:t0 + tn]) for k in range(DT)])
                        m.then_inc(pe_done, mark("pe", ("r", 2 * c + j, t0), used(("gla_r", c))))

        def gla_r_act():
            i = 0
            for n in range(8):
                for t0, tn in ALL:
                    nc.scalar.wait_ge(pe_done, at(("r", n, t0)))
                    if i >= 2:
                        nc.scalar.wait_ge(dve_done, at(("y", i - 2)))
                    nc.scalar.activation(SR[:, i % 2, 0:tn], bank_of(("r", n, t0))[:, 0:tn], ACT.Silu).then_inc(act_done, mark("act", ("silu_r", i), ("free", ("r", n, t0))))
                    i += 1

        def gla_r_dve():
            i = 0
            for n in range(8):
                for t0, tn in ALL:
                    nc.vector.wait_ge(act_done, at(("silu_r", i)))
                    nc.vector.wait_ge(dve_done, at(("normed", ("glan", n // 2, t0))))
                    y = Y[:, n, t0:t0 + tn]
                    nc.vector.tensor_tensor(y, y, SR[:, i % 2, 0:tn], ALU.mult).then_inc(dve_done, mark("dve", ("y", i)))
                    i += 1

        GROUPS = -(-FT // GROUP)

        def group(g):
            return range(GROUP * g, min(GROUP * g + GROUP, FT))

        def up_pe(tag, groups, g, extra):
            for j in group(g):
                w = split_weights(("up", tag, j))
                for part in range(2):
                    for t0, tn in groups:
                        out = take(("up", tag, j, part, t0))[:, 0:tn]
                        m = mms3(out, [(two(w, k, 128 * part, 128 * part + 128), hs(k, t0, tn)) for k in range(DT)])
                        m.then_inc(pe_done, mark("pe", ("up", tag, j, part, t0), split_used(("up", tag, j))))
                if j % 2:
                    extra(j // 2)

        def down_pe(tag, groups, g):
            for j in group(g):
                nc.tensor.wait_ge(dve_done, at(("inter", tag, j)))
            for i in range(2):
                w = split_weights((("down", tag, g), i))
                for n in range(4):
                    for t0, tn in groups:
                        out = take(("down", tag, g, 4 * i + n, t0))[:, 0:tn]
                        m = mms3(out, [(two(w, k, 128 * n, 128 * n + 128),
                                        (IH[:, g % 2, k, t0:t0 + tn], IL[:, g % 2, k, t0:t0 + tn]))
                                       for k in range(len(group(g)))])
                        m.then_inc(pe_done, mark("pe", ("down", tag, g, 4 * i + n, t0), ("down", tag, g),
                                                 split_used((("down", tag, g), i))))

        def ffn_pe(tag, groups, extra):
            for g in range(GROUPS + 1):
                if g < GROUPS:
                    up_pe(tag, groups, g, extra)
                if g:
                    down_pe(tag, groups, g - 1)

        def round_inter_act(tag, j, t0):
            g, k = j // GROUP, j % GROUP
            if g >= 2:
                nc.scalar.wait_ge(pe_done, at(("down", tag, g - 2)))
            nc.scalar.wait_ge(dve_done, at(("hidden", tag, j)))
            nc.scalar.copy(IH[:, g % 2, k, t0:TOK], conv[:, j % 2, 0, t0:TOK]).then_inc(
                act_done, mark("act", ("inter_rounded", tag, j)))

        def rest_inter_dve(tag, j, t0):
            g, k = j // GROUP, j % GROUP
            nc.vector.wait_ge(act_done, at(("inter_rounded", tag, j)))
            nc.vector.tensor_tensor(IL[:, g % 2, k, t0:TOK], conv[:, j % 2, 0, t0:TOK],
                                    IH[:, g % 2, k, t0:TOK].bitcast(F32), ALU.subtract).then_inc(
                                        dve_done, mark("dve", ("inter", tag, j)))

        def conv_act(tag, l, groups, g, extra):
            for j in group(g):
                split_act(after(("up", tag, j)))
                if j >= 2:
                    nc.scalar.wait_ge(dve_done, at(("inter", tag, j - 2)))
                for part in range(2):
                    t = 22 * part + j
                    for t0, tn in groups:
                        key = ("up", tag, j, part, t0)
                        nc.scalar.wait_ge(pe_done, at(key))
                        nc.scalar.activation(
                            conv[:, j % 2, part, t0:t0 + tn], bank_of(key)[:, 0:tn], ACT.Identity,
                            scale=v("conv_w", 132 * l + 44 + t), bias=v("conv_b", 44 * l + t)).then_inc(
                                act_done, mark("act", ("mid", tag, j, part, t0), ("free", key)))
                h = conv[:, j % 2, 1, groups[0][0]:TOK]
                nc.scalar.wait_ge(dve_done, at(("conv", tag, j, 1)))
                nc.scalar.activation(h, h, ACT.Silu).then_inc(act_done, mark("act", ("silu", tag, j)))
                round_inter_act(tag, j, groups[0][0])
                if j % 2:
                    extra(j // 2)

        def conv_dve(tag, l, groups, g, extra):
            for j in group(g):
                split_dve(after(("up", tag, j)))
                for part in range(2):
                    t = 22 * part + j
                    for t0, tn in groups:
                        key = ("up", tag, j, part, t0)
                        u = bank_of(key)
                        cv = conv[:, j % 2, part, :]
                        nc.vector.wait_ge(act_done, at(("mid", tag, j, part, t0)))
                        nc.vector.scalar_tensor_tensor(
                            cv[:, t0 + 1:t0 + tn], u[:, 0:tn - 1], v("conv_w", 132 * l + t), cv[:, t0 + 1:t0 + tn],
                            ALU.mult, ALU.add).then_inc(dve_done, mark("dve", ("left", tag, j, part, t0)))
                        nc.vector.wait_ge(dve_done, at(("left", tag, j, part, t0)))
                        nc.vector.scalar_tensor_tensor(
                            cv[:, t0:t0 + tn - 1], u[:, 1:tn], v("conv_w", 132 * l + 88 + t), cv[:, t0:t0 + tn - 1],
                            ALU.mult, ALU.add).then_inc(dve_done, mark("dve", ("conv", tag, j, part), ("free", key)))
                nc.vector.wait_ge(act_done, at(("silu", tag, j)))
                nc.vector.wait_ge(dve_done, at(("conv", tag, j, 0)))
                t0 = groups[0][0]
                a = conv[:, j % 2, 0, t0:TOK]
                nc.vector.tensor_tensor(a, a, conv[:, j % 2, 1, t0:TOK], ALU.mult).then_inc(
                    dve_done, mark("dve", ("hidden", tag, j)))
                rest_inter_dve(tag, j, t0)
                if j % 2:
                    extra(j // 2)

        def swiglu_act(tag, g):
            for j in group(g):
                split_act(after(("up", tag, j)))
                key = ("up", tag, j, 0, CTX)
                nc.scalar.wait_ge(pe_done, at(key))
                if j >= 2:
                    nc.scalar.wait_ge(dve_done, at(("inter", tag, j - 2)))
                nc.scalar.activation(conv[:, j % 2, 1, CTX:TOK], bank_of(key), ACT.Silu).then_inc(
                    act_done, mark("act", ("silu", tag, j), ("free", key)))
                round_inter_act(tag, j, CTX)

        def swiglu_dve(tag, g):
            for j in group(g):
                split_dve(after(("up", tag, j)))
                key = ("up", tag, j, 1, CTX)
                nc.vector.wait_ge(pe_done, at(key))
                nc.vector.wait_ge(act_done, at(("silu", tag, j)))
                nc.vector.tensor_tensor(conv[:, j % 2, 0, CTX:TOK], bank_of(key), conv[:, j % 2, 1, CTX:TOK],
                                        ALU.mult).then_inc(dve_done, mark("dve", ("hidden", tag, j), ("free", key)))
                rest_inter_dve(tag, j, CTX)

        def down_act(tag, g):
            for i in range(2):
                split_act(after((("down", tag, g), i)))

        def down_dve(tag, groups, g, gate):
            for i in range(2):
                split_dve(after((("down", tag, g), i)))
                for n in range(4 * i, 4 * i + 4):
                    for t0, tn in groups:
                        key = ("down", tag, g, n, t0)
                        nc.vector.wait_ge(pe_done, at(key))
                        x, o = X[:, n, t0:t0 + tn], bank_of(key)[:, 0:tn]
                        if g:
                            nc.vector.wait_ge(dve_done, at(("added", tag, g - 1, n, t0)))
                        if gate is None:
                            m = nc.vector.tensor_tensor(x, o, x, ALU.add)
                        else:
                            m = nc.vector.scalar_tensor_tensor(x, o, gate(n, 0 if t0 else 1), x, ALU.mult, ALU.add)
                        m.then_inc(dve_done, mark("dve", ("free", key), ("added", tag, g, n, t0)))

        def conv_ffn_act(tag, l, groups, extra):
            for g in range(GROUPS + 1):
                if g < GROUPS:
                    conv_act(tag, l, groups, g, extra)
                if g:
                    down_act(tag, g - 1)

        def conv_ffn_dve(tag, l, groups, gate, extra):
            for g in range(GROUPS + 1):
                if g < GROUPS:
                    conv_dve(tag, l, groups, g, extra)
                if g:
                    down_dve(tag, groups, g - 1, gate)

        def swiglu_ffn_act(tag):
            for g in range(GROUPS + 1):
                if g < GROUPS:
                    swiglu_act(tag, g)
                if g:
                    down_act(tag, g - 1)

        def swiglu_ffn_dve(tag):
            for g in range(GROUPS + 1):
                if g < GROUPS:
                    swiglu_dve(tag, g)
                if g:
                    down_dve(tag, MAIN, g - 1, None)

        def attention(name, items, scale, P_, PT, small, combine=None, P1=None):
            N = len(items)

            def sm(i, c, what):
                at = ((i % 4) * 2 + c) * 4 + what
                return small[:, at:at + 1]

            def scores_ap(i, c):
                it = items[i]
                b = (i % 2) * 2 + c
                return ps[:, b:b + 2, :].rearrange("p b n -> p (b n)")[:, 0:it["keys"]] if it["keys"] > BANK else ps[:, b, 0:it["keys"]]

            def skeys(i, c):
                it = items[i]
                return [(name, "s", i, c, b) for b in range(-(-it["keys"] // BANK))]

            def scores_pe(i):
                it = items[i]
                for c in range(len(it["prods"])):
                    for b, key in enumerate(skeys(i, c)):
                        k0, k1 = BANK * b, min(BANK * b + BANK, it["keys"])
                        out = take(key, (i % 2) * 2 + c + b)[:, 0:k1 - k0]
                        m = mms(out, [(q, k[:, k0:k1]) for q, k in it["prods"][c]])
                        m.then_inc(pe_done, mark("pe", (name, "scores", i, c)))

            def trans_pe(i):
                it = items[i]
                nc.tensor.wait_ge(dve_done, at((name, "p", i)))
                nb = it["keys"] // P
                for b in range(0, nb, 4):
                    out = take((name, "t", i, b), 4 + b // 4 if it["keys"] > BANK else 4 + i % 2)
                    for k in range(b, min(b + 4, nb)):
                        m = nc.tensor.transpose(out[:, 128 * (k - b):128 * (k - b) + 128],
                                                P_[:, i % 3, 128 * k:128 * k + 128], mat("ident"))
                    m.then_inc(pe_done, mark("pe", (name, "t", i, b)))

            def pv_pe(i):
                it = items[i]
                nb = it["keys"] // P
                po, pn = it["part"]
                nc.tensor.wait_ge(act_done, at((name, "pt", i)))
                out = take((name, "o", i), 6 + i % 2)[po:po + pn, 0:P]
                m = mms(out, [(it["v"](k), PT[:, i % 2, 128 * k:128 * k + 128]) for k in range(nb)])
                m.then_inc(pe_done, mark("pe", (name, "o", i)))

            def pe():
                for s in range(N + 3):
                    if s < N:
                        scores_pe(s)
                    if 0 <= s - 2 < N:
                        trans_pe(s - 2)
                    if 0 <= s - 3 < N:
                        pv_pe(s - 3)

            def smax_dve(i):
                it = items[i]
                for c in range(len(it["prods"])):
                    nc.vector.wait_ge(pe_done, at((name, "scores", i, c)))
                    s = scores_ap(i, c)
                    if it["mask"] == "edge":
                        nc.vector.memset(s[0:64, it["keys"] - 64:it["keys"]], NEG).then_inc(dve_done, mark("dve", (name, "edge", i, c)))
                        nc.vector.wait_ge(dve_done, at((name, "edge", i, c)))
                    elif it["mask"] is not None:
                        if i >= 3:
                            nc.vector.wait_ge(pe_done, at((name, "t", i - 3, 0)))
                        sc, bias = it["mask"]
                        S = P_[:, i % 3, 0:it["keys"]]
                        nc.vector.scalar_tensor_tensor(S, s, sc, bias, ALU.mult, ALU.add).then_inc(dve_done, mark("dve", (name, "biased", i), *[("free", k) for k in skeys(i, c)]))
                        nc.vector.wait_ge(dve_done, at((name, "biased", i)))
                        s = S
                    nc.vector.tensor_reduce(sm(i, c, 0), s, AXX, ALU.max).then_inc(dve_done, mark("dve", (name, "max", i, c)))
                    nc.vector.wait_ge(dve_done, at((name, "max", i, c)))
                    nc.vector.tensor_scalar(sm(i, c, 1), sm(i, c, 0), -scale, None, ALU.mult).then_inc(dve_done, mark("dve", (name, "nmax", i, c)))

            def norm_dve_(i):
                it = items[i]
                p = P_[:, i % 3, 0:it["keys"]]
                for c in range(len(it["prods"])):
                    nc.vector.wait_ge(act_done, at((name, "e", i, c)))
                    nc.vector.reciprocal(sm(i, c, 3), sm(i, c, 2)).then_inc(dve_done, mark("dve", (name, "r", i, c)))
                if len(it["prods"]) == 2:
                    p1 = P1[:, i % 2, 0:it["keys"]]
                    nc.vector.wait_ge(dve_done, at((name, "r", i, 1)))
                    nc.vector.tensor_scalar(p1, p1, sm(i, 1, 3), combine, ALU.mult, ALU.mult).then_inc(dve_done, mark("dve", (name, "p1", i)))
                    nc.vector.wait_ge(dve_done, at((name, "p1", i)))
                    nc.vector.scalar_tensor_tensor(p, p, sm(i, 0, 3), p1, ALU.mult, ALU.add).then_inc(dve_done, mark("dve", (name, "p", i)))
                else:
                    nc.vector.wait_ge(dve_done, at((name, "r", i, 0)))
                    nc.vector.tensor_scalar(p, p, sm(i, 0, 3), None, ALU.mult).then_inc(dve_done, mark("dve", (name, "p", i)))

            def dve():
                for s in range(N + 1):
                    if s < N:
                        smax_dve(s)
                    if s:
                        norm_dve_(s - 1)

            def exp_act(i):
                it = items[i]
                if i >= 2 and len(it["prods"]) == 2:
                    nc.scalar.wait_ge(dve_done, at((name, "p", i - 2)))
                if i >= 3:
                    for b in range(0, it["keys"] // P, 4):
                        if (name, "t", i - 3, b) in (known.at if known else {}):
                            nc.scalar.wait_ge(pe_done, at((name, "t", i - 3, b)))
                    nc.scalar.wait_ge(pe_done, at((name, "t", i - 3, 0)))
                for c in range(len(it["prods"])):
                    nc.scalar.wait_ge(dve_done, at((name, "nmax", i, c)))
                    biased = it["mask"] is not None and it["mask"] != "edge"
                    s = P_[:, i % 3, 0:it["keys"]] if biased else scores_ap(i, c)
                    p = P1[:, i % 2, 0:it["keys"]] if c else P_[:, i % 3, 0:it["keys"]]
                    nc.scalar.activation(p, s, ACT.Exp, scale=scale,
                                                     bias=sm(i, c, 1), accum_out=sm(i, c, 2)).then_inc(act_done, mark("act", (name, "e", i, c), (name, "e", i), *([] if biased else [("free", k) for k in skeys(i, c)])))

            def pt_act(i):
                it = items[i]
                nb = it["keys"] // P
                if i >= 2:
                    nc.scalar.wait_ge(pe_done, at((name, "o", i - 2)))
                for b in range(0, nb, 4):
                    nc.scalar.wait_ge(pe_done, at((name, "t", i, b)))
                    n = 128 * (min(b + 4, nb) - b)
                    nc.scalar.copy(PT[:, i % 2, 128 * b:128 * b + n],
                                               ps[:, 4 + b // 4 if it["keys"] > BANK else 4 + i % 2, 0:n]).then_inc(act_done, mark("act", (name, "pt", i), ("free", (name, "t", i, b))))

            def o_act(i):
                po, pn = items[i]["part"]
                nc.scalar.wait_ge(pe_done, at((name, "o", i)))
                nc.scalar.copy(items[i]["out"], ps[po:po + pn, 6 + i % 2, 0:P]).then_inc(act_done, mark("act", ("free", (name, "o", i)), (name, "O")))

            def act():
                for s in range(N + 3):
                    if s < N:
                        exp_act(s)
                    if 0 <= s - 2 < N:
                        pt_act(s - 2)
                    if 0 <= s - 3 < N:
                        o_act(s - 3)

            return {"pe": pe, "act": act, "dve": dve}

        def rope_pe(items, perm):
            for key, a, k, ready in items:
                if by_act := at(ready, "act"):
                    nc.tensor.wait_ge(act_done, by_act)
                if by_dve := at(ready, "dve"):
                    nc.tensor.wait_ge(dve_done, by_dve)
                out = take(("rot", key))[0:k, :]
                mms(out, [(mat(perm)[0:k, 0:k], a)]).then_inc(pe_done, mark("pe", ("rot", key)))

        def rope_dve(items, tab, tmp):
            for i, (key, a, k, ready) in enumerate(items):
                nc.vector.wait_ge(pe_done, at(("rot", key)))
                u = tmp[0:k, i % 2, :]
                if i >= 2:
                    nc.vector.wait_ge(dve_done, at(("roped", items[i - 2][0])))
                nc.vector.tensor_tensor(u, bank_of(("rot", key))[0:k, :], tab[0:k, 1, :], ALU.mult).then_inc(dve_done, mark("dve", ("ru", key), ("free", ("rot", key))))
                nc.vector.tensor_tensor(a, a, tab[0:k, 0, :], ALU.mult).then_inc(dve_done, mark("dve", ("rc", key)))
                nc.vector.wait_ge(dve_done, at(("rc", key)))
                nc.vector.tensor_tensor(a, a, u, ALU.add).then_inc(dve_done, mark("dve", ("roped", key)))

        arena_c = overlay("arena_c", [P, WHOLE], F32, 0)
        ma = Carve(0, arena_c)
        MO = ma(8, SEQ)
        Q4 = ma(4, SEQ)
        QP = ma(2, SEQ)
        K4 = ma(4, TOK)
        MR = ma(2, SEQ)
        MS = ma(32)
        assert ma.at <= 2 * HALF
        ma = Carve(2 * HALF, arena_c)
        tabs = ma(2, SEQ)
        CQ = ma(3, SEQ)
        CKV = ma(2, TOK)
        KPE = ma(TOK)
        SQ = ma(3, SEQ)
        RT = SQ[:, 0:2, :]
        V4 = ma(6, SEQ)
        MP = ma(3, TOK)
        MPT = ma(2, TOK)

        def down_items():
            its = [(("cq",), [CQ[:, k, :] for k in range(3)], [SQ[:, k, :] for k in range(3)], [CQ[:, k, :] for k in range(3)],
                    mat("mean384"), [v("q_lora_norm", k) for k in range(3)], None, MR[:, 0, :])]
            for i, (t0, tn) in enumerate(ALL):
                t = [CKV[:, k, t0:t0 + tn] for k in range(2)]
                its.append((("ckv", t0), t, [SQ[:, k, 0:tn] for k in range(2)], t, mat("mean256"),
                            [v("kv_lora_norm", k) for k in range(2)], None, MR[:, 0, 0:tn]))
            for i, (t0, tn) in enumerate(ALL):
                t = [KPE[:, t0:t0 + tn]]
                its.append((("kpe", t0), t, [SQ[:, 0, 0:tn]], t, mat("mean64"), [v("k_norm_rope", 0)], None,
                            MR[:, 0, 0:tn]))
            return its

        mla_down_items = down_items()

        down_tiles = ([(("dq", n), CQ[:, n, :], MAIN) for n in range(3)]
                      + [(("dkv", n), CKV[:, n, :], ALL) for n in range(2)] + [(("dkv", 2), KPE, ALL)])

        def mla_down_pe():
            for n, (name, dst, groups) in enumerate(down_tiles):
                w = split_weights(("mla_down", n // 2))
                for t0, tn in groups:
                    out = take((name, t0))[:, 0:tn]
                    m = mms3(out, [(two(w, k, n % 2 * 128, n % 2 * 128 + 128), hs(k, t0, tn)) for k in range(DT)])
                    m.then_inc(pe_done, mark("pe", (name, t0), split_used(("mla_down", n // 2))))

        def mla_down_act():
            for n, (name, dst, groups) in enumerate(down_tiles):
                if n % 2 == 0:
                    split_act(after(("mla_down", n // 2)))
                off = TOK - dst.shape[-1]
                for t0, tn in groups:
                    nc.scalar.wait_ge(pe_done, at((name, t0)))
                    nc.scalar.copy(dst[:, t0 - off:t0 - off + tn], bank_of((name, t0))[:, 0:tn]).then_inc(
                        act_done, mark("act", ("free", (name, t0)), ("CKV",)))

        def mla_down_dve():
            for n in range(3):
                split_dve(after(("mla_down", n)))

        kpe_rope = [("kpe", KPE[:, CTX:TOK], P, ("normed", ("kpe", CTX)))]

        def mla_rest_pe():
            norm_pe(mla_down_items)
            rope_pe(kpe_rope, "perm_axial")

        def mla_rest_act():
            nc.scalar.wait_ge(act_done, at(("CKV",)))
            norm_act(mla_down_items)

        def mla_rest_dve():
            norm_dve(mla_down_items)
            need_load(nc.vector, "axial")
            rope_dve(kpe_rope, tabs, RT)

        def uq_pe(g):
            for i in range(2):
                w = weights((("mla_uq", g), i)).rearrange("p t (h c) -> p t h c", c=192)
                for h in range(2):
                    out = take(("uq", g, 2 * i + h))
                    m = mms(out, [(w[:, k, h, 0:128], CQ[:, k, :]) for k in range(3)])
                    m.then_inc(pe_done, mark("pe", ("uq", g, 2 * i + h)))
                for half in range(2):
                    out = take(("uqr", g, i, half))[0:64, :]
                    m = mms(out, [(w[:, k, half, 128:192], CQ[:, k, :]) for k in range(3)])
                    m.then_inc(pe_done, mark("pe", ("uqr", g, i, half), used((("mla_uq", g), i))))
            w = weights(("mla_ukv", g)).rearrange("p t (h c) -> p t h c", c=256)
            for h in range(4):
                for t0, tn in ALL:
                    out = take(("uk", g, h, t0))[:, 0:tn]
                    m = mms(out, [(w[:, k, h, 0:128], CKV[:, k, t0:t0 + tn]) for k in range(2)])
                    m.then_inc(pe_done, mark("pe", ("uk", g, h, t0)))
            for t in range(6):
                out = take(("uv", g, t)).rearrange("p (h c) -> p h c", c=128)
                m = mms(out, [(CKV[:, k, 128 * t:128 * t + 128], w[:, k, :, 128:256]) for k in range(2)])
                m.then_inc(pe_done, mark("pe", ("uv", g, t), used(("mla_ukv", g))))

        def uq_act(g):
            for i in range(2):
                for h in (2 * i, 2 * i + 1):
                    nc.scalar.wait_ge(pe_done, at(("uq", g, h)))
                    nc.scalar.copy(Q4[:, h, :], bank_of(("uq", g, h))).then_inc(act_done, mark("act", ("free", ("uq", g, h)), ("Q4", g)))
                for half in range(2):
                    nc.scalar.wait_ge(pe_done, at(("uqr", g, i, half)))
                    nc.scalar.copy(QP[64 * half:64 * half + 64, i, :], bank_of(("uqr", g, i, half))[0:64, :]).then_inc(act_done, mark("act", ("free", ("uqr", g, i, half)), ("Q4", g)))
            for h in range(4):
                for t0, tn in ALL:
                    nc.scalar.wait_ge(pe_done, at(("uk", g, h, t0)))
                    nc.scalar.copy(K4[:, h, t0:t0 + tn], bank_of(("uk", g, h, t0))[:, 0:tn]).then_inc(act_done, mark("act", ("free", ("uk", g, h, t0)), ("Q4", g)))

        def uq_dve(g):
            for t in range(6):
                nc.vector.wait_ge(pe_done, at(("uv", g, t)))
                nc.vector.tensor_copy(V4[:, t, :], bank_of(("uv", g, t))).then_inc(dve_done, mark("dve", ("free", ("uv", g, t)), ("V4", g)))

        def qk_items(g):
            its = []

            def add(key, t, mean, gn, n):
                i = len(its) % 2
                its.append((key, [t], [SQ[:, i, 0:n]], [t], mat(mean), [gn], None, MR[:, i, 0:n]))

            for i in range(2):
                add(("qp", g, i), QP[:, i, :], "mean64", v("q_norm_rope", 0), SEQ)
            for h in range(4):
                add(("qn", g, h), Q4[:, h, :], "mean128", v("q_norm_nope", 0), SEQ)
                for t0, tn in ALL:
                    add(("kn", g, h, t0), K4[:, h, t0:t0 + tn], "mean128", v("k_norm_nope", 0), tn)
            return its

        def mla_attention(g):
            its = []
            for h in range(4):
                e = 64 * (h % 2)
                for qt in range(4):
                    qs = slice(128 * qt, 128 * qt + 128)
                    its.append(dict(keys=TOK, mask=None, part=(0, P),
                                    prods=[[(Q4[:, h, qs], K4[:, h, :]),
                                            (QP[e:e + 64, h // 2, qs], KPE[e:e + 64, :])]],
                                    v=lambda k, h=h: V4[:, k, 128 * h:128 * h + 128],
                                    out=MO[:, 4 * g + h, qs]))
            return attention(("mla", g), its, 192 ** -0.5, MP, MPT, MS)

        mla_att = [mla_attention(g) for g in range(2)]
        mla_qk = [qk_items(g) for g in range(2)]
        q_rope = [[(("qp", g, i), QP[:, i, :], P, ("normed", ("qp", g, i))) for i in range(2)] for g in range(2)]

        ba = Carve()
        OO = {b: ba(4, SEQ) for b in (0, 2, 1)}
        KB = ba(4, SEQ)
        VB = ba(4, SEQ)
        BP = ba(3, SEQ)
        BPT = ba(2, SEQ)
        btab = ba(2, SEQ)
        BSM = ba(32)
        WI = ba(4, 4)
        LV = ba(4, HD)
        LAM = ba(8)
        MX8 = ba(8)
        BP1 = btab
        TT = Carve(2048)(8, SEQ)
        bm = Carve(4096)
        MQ = [bm(128 * qt + 128) for qt in range(4)]
        IT = bm(SEQ)
        bw = Carve(10240)
        WK = bw(2, SEQ)
        QI = bw(2, SEQ)
        KIX = bw(SEQ)
        BRT = WK
        gc = Carve(6144)
        Y2 = gc(8, SEQ)
        GSB = gc(4, SEQ)
        YTB = gc(2, SEQ)
        xa = Carve()
        XQ = xa(2, SEQ)
        XK = xa(2, CTX)
        XV = xa(2, CTX)
        XO = xa(2, SEQ)
        XP = xa(3, CTX)
        XPT = xa(2, CTX)
        XS = xa(32)

        def idx_pe(l):
            for n in range(3):
                w = split_weights(("idx", l, n // 2))
                out = take(("ip", l, n))
                m = mms3(out, [(two(w, k, 128 * (n % 2), 128 * (n % 2) + 128), hs(k, CTX, SEQ)) for k in range(DT)])
                m.then_inc(pe_done, mark("pe", ("ip", l, n), split_used(("idx", l, n // 2))))
            out = take(("wi", l))
            for t in range(4):
                m = mms3(out[:, 4 * t:4 * t + 4], [(hs(k, CTX + 128 * t, 128), two(w, k, 128, 132)) for k in range(DT)])
            m.then_inc(pe_done, mark("pe", ("wi", l), split_used(("idx", l, 1))))
            rope_pe(idx_rope[l], "perm_half")

        idx_rope = [[(("ix", l, n), QI[:, n, :] if n < 2 else KIX, P, ("ips", l, n)) for n in range(3)]
                    for l in range(2)]

        def idx_act(l):
            for n in range(3):
                if n != 1:
                    split_act(after(("idx", l, n // 2)))
                dst = QI[:, n, :] if n < 2 else KIX
                nc.scalar.wait_ge(pe_done, at(("ip", l, n)))
                nc.scalar.copy(dst, bank_of(("ip", l, n))).then_inc(act_done, mark("act", ("free", ("ip", l, n)), ("ips", l, n)))

        def idx_dve(l):
            split_dve(after(("idx", l, 0)))
            split_dve(after(("idx", l, 1)))
            nc.vector.wait_ge(pe_done, at(("wi", l)))
            nc.vector.tensor_scalar(WI, bank_of(("wi", l))[:, 0:16].rearrange("p (t h) -> p t h", h=4),
                                                0.5 * HD ** -0.5, None, ALU.mult).then_inc(dve_done, mark("dve", ("free", ("wi", l)), ("WI", l)))
            need_load(nc.vector, ("block2", l))
            rope_dve(idx_rope[l], btab, BRT)

        def logits_pe(l, tiles):
            for qt in tiles:
                n = 128 * qt + 128
                for h in range(4):
                    e = 64 * (h % 2)
                    out = take(("lg", l, qt, h))[:, 0:n]
                    m = mms(out, [(QI[e:e + 64, h // 2, 128 * qt:128 * qt + 128], KIX[e:e + 64, 0:n])])
                    m.then_inc(pe_done, mark("pe", ("lg", l, qt, h)))

        def topk_dve(l):
            nc.vector.memset(MQ[0], 0.0).then_inc(dve_done, mark("dve", ("m0", l)))
            nc.vector.wait_ge(dve_done, at(("m0", l)))
            nc.vector.memset(MQ[0][0:64, 64:128], NEG).then_inc(dve_done, mark("dve", ("mask", l)))
            for qt in range(1, 4):
                n = 128 * qt + 128
                cur, tmp, acc = WK[:, 0, 0:n], IT[:, 0:n], WK[:, 1, 0:n]
                for h in range(4):
                    nc.vector.wait_ge(pe_done, at(("lg", l, qt, h)))
                    dst = acc if h == 0 else tmp
                    if h >= 2:
                        nc.vector.wait_ge(dve_done, at(("acc", l, qt, h - 1)))
                    elif h == 0 and qt > 1:
                        nc.vector.wait_ge(dve_done, at(("m1", l, qt - 1)))
                    nc.vector.tensor_scalar(dst, bank_of(("lg", l, qt, h))[:, 0:n], 0.0, WI[:, qt, h:h + 1],
                                                        ALU.max, ALU.mult).then_inc(dve_done, mark("dve", ("free", ("lg", l, qt, h)), ("lr", l, qt, h)))
                    if h:
                        nc.vector.wait_ge(dve_done, at(("lr", l, qt, h)))
                        nc.vector.tensor_tensor(acc, acc, tmp, ALU.add).then_inc(dve_done, mark("dve", ("acc", l, qt, h)))
                nc.vector.wait_ge(dve_done, at(("acc", l, qt, 3)))
                nc.vector.memset(acc[0:64, n - 64:n], NEG).then_inc(dve_done, mark("dve", ("sc", l, qt, 0)))
                a, b = acc, cur
                for r in range(TOPK // 8):
                    if r % 8 == 2:
                        split_dve(after(in_pieces(l, 2)[2 * (qt - 1) + r // 8]))
                    nc.vector.wait_ge(dve_done, at(("sc", l, qt, r)))
                    nc.vector.max(MX8, a).then_inc(dve_done, mark("dve", ("mx", l, qt, r)))
                    nc.vector.wait_ge(dve_done, at(("mx", l, qt, r)))
                    nc.vector.match_replace(b, MX8, a, TAKEN).then_inc(dve_done, mark("dve", ("sc", l, qt, r + 1)))
                    a, b = b, a
                nc.vector.wait_ge(dve_done, at(("sc", l, qt, TOPK // 8)))
                nc.vector.tensor_scalar(MQ[qt], a, 0.1 * TAKEN, NEG, ALU.is_gt, ALU.mult).then_inc(dve_done, mark("dve", ("m1", l, qt)))
                nc.vector.wait_ge(dve_done, at(("m1", l, qt)))
                nc.vector.memset(MQ[qt][0:64, n - 64:n], NEG).then_inc(dve_done, mark("dve", ("mask", l)))

        def in_pieces(l, b):
            return [(("in", l, b, n), i) for n in range(3) for i in range(2)]

        def qk_pe(l, b, n):
            for i in range(2):
                w = split_weights((("in", l, b, n), i))
                for j in range(2):
                    key = ("qk", l, b, n, 2 * i + j)
                    m = mms3(take(key), [(two(w, k, 128 * j, 128 * j + 128), hs(k, CTX, SEQ)) for k in range(DT)])
                    m.then_inc(pe_done, mark("pe", key, split_used((("in", l, b, n), i))))

        def v_pe(l, b):
            for i in range(2):
                w = split_weights((("in", l, b, 2), i))
                for t in range(4):
                    out = take(("vv", l, b, i, t))[:, 0:256]
                    m = mms3(out, [(hs(k, CTX + 128 * t, 128), two(w, k, 0, 256)) for k in range(DT)])
                    m.then_inc(pe_done, mark("pe", ("vv", l, b, i, t), split_used((("in", l, b, 2), i))))

        def qk_rope(l, b):
            return [(("qk", l, b, n, j), (OO[b], KB)[n][:, j, :], P, ("qks", l, b, n, j)) for n in range(2) for j in range(4)]

        def qkv_act(l, b):
            for n in range(2):
                for j in range(4):
                    if j % 2 == 0:
                        split_act(after((("in", l, b, n), j // 2)))
                    nc.scalar.wait_ge(pe_done, at(("qk", l, b, n, j)))
                    nc.scalar.copy((OO[b], KB)[n][:, j, :], bank_of(("qk", l, b, n, j))).then_inc(act_done, mark("act", ("free", ("qk", l, b, n, j)), ("qks", l, b, n, j)))
            for i in range(2):
                split_act(after((("in", l, b, 2), i)))
                for t in range(4):
                    nc.scalar.wait_ge(pe_done, at(("vv", l, b, i, t)))
                    nc.scalar.copy(VB[:, t, 256 * i:256 * i + 256], bank_of(("vv", l, b, i, t))[:, 0:256]).then_inc(
                        act_done, mark("act", ("free", ("vv", l, b, i, t))))

        def qkv_dve(l, b):
            for key in in_pieces(l, b):
                split_dve(after(key))

        def flip_pe(l):
            need_load(nc.tensor, ("block2", l))
            for h in range(8):
                out = take(("fl", l, h))
                mms(out, [(mat("flip"), TT[:, h, :])]).then_inc(pe_done, mark("pe", ("fl", l, h)))

        def flip_act(l):
            for h in range(8):
                nc.scalar.wait_ge(pe_done, at(("fl", l, h)))
                nc.scalar.copy(TT[:, h, :], bank_of(("fl", l, h))).then_inc(act_done, mark("act", ("free", ("fl", l, h)), ("TT", l)))

        def mix_attention(l, b):
            its = []
            nh = 4 if b == 1 else 8
            for h in range(nh):
                for qt in range(4):
                    n = 128 * qt + 128
                    qs = slice(128 * qt, 128 * qt + 128)
                    if b == 1:
                        prods = [[(OO[1][e:e + 64, h, qs], KB[e:e + 64, h, :])] for e in (0, 64)]
                        part, vv = (0, P), (lambda k, h=h: VB[:, k, 128 * h:128 * h + 128])
                        out = OO[1][:, h, qs]
                        mask = "edge"
                    else:
                        e = 64 * (h % 2)
                        prods = [[(OO[b][e:e + 64, h // 2, qs], KB[e:e + 64, h // 2, :])]]
                        part, vv = (e, 64), (lambda k, h=h: VB[:, k, 64 * h:64 * h + 64])
                        out = OO[b][e:e + 64, h // 2, qs]
                        mask = (HD ** -0.5, TT[:, h, 384 - 128 * qt:512]) if b == 0 else (1.0, MQ[qt])
                    its.append(dict(keys=n, mask=mask, part=part, prods=prods, v=vv, out=out))
            return attention(("mix", l, b), its, 1.0 if b == 0 else HD ** -0.5, BP, BPT, BSM,
                             combine=LAM[:, 4:5] if b == 1 else None, P1=BP1)

        mix_att = {(l, b): mix_attention(l, b) for l in range(2) for b in range(3)}

        def lam_init(l):
            return 0.8 - 0.6 * math.exp(-0.3 * l)

        def lambda_dve(l):
            need_load(nc.vector, ("block2", l))
            for i in range(2):
                nc.vector.tensor_tensor(LV[:, 2 * i, :], LV[:, 2 * i, :], LV[:, 2 * i + 1, :], ALU.mult).then_inc(dve_done, mark("dve", ("lm", l, i)))
                nc.vector.wait_ge(dve_done, at(("lm", l, i)))
                nc.vector.tensor_reduce(LAM[:, i:i + 1], LV[:, 2 * i, :], AXX, ALU.add).then_inc(dve_done, mark("dve", ("ls", l)))
            nc.vector.wait_ge(act_done, at(("le", l)))
            nc.vector.tensor_tensor(LAM[:, 5:6], LAM[:, 3:4], LAM[:, 2:3], ALU.subtract).then_inc(dve_done, mark("dve", ("ld", l)))
            nc.vector.wait_ge(dve_done, at(("ld", l)))
            nc.vector.tensor_scalar(LAM[:, 4:5], LAM[:, 5:6], -lam_init(l), None, ALU.add).then_inc(dve_done, mark("dve", ("lam", l)))

        def lambda_act(l):
            nc.scalar.wait_ge(dve_done, at(("ls", l)))
            nc.scalar.activation(LAM[:, 2:4], LAM[:, 0:2], ACT.Exp).then_inc(act_done, mark("act", ("le", l)))

        def subln_items(l):
            its = []
            for h in range(4):
                o = OO[1][:, h, :]
                its.append((("subln", l, h), [o], [BP[:, h % 2, :]], [o], mat("mean128"), [LAM[:, 6:7]], None,
                            BPT[:, h % 2, :]))
            return its

        def gate_pe(l):
            for c in range(2):
                for b in range(3):
                    for j in range(4):
                        key = (("gate", l, b, c), j // 2)
                        w = split_weights(key)
                        out = take(("gt", l, b, c, j))
                        m = mms3(out, [(two(w, k, j % 2 * 128, j % 2 * 128 + 128), hs(k, CTX, SEQ)) for k in range(DT)])
                        m.then_inc(pe_done, mark("pe", ("gt", l, b, c, j), split_used(key)))
                    w = weights(("mixup", l, b, c))
                    for j in range(4):
                        out = take(("mu", l, b, c, j))
                        m = mms(out, [(w[:, k, 128 * j:128 * j + 128], OO[b][:, k, :]) for k in range(4)])
                        m.then_inc(pe_done, mark("pe", ("mu", l, b, c, j), used(("mixup", l, b, c))))

        def gate_act(l):
            i = 0
            for c in range(2):
                for b in range(3):
                    for j in range(4):
                        if j % 2 == 0:
                            split_act(after((("gate", l, b, c), j // 2)))
                        nc.scalar.wait_ge(pe_done, at(("gt", l, b, c, j)))
                        if i >= 4:
                            nc.scalar.wait_ge(dve_done, at(("gated", l, i - 4)))
                        nc.scalar.activation(GSB[:, i % 4, :], bank_of(("gt", l, b, c, j)), ACT.Sigmoid).then_inc(act_done, mark("act", ("free", ("gt", l, b, c, j)), ("sig", l, i)))
                        i += 1

        def gate_dve(l):
            i = 0
            for c in range(2):
                for b in range(3):
                    split_dve(after((("gate", l, b, c), 0)))
                    split_dve(after((("gate", l, b, c), 1)))
                    for j in range(4):
                        nc.vector.wait_ge(pe_done, at(("mu", l, b, c, j)))
                        nc.vector.wait_ge(act_done, at(("sig", l, i)))
                        y = Y2[:, 4 * c + j, :]
                        dst = y if b == 0 else YTB[:, i % 2, :]
                        if b and (i - 2) // 4 % 3:
                            nc.vector.wait_ge(dve_done, at(("summed", l, i - 2)))
                        nc.vector.tensor_tensor(dst, bank_of(("mu", l, b, c, j)), GSB[:, i % 4, :], ALU.mult).then_inc(dve_done, mark("dve", ("free", ("mu", l, b, c, j)), ("gated", l, i)))
                        if b:
                            nc.vector.wait_ge(dve_done, at(("gated", l, i)))
                            nc.vector.tensor_tensor(y, y, dst, ALU.add).then_inc(dve_done, mark("dve", ("summed", l, i)))
                        i += 1

        def cross_pe(l):
            w = weights((("xkv", l), 0))
            for j in range(2):
                out = take(("xk", l, j))[:, 0:CTX]
                m = mms(out, [(w[:, k, 128 * j:128 * j + 128], X[:, k, 0:CTX]) for k in range(DT)])
                m.then_inc(pe_done, mark("pe", ("xk", l, j), used((("xkv", l), 0))))
            w = weights((("xkv", l), 1))
            for t in range(2):
                out = take(("xv", l, t))[:, 0:CTX]
                m = mms(out, [(X[:, k, 128 * t:128 * t + 128], w[:, k, :]) for k in range(DT)])
                m.then_inc(pe_done, mark("pe", ("xv", l, t), used((("xkv", l), 1))))
            w = split_weights(("xq", l))
            for j in range(2):
                m = mms3(take(("xq", l, j)), [(two(w, k, 128 * j, 128 * j + 128), hs(k, CTX, SEQ)) for k in range(DT)])
                m.then_inc(pe_done, mark("pe", ("xq", l, j), split_used(("xq", l))))

        def cross_act(l):
            split_act(after(("xq", l)))
            for n, dst, w in (("xk", XK, CTX), ("xv", XV, CTX), ("xq", XQ, SEQ)):
                for j in range(2):
                    nc.scalar.wait_ge(pe_done, at((n, l, j)))
                    nc.scalar.copy(dst[:, j, :], bank_of((n, l, j))[:, 0:w]).then_inc(act_done, mark("act", ("free", (n, l, j))))

        def cross_attention(l):
            its = []
            for h in range(4):
                e = 64 * (h % 2)
                for qt in range(4):
                    qs = slice(128 * qt, 128 * qt + 128)
                    its.append(dict(keys=CTX, mask=None, part=(e, 64),
                                    prods=[[(XQ[e:e + 64, h // 2, qs], XK[e:e + 64, h // 2, :])]],
                                    v=lambda k, h=h: XV[:, k, 64 * h:64 * h + 64], out=XO[e:e + 64, h // 2, qs]))
            return attention(("cross", l), its, HD ** -0.5, XP, XPT, XS)

        cross_att = [cross_attention(l) for l in range(2)]

        def after_x(eng):
            eng.wait_ge(x_loaded, 16)

        def mod_gate(l, which):
            return lambda n, c: modv[:, l, 16 + 24 * which + n, c:c + 1]

        def memory_norm():
            a = Carve()
            x = [X[:, k, 0:CTX] for k in range(DT)]
            sq = a(DT, CTX)
            return [block_norm("mem", 0, CTX, x, [sq[:, k, :] for k in range(DT)], x,
                               [v("mem_norm", k) for k in range(DT)], None, a(CTX))]

        fa = Carve()
        FIN = fa(DT, SEQ)

        def final_norm():
            sq = fa(DT, SEQ)
            return [block_norm("final", CTX, SEQ, [X[:, k, CTX:TOK] for k in range(DT)], [sq[:, k, :] for k in range(DT)],
                               [FIN[:, k, :] for k in range(DT)], [v("final_norm", k) for k in range(DT)], None, fa(SEQ))]

        norms = {"n0": gla_input_norm(), "mem": memory_norm(), "final": final_norm()}
        hnorms = {"n0f": adaln("n0f", ALL, 0, 1), "n1": adaln("n1", ALL, 1, 0), "n1f": adaln("n1f", MAIN, 1, 1)}
        for l in range(2):
            for key, name in (("m", "norm_mix_2"), ("x", "norm_cross"), ("f", "norm_ffn_2")):
                hnorms[key, l] = ((key, l), MAIN, lambda k, c, name=name, l=l: v(name, 8 * l + k), None)
            norms["subln", l] = subln_items(l)

        def hide_dve(l):
            nc.vector.memset(TT[0:64, :, 448:512], NEG).then_inc(dve_done, mark("dve", ("ttm", l)))
            nc.vector.wait_ge(dve_done, at(("ttm", l)))

        def subln_gain_dve(l):
            nc.vector.tensor_scalar(LAM[:, 6:7], v("subln", l), 1.0 - lam_init(l), None, ALU.mult).then_inc(
                dve_done, mark("dve", ("sg", l)))
            nc.vector.wait_ge(dve_done, at(("sg", l)))

        def ada1_pe(c):
            ada_pe(1, c)
            if c:
                ada_turn_pe(1, c - 1)
            if c == FT // 2 - 1:
                ada_pe(1, c + 1)
                ada_turn_pe(1, c)
                ada_turn_pe(1, c + 1)

        def ada1_act(c):
            ada_act(1, c)
            if c == FT // 2 - 1:
                ada_act(1, c + 1)

        def ada1_dve(c):
            if c:
                ada_dve(1, c - 1)
            if c == FT // 2 - 1:
                ada_dve(1, c)
                ada_dve(1, c + 1)

        def nothing(c):
            pass

        block = ctx.enter_context(nc.Block())

        @block.sync
        def _(sp):
            for i, (key, parts, split) in enumerate(plan):
                if i >= SLOTS and plan[i - SLOTS][2]:
                    sp.wait_ge(dve_done, at(("slot_used", i - SLOTS)))
                elif i >= SLOTS:
                    sp.wait_ge(pe_done, at(("slot_used", i - SLOTS)))
                width = parts[-1][0] + parts[-1][1].shape[2]
                kt = parts[0][1].shape[1]
                slot = ring[:, i % SLOTS, 0:kt * width].rearrange("p (t n) -> p t n", n=width)
                for c0, src in parts:
                    sp.dma_start(slot[:, :, c0:c0 + src.shape[2]], src).then_inc(slot_loaded[i % SLOTS], 16)
            sp.wait_ge(dve_done, at(("end", "final"), "dve"))
            sp.dma_start(io["outT"], FIN).then_inc(out_stored, 16)
            sp.wait_ge(out_stored, 16)

        @block.tensor
        def _(pe):
            start_pe()
            meet("pe", pe, "start")
            norm_pe(norms["n0"])
            meet("pe", pe, "norm0")
            gla_z_pe()
            meet("pe", pe, "gla_z")
            for h in range(GLA_H):
                gla_proj_pe(h)
                meet("pe", pe, ("gla_proj", h))
                gla_scan_pe(h)
                meet("pe", pe, ("gla_scan", h))
            norm_pe(gla_items)
            gla_r_pe()
            meet("pe", pe, "gla_norm")
            residual_pe("gla_out", lambda k, t0, tn: Y[:, k, t0:t0 + tn], ALL)
            meet("pe", pe, "gla_out")
            hnorm_pe(hnorms["n0f"])
            meet("pe", pe, "norm0f")
            ffn_pe("a0", ALL, ada1_pe)
            meet("pe", pe, "ffn0")
            hnorm_pe(hnorms["n1"])
            meet("pe", pe, "norm1")
            mla_down_pe()
            meet("pe", pe, "mla_down")
            mla_rest_pe()
            meet("pe", pe, "mla_rest")
            for g in range(2):
                uq_pe(g)
                meet("pe", pe, ("mla_up", g))
                norm_pe(mla_qk[g])
                rope_pe(q_rope[g], "perm_axial")
                meet("pe", pe, ("mla_qk", g))
                mla_att[g]["pe"]()
                meet("pe", pe, ("mla_att", g))
            residual_pe("mla_out", lambda k, t0, tn: MO[:, k, :], MAIN)
            meet("pe", pe, "mla_out")
            hnorm_pe(hnorms["n1f"])
            meet("pe", pe, "norm1f")
            ffn_pe("a1", MAIN, nothing)
            meet("pe", pe, "ffn1")
            norm_pe(norms["mem"])
            meet("pe", pe, "memnorm")
            for l in range(2):
                hnorm_pe(hnorms["m", l])
                meet("pe", pe, ("norm_m", l))
                qk_pe(l, 0, 0)
                qk_pe(l, 0, 1)
                v_pe(l, 0)
                flip_pe(l)
                meet("pe", pe, ("qkv0", l))
                mix_att[l, 0]["pe"]()
                meet("pe", pe, ("att0", l))
                idx_pe(l)
                meet("pe", pe, ("idx", l))
                logits_pe(l, (1, 2))
                qk_pe(l, 2, 0)
                logits_pe(l, (3,))
                qk_pe(l, 2, 1)
                v_pe(l, 2)
                rope_pe(qk_rope(l, 2), "perm_half")
                meet("pe", pe, ("topk", l))
                mix_att[l, 2]["pe"]()
                meet("pe", pe, ("att2", l))
                qk_pe(l, 1, 0)
                qk_pe(l, 1, 1)
                v_pe(l, 1)
                rope_pe(qk_rope(l, 1), "perm_half")
                meet("pe", pe, ("qkv1", l))
                mix_att[l, 1]["pe"]()
                meet("pe", pe, ("att1", l))
                norm_pe(norms["subln", l])
                meet("pe", pe, ("subln", l))
                gate_pe(l)
                meet("pe", pe, ("gate", l))
                residual_pe(("mixout", l), lambda k, t0, tn: Y2[:, k, :], MAIN)
                meet("pe", pe, ("mixout", l))
                hnorm_pe(hnorms["x", l])
                meet("pe", pe, ("norm_x", l))
                cross_pe(l)
                meet("pe", pe, ("cross", l))
                cross_att[l]["pe"]()
                meet("pe", pe, ("crossatt", l))
                residual_pe(("xo", l), lambda k, t0, tn: XO[:, k, :], MAIN, [(("xo", l), 0, 8)])
                meet("pe", pe, ("crossout", l))
                hnorm_pe(hnorms["f", l])
                meet("pe", pe, ("norm_f", l))
                ffn_pe(f"b{l}", MAIN, nothing)
                meet("pe", pe, ("ffn", l))
            norm_pe(norms["final"])
            meet("pe", pe, "final")

        @block.scalar
        def _(act):
            start_act()
            ln_exp_tables()
            meet("act", act, "start")
            after_x(act)
            norm_act(norms["n0"])
            meet("act", act, "norm0")
            gla_z_act()
            meet("act", act, "gla_z")
            for h in range(GLA_H):
                gla_proj_act(h)
                meet("act", act, ("gla_proj", h))
                meet("act", act, ("gla_scan", h))
            norm_act(gla_items)
            gla_r_act()
            ln_exp_tables()
            meet("act", act, "gla_norm")
            split_act(0)
            meet("act", act, "gla_out")
            hnorm_act(hnorms["n0f"])
            meet("act", act, "norm0f")
            conv_ffn_act("a0", 0, ALL, ada1_act)
            ln_exp_tables()
            meet("act", act, "ffn0")
            hnorm_act(hnorms["n1"])
            meet("act", act, "norm1")
            mla_down_act()
            meet("act", act, "mla_down")
            mla_rest_act()
            meet("act", act, "mla_rest")
            for g in range(2):
                uq_act(g)
                meet("act", act, ("mla_up", g))
                norm_act(mla_qk[g])
                meet("act", act, ("mla_qk", g))
                mla_att[g]["act"]()
                meet("act", act, ("mla_att", g))
            split_act(split_at["up", "a1", 0])
            meet("act", act, "mla_out")
            hnorm_act(hnorms["n1f"])
            meet("act", act, "norm1f")
            conv_ffn_act("a1", 1, MAIN, nothing)
            ln_exp_tables()
            meet("act", act, "ffn1")
            need_load(act, "axial")
            norm_act(norms["mem"])
            meet("act", act, "memnorm")
            for l in range(2):
                hnorm_act(hnorms["m", l])
                meet("act", act, ("norm_m", l))
                qkv_act(l, 0)
                flip_act(l)
                meet("act", act, ("qkv0", l))
                mix_att[l, 0]["act"]()
                meet("act", act, ("att0", l))
                idx_act(l)
                meet("act", act, ("idx", l))
                qkv_act(l, 2)
                lambda_act(l)
                meet("act", act, ("topk", l))
                mix_att[l, 2]["act"]()
                meet("act", act, ("att2", l))
                qkv_act(l, 1)
                meet("act", act, ("qkv1", l))
                mix_att[l, 1]["act"]()
                meet("act", act, ("att1", l))
                norm_act(norms["subln", l])
                meet("act", act, ("subln", l))
                gate_act(l)
                ln_exp_tables()
                meet("act", act, ("gate", l))
                split_act(split_at["xq", l])
                meet("act", act, ("mixout", l))
                hnorm_act(hnorms["x", l])
                meet("act", act, ("norm_x", l))
                cross_act(l)
                meet("act", act, ("cross", l))
                cross_att[l]["act"]()
                meet("act", act, ("crossatt", l))
                meet("act", act, ("crossout", l))
                hnorm_act(hnorms["f", l])
                meet("act", act, ("norm_f", l))
                swiglu_ffn_act(f"b{l}")
                ln_exp_tables()
                meet("act", act, ("ffn", l))
            norm_act(norms["final"])
            meet("act", act, "final")

        @block.vector
        def _(dve):
            start_dve()
            meet("dve", dve, "start")
            after_x(dve)
            norm_dve(norms["n0"])
            meet("dve", dve, "norm0")
            gla_z_dve()
            meet("dve", dve, "gla_z")
            for h in range(GLA_H):
                gla_proj_dve(h)
                meet("dve", dve, ("gla_proj", h))
                gla_scan_dve(h)
                meet("dve", dve, ("gla_scan", h))
            norm_dve(gla_items)
            gla_r_dve()
            meet("dve", dve, "gla_norm")
            gains_dve(0, 1)
            residual_dve("gla_out", ALL, mod_gate(0, 0))
            split_dve(0)
            meet("dve", dve, "gla_out")
            hnorm_dve(hnorms["n0f"])
            meet("dve", dve, "norm0f")
            conv_ffn_dve("a0", 0, ALL, mod_gate(0, 1), ada1_dve)
            gains_dve(1, 0)
            gains_dve(1, 1)
            meet("dve", dve, "ffn0")
            hnorm_dve(hnorms["n1"])
            meet("dve", dve, "norm1")
            mla_down_dve()
            meet("dve", dve, "mla_down")
            mla_rest_dve()
            meet("dve", dve, "mla_rest")
            for g in range(2):
                uq_dve(g)
                meet("dve", dve, ("mla_up", g))
                norm_dve(mla_qk[g])
                rope_dve(q_rope[g], tabs, RT)
                meet("dve", dve, ("mla_qk", g))
                mla_att[g]["dve"]()
                meet("dve", dve, ("mla_att", g))
            residual_dve("mla_out", MAIN, mod_gate(1, 0))
            split_dve(split_at["up", "a1", 0])
            meet("dve", dve, "mla_out")
            hnorm_dve(hnorms["n1f"])
            meet("dve", dve, "norm1f")
            conv_ffn_dve("a1", 1, MAIN, mod_gate(1, 1), nothing)
            meet("dve", dve, "ffn1")
            need_load(dve, "axial")
            norm_dve(norms["mem"])
            meet("dve", dve, "memnorm")
            for l in range(2):
                hnorm_dve(hnorms["m", l])
                meet("dve", dve, ("norm_m", l))
                qkv_dve(l, 0)
                meet("dve", dve, ("qkv0", l))
                hide_dve(l)
                mix_att[l, 0]["dve"]()
                meet("dve", dve, ("att0", l))
                idx_dve(l)
                meet("dve", dve, ("idx", l))
                topk_dve(l)
                rope_dve(qk_rope(l, 2), btab, BRT)
                lambda_dve(l)
                meet("dve", dve, ("topk", l))
                mix_att[l, 2]["dve"]()
                meet("dve", dve, ("att2", l))
                qkv_dve(l, 1)
                rope_dve(qk_rope(l, 1), btab, BRT)
                meet("dve", dve, ("qkv1", l))
                mix_att[l, 1]["dve"]()
                meet("dve", dve, ("att1", l))
                subln_gain_dve(l)
                norm_dve(norms["subln", l])
                meet("dve", dve, ("subln", l))
                gate_dve(l)
                meet("dve", dve, ("gate", l))
                residual_dve(("mixout", l), MAIN, None)
                split_dve(split_at["xq", l])
                meet("dve", dve, ("mixout", l))
                hnorm_dve(hnorms["x", l])
                meet("dve", dve, ("norm_x", l))
                split_dve(after(("xq", l)))
                meet("dve", dve, ("cross", l))
                cross_att[l]["dve"]()
                meet("dve", dve, ("crossatt", l))
                residual_dve(("xo", l), MAIN, None)
                meet("dve", dve, ("crossout", l))
                hnorm_dve(hnorms["f", l])
                meet("dve", dve, ("norm_f", l))
                swiglu_ffn_dve(f"b{l}")
                meet("dve", dve, ("ffn", l))
            norm_dve(norms["final"])
            meet("dve", dve, "final")

        @block.gpsimd
        def _(pool):
            start_pool()
            meet("pool", pool, "norm1")
            stage_load("axial", [(tabs, io["rope"][:, 0]), (X[:, :, 0:CTX], io["memT"])])
            for l in range(2):
                meet("pool", pool, ("norm_m", l))
                biases = [(TT[:, h, :], bass.AP(tensor=io["relb"].tensor, offset=(l * 8 + h) * 639,
                                                ap=[[1, P], [1, SEQ]])) for h in range(8)]
                stage_load(("block2", l), biases + [(btab, io["rope"][:, 1]),
                                                    (LV, io["lambda_vecs_2"][l].partition_broadcast(P))])


WEIGHTS = ["w_ada", "gla_w_in", "gla_gate_w1", "gla_gate_w2", "gla_w_out", "mla_w_down", "mla_w_uq", "mla_w_ukv",
           "mla_w_out", "ffn_w_up", "ffn_w_down", "w_in_2", "w_up_a_2", "w_up_b_2", "w_up_c_2", "w_out_2", "w_q_x_2",
           "w_kv_x_2", "w_o_x_2", "w_gu_2", "w_down_2", "lambda_vecs_2"]


def kernel(**inputs):
    import concourse.bacc as bacc
    from concourse.bass_utils import run_bass_kernel_spmd

    a = {k: np.asarray(x) for k, x in inputs.items()}

    def by_partition(x):
        return x.reshape(-1, P).T

    def twice(x):
        return np.concatenate([x, x])

    vectors = dict(
        c=a["c"], c_ctx=a["c_ctx"], b_ada=a["b_ada"], norm_mix=a["norm_mix"], norm_ffn=a["norm_ffn"],
        gate_b=a["gla_gate_b"], gla_out_norm=a["gla_out_norm"], q_lora_norm=a["mla_q_lora_norm"],
        kv_lora_norm=a["mla_kv_lora_norm"], q_norm_nope=a["mla_q_norm"][:, :NOPE],
        q_norm_rope=twice(a["mla_q_norm"][:, NOPE:]), k_norm_nope=a["mla_k_norm"][:, :NOPE],
        k_norm_rope=twice(a["mla_k_norm"][:, NOPE:]), conv_w=a["ffn_conv_w"], conv_b=a["ffn_conv_b"],
        norm_mix_2=a["norm_mix_2"], subln=a["subln_b_2"], norm_cross=a["norm_cross_2"],
        norm_ffn_2=a["norm_ffn_2"], mem_norm=a["mem_norm_2"], final_norm=a["final_norm_2"])
    arrays = {n: np.ascontiguousarray(a[n]) for n in WEIGHTS}
    arrays["vec"] = np.ascontiguousarray(np.concatenate([by_partition(vectors[n]) for n, _ in VECTORS], 1))
    arrays["mats"], arrays["rope"] = shape_constants()

    def feature_major(x):
        return x.reshape(-1, DT, P).transpose(2, 1, 0)

    arrays["xT"] = np.ascontiguousarray(np.concatenate([feature_major(a["ctx"][0]), feature_major(a["x"][0])], 2))
    arrays["memT"] = np.ascontiguousarray(feature_major(a["mem_2"][0]))
    at = np.clip(SEQ - 1 - np.arange(639), -63, 256) + 63
    arrays["relb"] = np.ascontiguousarray(a["rel_bias_a_2"][:, :, at])

    def make(counts):
        nc = bacc.Bacc("TRN2", target_bir_lowering=False, num_devices=1)
        io = {n: nc.dram_tensor(f"in_{n}", x.shape, F32, kind="ExternalInput").ap() for n, x in arrays.items()}
        io["outT"] = nc.dram_tensor("out_0", (P, DT, SEQ), F32, kind="ExternalOutput").ap()
        build(nc, io, counts)
        return nc

    first = Counts()
    make(first)
    nc = make(Counts(first))
    r = run_bass_kernel_spmd(nc, [{f"in_{n}": x for n, x in arrays.items()}], core_ids=[0])
    out = np.asarray(r.results[0]["out_0"])
    return np.ascontiguousarray(out.transpose(2, 1, 0)).reshape(1, SEQ, D)
```
